# Optimizing a Trainium2 kernel written in Bass

```python
import math
import jax
import jax.numpy as jnp
from jax import lax
import numpy as np

D_MODEL = 1024
BATCH = 1
SEQ = 256
DEPTH = 1
DEC_BATCH = 8
DEC_SEQ = 1
PAST_LEN = 2048
PAGE_SIZE = 128

A_GROUPS = ((128, 1), (512, 4), (2048, 16))
N_A_GROUPS = len(A_GROUPS)
A_HEADS = 8
A_HEAD_DIM = 64
A_ROT_DIM = A_HEAD_DIM // 4
A_BAND = 128
A_SCALE = A_HEAD_DIM ** -0.5
ROPE_THETA = 500000.0
R_HEADS = 4
R_QK_DIM = D_MODEL // R_HEADS
R_V_DIM = 2 * R_QK_DIM
R_CHUNK = 128
R_THETA = 10000.0
D_FF = ((8 * D_MODEL // 3 + 127) // 128) * 128
EPS = 1e-6
NEG = -1e30
A_QKV_W = N_A_GROUPS * A_HEADS * A_HEAD_DIM
R_QK_W = R_HEADS * R_QK_DIM
R_V_W = R_HEADS * R_V_DIM
SPLIT_SIZES = (A_QKV_W, A_QKV_W, A_QKV_W, R_QK_W, R_QK_W, R_V_W, R_V_W, D_MODEL, D_MODEL)
SPLIT_POINTS = tuple(sum(SPLIT_SIZES[:i + 1]) for i in range(len(SPLIT_SIZES) - 1))
D_IN = sum(SPLIT_SIZES)

kernel_name = 'hybrid_dilated_retention_macaron_step'

def _rmsnorm(x, g):
    xf = x.astype(jnp.float32)
    y = xf * lax.rsqrt(jnp.mean(xf * xf, axis=-1, keepdims=True) + EPS)
    return (y * g.astype(jnp.float32)).astype(x.dtype)

def _rms_plain(x):
    xf = x.astype(jnp.float32)
    return xf * lax.rsqrt(jnp.mean(xf * xf, axis=-1, keepdims=True) + EPS)

def _half_ffn(x, g, w_in, w_out):
    h = _rmsnorm(x, g)
    a, b = jnp.split(h @ w_in, 2, axis=-1)
    return x + (0.5 * ((jax.nn.silu(a) * b) @ w_out)).astype(x.dtype)

def _partial_rope(x, pos):
    half = A_ROT_DIM // 2
    inv = ROPE_THETA ** (-jnp.arange(half, dtype=jnp.float32) / half)
    ang = pos.astype(jnp.float32)[:, None] * inv[None, :]
    cos = jnp.cos(ang)[:, None, :]
    sin = jnp.sin(ang)[:, None, :]
    xf = x.astype(jnp.float32)
    x1 = xf[..., :half]
    x2 = xf[..., half:A_ROT_DIM]
    out = jnp.concatenate([x1 * cos - x2 * sin, x2 * cos + x1 * sin, xf[..., A_ROT_DIM:]], axis=-1)
    return out.astype(x.dtype)

def _retention_rotary(x, pos):
    half = x.shape[-1] // 2
    inv = 1.0 / (R_THETA ** jnp.linspace(0.0, 1.0, half, dtype=jnp.float32))
    ang = pos.astype(jnp.float32)[:, None] * inv[None, :]
    cos = jnp.cos(ang)[:, None, :]
    sin = jnp.sin(ang)[:, None, :]
    xf = x.astype(jnp.float32).reshape(x.shape[:-1] + (half, 2))
    xe, xo = xf[..., 0], xf[..., 1]
    out = jnp.stack([xe * cos - xo * sin, xo * cos + xe * sin], axis=-1).reshape(x.shape)
    return out.astype(x.dtype)

def _dilated_prompt(q, k, v, dil):
    B, S, H, E = q.shape
    L = S // dil
    N = B * dil
    nb = -(-L // A_BAND)
    Lp = nb * A_BAND

    def fold(t):
        return t.reshape(B, L, dil, H, E).transpose(0, 2, 1, 3, 4).reshape(N, L, H, E)

    def band(t):
        tp = jnp.pad(t, ((0, 0), (A_BAND, Lp - L), (0, 0), (0, 0))).reshape(N, nb + 1, A_BAND, H, E)
        return jnp.concatenate([tp[:, :-1], tp[:, 1:]], axis=2)

    qb = jnp.pad(fold(q), ((0, 0), (0, Lp - L), (0, 0), (0, 0))).reshape(N, nb, A_BAND, H, E)
    kb = band(fold(k))
    vb = band(fold(v))
    s = jnp.einsum('nbqhe,nbkhe->nbhqk', qb, kb, preferred_element_type=jnp.float32)
    qi = jnp.arange(A_BAND)[:, None]
    kc = jnp.arange(2 * A_BAND)[None, :]
    dist = qi - kc + A_BAND
    kpos = jnp.arange(nb)[:, None, None] * A_BAND + kc[None] - A_BAND
    mask = (dist >= 0) & (dist <= A_BAND) & (kpos >= 0)
    s = jnp.where(mask[None, :, None], s, NEG)
    lse = jax.nn.logsumexp(s, axis=-1)
    p = jnp.exp(s - lse[..., None])
    o = jnp.einsum('nbhqk,nbkhe->nbqhe', p, vb.astype(jnp.float32))
    o = o.reshape(N, Lp, H, E)[:, :L]
    lse = lse.transpose(0, 1, 3, 2).reshape(N, Lp, H)[:, :L]

    def unfold(t):
        perm = (0, 2, 1) + tuple(range(3, t.ndim + 1))
        return t.reshape((B, dil, L) + t.shape[2:]).transpose(perm).reshape((B, S) + t.shape[2:])

    return unfold(o), unfold(lse)

def _dilated_step(q, k, v, buf, window, dil):
    T = q.shape[1]
    wb = buf.shape[1]
    kv = jnp.concatenate([buf, jnp.stack([k, v], axis=2).astype(buf.dtype)], axis=1)
    nk = window // dil + 1
    cidx = wb + jnp.arange(T)[:, None] - dil * jnp.arange(nk)[None, :]
    valid = cidx >= 0
    g = kv[:, jnp.maximum(cidx, 0)]
    s = jnp.einsum('bthe,btjhe->bthj', q, g[:, :, :, 0], preferred_element_type=jnp.float32)
    s = jnp.where(valid[None, :, None, :], s, NEG)
    lse = jax.nn.logsumexp(s, axis=-1)
    p = jnp.exp(s - lse[..., None])
    o = jnp.einsum('bthj,btjhe->bthe', p, g[:, :, :, 1].astype(jnp.float32))
    return o, lse, kv[:, T:]

def _combine_groups(outs, lses):
    w = jax.nn.softmax(jnp.stack(lses, axis=0), axis=0)
    return jnp.sum(w[..., None] * jnp.stack(outs, axis=0), axis=0)

def _retention(q, k, v, s0, chunk):
    B, T, H, Dk = q.shape
    Dv = v.shape[-1]
    n = T // chunk
    log_g = jnp.log(1.0 - 2.0 ** (-5.0 - jnp.arange(H, dtype=jnp.float32)))
    i = jnp.arange(chunk, dtype=jnp.float32)
    diff = i[:, None] - i[None, :]
    causal = diff >= 0
    dmat = jnp.where(causal[None], jnp.exp(jnp.where(causal, diff, 0.0)[None] * log_g[:, None, None]), 0.0)
    q_dec = jnp.exp((i[:, None] + 1.0) * log_g[None, :])
    k_dec = jnp.exp((chunk - 1.0 - i)[:, None] * log_g[None, :])
    s_dec = jnp.exp(chunk * log_g)

    def blocks(t):
        return t.astype(jnp.float32).reshape(B, n, chunk, H, t.shape[-1]).transpose(1, 0, 2, 3, 4)

    def step(state, qkv):
        qc, kc, vc = qkv
        a = jnp.einsum('bihd,bjhd->bhij', qc, kc) * dmat[None]
        o = (jnp.einsum('bhij,bjhe->bihe', a, vc)
             + jnp.einsum('bihd,bhde->bihe', qc, state) * q_dec[None, :, :, None])
        state = state * s_dec[None, :, None, None] + jnp.einsum('bjhd,bjhe->bhde', kc * k_dec[None, :, :, None], vc)
        return state, o

    s_fin, o = lax.scan(step, s0.astype(jnp.float32), (blocks(q), blocks(k), blocks(v)))
    return o.transpose(1, 0, 2, 3, 4).reshape(B, T, H, Dv), s_fin

def _block(x, pos, attend_a, s0, p):
    (ffn1_norm, ffn1_in, ffn1_out, mix_norm, w_in, a_q_norm, a_k_norm,
     w_pa, w_pb, w_o, ffn2_norm, ffn2_in, ffn2_out) = p
    B, T, _ = x.shape
    x = _half_ffn(x, ffn1_norm, ffn1_in, ffn1_out)
    h = _rmsnorm(x, mix_norm)
    qa, ka, va, qr, kr, vr, gr, ga, gb = jnp.split(h @ w_in, SPLIT_POINTS, axis=-1)
    ha = (B, T, N_A_GROUPS * A_HEADS, A_HEAD_DIM)
    g5 = (B, T, N_A_GROUPS, A_HEADS, A_HEAD_DIM)
    qa = (_partial_rope(_rmsnorm(qa.reshape(ha), a_q_norm), pos) * A_SCALE).reshape(g5)
    ka = _partial_rope(_rmsnorm(ka.reshape(ha), a_k_norm), pos).reshape(g5)
    va = va.reshape(g5)
    oa, kv_new = attend_a(qa, ka, va)
    qr = _retention_rotary(qr.reshape(B, T, R_HEADS, R_QK_DIM), pos)
    kr = _retention_rotary(kr.reshape(B, T, R_HEADS, R_QK_DIM), pos) * (R_QK_DIM ** -0.5)
    vr = vr.reshape(B, T, R_HEADS, R_V_DIM)
    chunk = R_CHUNK if T % R_CHUNK == 0 else T
    orr, s_new = _retention(qr, kr, vr, s0, chunk)
    ob = _rms_plain(orr).reshape(B, T, R_V_W) * jax.nn.silu(gr.astype(jnp.float32))
    m = (jax.nn.sigmoid(ga.astype(jnp.float32)) * (oa.reshape(B, T, A_HEADS * A_HEAD_DIM) @ w_pa)
         + jax.nn.sigmoid(gb.astype(jnp.float32)) * (ob @ w_pb))
    x = x + (m @ w_o).astype(x.dtype)
    x = _half_ffn(x, ffn2_norm, ffn2_in, ffn2_out)
    return x, kv_new, s_new

def _attend_prompt(qa, ka, va):
    T = qa.shape[1]
    outs, lses, kv = [], [], []
    for g, (win, dil) in enumerate(A_GROUPS):
        o, l = _dilated_prompt(qa[:, :, g], ka[:, :, g], va[:, :, g], dil)
        outs.append(o)
        lses.append(l)
        keep = min(win, T)
        kv.append(jnp.stack([ka[:, T - keep:, g], va[:, T - keep:, g]], axis=2))
    return _combine_groups(outs, lses), kv

def _attend_sample(bufs):
    def attend(qa, ka, va):
        outs, lses, kv = [], [], []
        for g, (win, dil) in enumerate(A_GROUPS):
            o, l, nb = _dilated_step(qa[:, :, g], ka[:, :, g], va[:, :, g], bufs[g], win, dil)
            outs.append(o)
            lses.append(l)
            kv.append(nb)
        return _combine_groups(outs, lses), kv
    return attend

def setup_inputs(seed: int = 0) -> dict:
    key = jax.random.key(seed)
    ks = jax.random.split(key, 19)
    f32 = jnp.float32

    def nrm(k, shape, scale):
        return jax.random.normal(k, shape, f32) * scale

    def gain(k, n):
        return 1.0 + 0.05 * jax.random.normal(k, (DEPTH, n), f32)

    kv_tail = (2, A_HEADS, A_HEAD_DIM)
    return {
        'x_prompt': nrm(ks[0], (BATCH, SEQ, D_MODEL), 1.0),
        'x_sample': nrm(ks[1], (DEC_BATCH, DEC_SEQ, D_MODEL), 1.0),
        'cache_kv_a0': nrm(ks[2], (DEPTH, DEC_BATCH, min(A_GROUPS[0][0], PAST_LEN)) + kv_tail, 1.0),
        'cache_kv_a1': nrm(ks[3], (DEPTH, DEC_BATCH, min(A_GROUPS[1][0], PAST_LEN)) + kv_tail, 1.0),
        'cache_kv_a2': nrm(ks[4], (DEPTH, DEC_BATCH, min(A_GROUPS[2][0], PAST_LEN)) + kv_tail, 1.0),
        'state_ret': nrm(ks[5], (DEPTH, DEC_BATCH, R_HEADS, R_QK_DIM, R_V_DIM), 0.5),
        'ffn1_norm': gain(ks[6], D_MODEL),
        'ffn1_in': nrm(ks[7], (DEPTH, D_MODEL, 2 * D_FF), D_MODEL ** -0.5),
        'ffn1_out': nrm(ks[8], (DEPTH, D_FF, D_MODEL), D_FF ** -0.5),
        'mix_norm': gain(ks[9], D_MODEL),
        'w_in': nrm(ks[10], (DEPTH, D_MODEL, D_IN), D_MODEL ** -0.5),
        'a_q_norm': gain(ks[11], A_HEAD_DIM),
        'a_k_norm': gain(ks[12], A_HEAD_DIM),
        'w_pa': nrm(ks[13], (DEPTH, A_HEADS * A_HEAD_DIM, D_MODEL), (A_HEADS * A_HEAD_DIM) ** -0.5),
        'w_pb': nrm(ks[14], (DEPTH, R_V_W, D_MODEL), R_V_W ** -0.5),
        'w_o': nrm(ks[15], (DEPTH, D_MODEL, D_MODEL), D_MODEL ** -0.5),
        'ffn2_norm': gain(ks[16], D_MODEL),
        'ffn2_in': nrm(ks[17], (DEPTH, D_MODEL, 2 * D_FF), D_MODEL ** -0.5),
        'ffn2_out': nrm(ks[18], (DEPTH, D_FF, D_MODEL), D_FF ** -0.5),
    }

def reference(x_prompt, x_sample, cache_kv_a0, cache_kv_a1, cache_kv_a2, state_ret,
              ffn1_norm, ffn1_in, ffn1_out, mix_norm, w_in, a_q_norm, a_k_norm,
              w_pa, w_pb, w_o, ffn2_norm, ffn2_in, ffn2_out):
    yp, ys = x_prompt, x_sample
    pos_p = jnp.arange(x_prompt.shape[1], dtype=jnp.int32)
    pos_s = PAST_LEN + jnp.arange(x_sample.shape[1], dtype=jnp.int32)
    kvp0, kvp1, kvp2, rp = [], [], [], []
    kvs0, kvs1, kvs2, rs = [], [], [], []
    for l in range(DEPTH):
        p = (ffn1_norm[l], ffn1_in[l], ffn1_out[l], mix_norm[l], w_in[l], a_q_norm[l], a_k_norm[l],
             w_pa[l], w_pb[l], w_o[l], ffn2_norm[l], ffn2_in[l], ffn2_out[l])
        s0 = jnp.zeros((yp.shape[0], R_HEADS, R_QK_DIM, R_V_DIM), jnp.float32)
        yp, kv_p, r_p = _block(yp, pos_p, _attend_prompt, s0, p)
        attend_s = _attend_sample((cache_kv_a0[l], cache_kv_a1[l], cache_kv_a2[l]))
        ys, kv_s, r_s = _block(ys, pos_s, attend_s, state_ret[l], p)
        kvp0.append(kv_p[0]); kvp1.append(kv_p[1]); kvp2.append(kv_p[2]); rp.append(r_p)
        kvs0.append(kv_s[0]); kvs1.append(kv_s[1]); kvs2.append(kv_s[2]); rs.append(r_s)
    return (yp, ys,
            jnp.stack(kvp0), jnp.stack(kvp1), jnp.stack(kvp2), jnp.stack(rp),
            jnp.stack(kvs0), jnp.stack(kvs1), jnp.stack(kvs2), jnp.stack(rs))


_drawn_inputs = setup_inputs


def setup_inputs(seed=0):
    import zlib

    import numpy as np

    out = dict(_drawn_inputs(seed))
    spreads = {}
    factors = {'a_q_norm': 8.0, 'ffn2_norm': 3.014}
    for name, (base, spread) in spreads.items():
        noise = np.random.default_rng([zlib.crc32(name.encode()), seed]).standard_normal(out[name].shape)
        drawn = base * np.exp(spread * noise) if base else spread * noise
        out[name] = jnp.asarray(drawn.astype(out[name].dtype))
    for name, factor in factors.items():
        out[name] = (out[name] * factor).astype(out[name].dtype)
    return out
```

```python
from contextlib import ExitStack

import numpy as np

import concourse.bass as bass
from concourse import mybir

F32 = mybir.dt.float32
F32R = mybir.dt.float32r
ALU = mybir.AluOpType
ACT = mybir.ActivationFunctionType
AX = mybir.AxisListType

P = 128
D = 1024
KD = D // P
S = 256
B = 8
T = S + B
PAST = 2048
DFF = ((8 * D // 3 + P - 1) // P) * P
FT = DFF // P
GROUPS = ((128, 1), (512, 4), (2048, 16))
G = len(GROUPS)
AH, AE = 8, 64
AW = AH * AE
AT = G * AW // P
RH, RQ, RV = 4, 256, 512
EPS = 1e-6
NEG = -1e30
SCALE = AE ** -0.5

PHASES = [
    ("fi", 11, 4, "dve"), ("fo", 8, 1, "dve"), ("qr", 2, 4, "act"), ("kr", 2, 4, "act"), ("vr", 4, 4, "act"),
    ("gr", 4, 4, "dve"), ("qk", 6, 4, "act"), ("v", 3, 4, "act"), ("gb", 2, 4, "act"), ("pb", 4, 2, "dve"),
    ("ga", 2, 4, "act"), ("pa", 1, 8, "dve"), ("wo", 2, 4, "dve"), ("fi", 11, 4, "dve"), ("fo", 8, 1, "dve"),
]
FO_HALVES = (6, 5, 6, 5)


def moving(it):
    return not isinstance(it, int)


class Phase:

    def __init__(self, index):
        self.kind, self.quads, self.per_quad, self.owner = PHASES[index]
        self.q0 = sum(p[1] for p in PHASES[:index])
        self.out0 = sum(p[1] * p[2] for p in PHASES[:index] if p[3] == self.owner)
        self.previous = PHASES[index - 1][3] if index else self.owner
        self.previous_out = sum(p[1] * p[2] for p in PHASES[:index] if p[3] == self.previous)


QUADS = sum(p[1] for p in PHASES)
KIND_OF = [p[0] for p in PHASES for _ in range(p[1])]


def half_tiles(q, j):
    return FO_HALVES[j] if KIND_OF[q] == "fo" else 8


def half_offset(q, j):
    return (0 if j % 2 == 0 else half_tiles(q, j - 1)) * P


TABLES = {}
_at = 0
for _name, _n in (("cos_a", T), ("sin_a", T), ("cos_r", T), ("sin_r", T), ("mask", G * 2 * P), ("decay", RH * 2 * P),
                  ("ident", P), ("ones", P), ("blocks", P), ("turn", P), ("kdec", RH * 2), ("gamma", RH),
                  ("rsel", B), ("eps", 1)):
    TABLES[_name] = (_at, _at + _n)
    _at += _n
NTAB = _at
NGAIN = 3 * KD + 2


def build_tables():
    tab = np.zeros((P, NTAB), np.float32)

    def put(name, value):
        a, b = TABLES[name]
        value = np.asarray(value, np.float32)
        tab[:value.shape[0], a:b] = value.reshape(value.shape[0], b - a)

    pos = np.concatenate([np.arange(S), np.full(B, PAST)]).astype(np.float32)
    half = AE // 8
    inv = (np.float32(500000.0) ** (-np.arange(half, dtype=np.float32) / np.float32(half))).astype(np.float32)
    ang = (pos[None, :] * inv[:, None]).astype(np.float32).astype(np.float64)
    cos_a, sin_a = np.ones((P, T)), np.zeros((P, T))
    turn = np.zeros((P, P))
    for base in (0, AE):
        for r in range(2):
            cos_a[base + r * half:base + (r + 1) * half] = np.cos(ang)
            sin_a[base + r * half:base + (r + 1) * half] = np.sin(ang)
        for i in range(half):
            turn[base + half + i, base + i] = -1.0
            turn[base + i, base + half + i] = 1.0
    put("cos_a", cos_a)
    put("sin_a", sin_a)
    put("turn", turn)
    inv_r = (np.float32(1.0) / np.float32(10000.0) ** np.linspace(0.0, 1.0, P, dtype=np.float32)).astype(np.float32)
    ang_r = (pos[None, :] * inv_r[:, None]).astype(np.float32).astype(np.float64)
    put("cos_r", np.cos(ang_r))
    put("sin_r", np.sin(ang_r))
    mask = np.zeros((P, G, 2, P))
    qi, kj = np.arange(P)[:, None], np.arange(P)[None, :]
    for g, (_, dil) in enumerate(GROUPS):
        for block, dist in ((0, P + qi - kj), (1, qi - kj)):
            ok = (dist >= 0) & (dist % dil == 0) & (dist // dil <= P)
            mask[:, g, block] = np.where(ok, 0.0, NEG)
    put("mask", mask)
    gamma = 1.0 - 2.0 ** (-5.0 - np.arange(RH))
    decay = np.zeros((P, RH, 2, P))
    j, i = np.arange(P)[:, None], np.arange(P)[None, :]
    for h in range(RH):
        decay[:, h, 0] = np.where(i >= j, gamma[h] ** np.maximum(i - j, 0), 0.0)
        decay[:, h, 1] = gamma[h] ** (P + i - j)
    put("decay", decay)
    put("ident", np.eye(P))
    put("ones", np.ones((P, P)))
    put("blocks", np.kron(np.eye(2), np.ones((AE, AE))))
    kdec = np.zeros((P, RH, 2))
    for h in range(RH):
        for c in range(2):
            kdec[:, h, c] = gamma[h] ** (S - 1 - c * P - np.arange(P))
    put("kdec", kdec)
    put("gamma", np.broadcast_to(gamma, (P, RH)))
    put("rsel", (np.arange(64)[:, None] % B == np.arange(B)[None, :]))
    put("eps", np.full((P, 1), EPS))
    return tab


def trunk_step(nc, xT, tables, gains, w16, w11, cache0, cache1, cache2, state_in,
               yT, kT_out, v_out, ret_out, kv0_out, kv1_out, kv2_out, state_out):
    caches, kv_outs = (cache0, cache1, cache2), (kv0_out, kv1_out, kv2_out)

    with ExitStack() as ctx:
        base = 16512
        place = {"at": base}

        def fixed(name, shape, dtype=F32):
            t = nc.alloc_sbuf_tensor_at(name, [P] + shape, dtype, offset=place["at"])
            place["at"] += (int(np.prod(shape)) * 4 + 31) // 32 * 32
            return t

        x = fixed("x", [KD, T])
        hh = fixed("hh", [KD, T], F32R)
        hl = fixed("hl", [KD, T], F32R)
        raw = [fixed(f"raw{i}", [16 * P]) for i in range(2)]
        wh = [fixed(f"wh{i}", [8 * P], F32R) for i in range(4)]
        wl = [fixed(f"wl{i}", [8 * P], F32R) for i in range(4)]
        tab = fixed("tab", [NTAB])
        gain = fixed("gain", [NGAIN])
        square = fixed("square", [2, T])
        square_sum = fixed("square_sum", [T])
        rms = fixed("rms", [T])
        normed = fixed("normed", [2, T])
        qr_s = fixed("qr_s", [2 * RH, B])
        kr_s = fixed("kr_s", [2 * RH, B])
        o_s = fixed("o_s", [RH * 4, B])
        o_s2 = fixed("o_s2", [RH * 4, B])
        os_sum = fixed("os_sum", [RH, B])
        arena = place["at"]

        def at(name, offset, shape, dtype=F32):
            return nc.alloc_sbuf_tensor_at(name, [P] + shape, dtype, offset=arena + offset)

        uh = at("uh", 0, [FT, T], F32R)
        ul = at("ul", 23232, [FT, T], F32R)
        silu = at("silu", 46464, [2, T])
        product = at("product", 48576, [2, T])
        v_ret = at("v_ret", 0, [2, RH * RV])
        vs_ret = at("vs_ret", 16384, [RH * RV])
        ob = at("ob", 24576, [RH * 4, T])
        qr = at("qr", 41472, [2 * RH, T])
        kr = at("kr", 49920, [2 * RH, T])
        pair = at("pair", 58368, [2, 2, T])
        turned = at("turned", 62592, [4, T])
        vT_ret = at("vT_ret", 66816, [2, T])
        sig = at("sig", 68928, [2, T])
        a_dec = at("a_dec", 71040, [3 * P])
        k_dec = at("k_dec", 72576, [2, RQ])
        o_ret = at("o_ret", 74624, [4, S])
        o_sq = at("o_sq", 78720, [4, S])
        o_sum = at("o_sum", 82816, [S])
        o_rms = at("o_rms", 83840, [S])
        s_new = at("s_new", 84864, [2, RV])
        state = at("state", 0, [4, 2 * RV])
        qk = at("qk", 41472, [2 * AT, T])
        v_tok = at("v_tok", 66816, [2, G * AW])
        vk_s = at("vk_s", 79104, [G * AW])
        v_s, k_s = vk_s[0:B, :], vk_s[32:32 + B, :]
        q_s = at("q_s", 85248, [G * AW])
        qk_sq = at("qk_sq", 91392, [2, T])
        qk_rms = at("qk_rms", 93504, [2, T])
        rot_s = at("rot_s", 95616, [2, T])
        rot_c = at("rot_c", 97728, [2, T])
        v_mask = at("v_mask", 99840, [2, RV])
        vT = at("vT", 103936, [2, T])
        qk_n = at("qk_n", 112192, [2, T])
        obh = at("obh", 0, [RH * 4, T], F32R)
        dec_s = at("dec_s", 16896, [G, 64])
        dec_p = at("dec_p", 17664, [G * P + G])
        dec_pT = at("dec_pT", 19232, [G, 64])
        dec_own = at("dec_own", 20000, [G, 64])
        dec_diag = at("dec_diag", 20768, [G, 64])
        qk_own = at("qk_own", 21536, [AT, B])
        dec_m = at("dec_m", 21920, [4])
        att_m = at("att_m", 21952, [4])
        gate_b = at("gate_b", 24576, [KD, T])
        gate_a = at("gate_a", 33024, [KD, T])
        oa = at("oa", 85248, [4, T])
        kv = at("kv", 91392, [3, AW])
        q_mask = at("q_mask", 97536, [AW])
        prob = at("prob", 91392, [G, 2 * P])
        probT = at("probT", 94464, [6 * P])
        obl = at("obl", 99584, [RH * 4, T], F32R)
        oah = at("oah", 41472, [4, T], F32R)
        oal = at("oal", 45696, [4, T], F32R)
        merge_a = at("merge_a", 91392, [2, T])
        merge = at("merge", 93504, [2, T])

        def const(name, rows=P):
            a, b = TABLES[name]
            return tab[0:rows, a:b]

        ident, ones, blocks, turn = const("ident"), const("ones"), const("blocks"), const("turn")
        eps = const("eps")

        acc = [ctx.enter_context(nc.psum_tensor(f"acc{i}", [P, 512], F32)) for i in range(4)]
        aux45 = ctx.enter_context(nc.psum_tensor("aux45", [P, 2, 512], F32))
        aux67 = ctx.enter_context(nc.psum_tensor("aux67", [P, 2, 512], F32))
        bank4, bank5, bank6, bank7 = aux45[:, 0], aux45[:, 1], aux67[:, 0], aux67[:, 1]

        def sem(name):
            return ctx.enter_context(nc.semaphore(name))

        const_in = sem("const_in")
        raw_in = [sem("raw_in0"), sem("raw_in1")]
        hi_done, lo_done = sem("hi_done"), sem("lo_done")
        pe_half = sem("pe_half")
        out_of = {"act": sem("acc_out_act"), "dve": sem("acc_out_dve")}
        silu_done, u_split = sem("silu_done"), sem("u_split")
        sq_done, sum_done, sum_psum = sem("sq_done"), sem("sum_done"), sem("sum_psum")
        rms_done, rinv_done = sem("rms_done"), sem("rinv_done")
        normed_done, normed_hi, normed_split = sem("normed_done"), sem("normed_hi"), sem("normed_split")
        rr_dve, rr_pool, rr_done = sem("rr_dve"), sem("rr_pool"), sem("rr_done")
        rs_copied = sem("rs_copied")
        vr_turned, vr_out, vrs_out = sem("vr_turned"), sem("vr_out"), sem("vrs_out")
        sig_done = sem("sig_done")
        kt_psum, kdec_done = sem("kt_psum"), sem("kdec_done")
        a_psum, adec_done = sem("a_psum"), sem("adec_done")
        o_psum, o_out, osq_done, osum_done = sem("o_psum"), sem("o_out"), sem("osq_done"), sem("osum_done")
        oms_psum, orms_done, orinv_done, on_done, ob_done = (
            sem("oms_psum"), sem("orms_done"), sem("orinv_done"), sem("on_done"), sem("ob_done"))
        snew_psum, snew_out, ret_stored = sem("snew_psum"), sem("snew_out"), sem("ret_stored")
        qk_sq_done, qk_ms_psum, qk_rms_done, qk_rinv = (
            sem("qk_sq_done"), sem("qk_ms_psum"), sem("qk_rms_done"), sem("qk_rinv"))
        qk_normed, qk_rot_psum, qk_sin, qk_cos, qk_done = (
            sem("qk_normed"), sem("qk_rot_psum"), sem("qk_sin"), sem("qk_cos"), sem("qk_done"))
        state_in_sem = [sem(f"state_in{i}") for i in range(4)]
        state_stored = [sem(f"state_stored{i}") for i in range(4)]
        vmask_done, vb_psum, state_scaled, state_new = (
            sem("vmask_done"), sem("vb_psum"), sem("state_scaled"), sem("state_new"))
        os_psum, os_out = sem("os_psum"), sem("os_out")
        v_turned, v_out_sem, vs_out = sem("v_turned"), sem("v_tok_out"), sem("v_s_out")
        qks_psum, qks_out = sem("qks_psum"), sem("qks_out")
        small_step = sem("small_step")
        small_act = sem("small_act")
        small_pe = sem("small_pe")
        ob_hi, ob_split = sem("ob_hi"), sem("ob_split")
        kv_in = [sem(f"kv_in{i}") for i in range(3)]
        qmask_done, qb_psum, kq_done, dec_k_done = sem("qmask_done"), sem("qb_psum"), sem("kq_done"), sem("dec_k_done")
        dec_pe, dec_dve, dec_act, dec_v_done = sem("dec_pe"), sem("dec_dve"), sem("dec_act"), sem("dec_v_done")
        att_scores, att_masked, att_negmax = sem("att_scores"), sem("att_masked"), sem("att_negmax")
        att_exp, att_rinv, att_prob = sem("att_exp"), sem("att_rinv"), sem("att_prob")
        att_turned, att_turned_out = sem("att_turned"), sem("att_turned_out")
        att_pv, att_out = sem("att_pv"), sem("att_out")
        oa_hi, oa_split = sem("oa_hi"), sem("oa_split")
        merge_a_done, merge_done, merge_hi, merge_split = (
            sem("merge_a_done"), sem("merge_done"), sem("merge_hi"), sem("merge_split"))
        rolled = sem("rolled")
        stored = sem("stored")
        STORES = 1 + 1 + KD + 2 * G

        phases = [Phase(i) for i in range(len(PHASES))]
        unit16 = {}
        for q in range(QUADS):
            for s in range(2):
                n = 2 * q + s
                kind = "11" if KIND_OF[q] == "fo" else "16"
                unit16[n] = (kind, sum(1 for v in unit16.values() if v[0] == kind))

        def load_unit(act, n, it=0):
            kind, index = unit16[n]
            src, cols = (w16, 16 * P) if kind == "16" else (w11, 11 * P)
            act.dma_start(raw[n % 2][:, 0:cols], src[index + 2 * it]).then_inc(raw_in[n % 2], 16)

        def hi_half(act, q, j, it=0):
            n = half_tiles(q, j) * P
            off = half_offset(q, j)
            act.wait_ge(raw_in[j // 2], 16 * (q + 1) + 16 * it)
            if q >= 1:
                act.wait_ge(pe_half, 4 * (q - 1) + j + 1 + 4 * it)
            nc.scalar.activation(wh[j][:, 0:n], raw[j // 2][:, off:off + n], ACT.Copy).then_inc(hi_done, 1)

        def lo_half(dve, q, j, it=0):
            n = half_tiles(q, j) * P
            off = half_offset(q, j)
            dve.wait_ge(hi_done, 4 * q + j + 1 + 4 * it)
            nc.vector.tensor_tensor(wl[j][:, 0:n], raw[j // 2][:, off:off + n], wh[j][:, 0:n].bitcast(F32),
                                    ALU.subtract).then_inc(lo_done, 1)

        def act_ahead(act, q, j, it=0):
            if q + 1 < QUADS:
                hi_half(act, q + 1, j, it)
            if j == 0 and q + 1 < QUADS:
                act.wait_ge(lo_done, 4 * q + 4 + 4 * it)
                load_unit(act, 2 * (q + 1) + 1, it)
            if j == 2 and q + 2 < QUADS:
                act.wait_ge(lo_done, 4 * (q + 1) + 2 + 4 * it)
                load_unit(act, 2 * (q + 2), it)

        def dve_ahead(dve, q, j, it=0):
            if q + 1 < QUADS:
                lo_half(dve, q + 1, j, it)

        def three_passes(out, j, t, xh, xl, first, last, skip=False):
            w_hi, w_lo = wh[j][:, t * P:(t + 1) * P], wl[j][:, t * P:(t + 1) * P]
            nc.tensor.matmul(out, w_hi, xh, start=first, stop=False)
            nc.tensor.matmul(out, w_hi, xl, start=False, stop=False)
            return nc.tensor.matmul(out, w_lo, xh, start=False, stop=last)

        def pe_wait_half(pe, q, j, it=0):
            pe.wait_ge(lo_done, 4 * q + j + 1 + 4 * it)

        def pe_wait_acc(pe, ph, local, keep, it=0):
            value = ph.out0 + local - keep + 1
            if value > 0:
                pe.wait_ge(out_of[ph.owner], value + ph.per_quad * it)

        def pe_enter(pe, ph):
            if ph.previous != ph.owner and ph.q0:
                pe.wait_ge(out_of[ph.previous], ph.previous_out)

        def pe_wide_half(pe, ph, qq, j, it=0, wait_x=None, midway=None):
            pe_wait_half(pe, ph.q0 + qq, j, it)
            pe_wait_acc(pe, ph, 4 * qq + j, 4, it)
            for k in range(KD):
                if wait_x is not None:
                    pe.wait_ge(wait_x[0], wait_x[1] + k + 1)
                if k == 5 and midway:
                    midway()
                last = three_passes(acc[j][:, 0:T], j, k, hh[:, k], hl[:, k], k == 0, k == KD - 1)
            last.then_inc(pe_half, 1)

        def pe_fo_quad(pe, ph, m, bank, it=0):
            r = 0 if ph.q0 < QUADS // 2 else 1
            pe_wait_acc(pe, ph, m, 2, it)
            k = 0
            for j in range(4):
                pe_wait_half(pe, ph.q0 + m, j, it)
                pe.wait_ge(u_split, FT * r + k + FO_HALVES[j])
                for t in range(FO_HALVES[j]):
                    last = three_passes(acc[bank][:, 0:T], j, t, uh[:, k], ul[:, k], k == 0, k == FT - 1)
                    k += 1
                last.then_inc(pe_half, 1)

        def dve_sum_square(dve, r, m, it=0):
            dve.wait_ge(sq_done, KD * r + m + 1 + it)
            if not isinstance(m, int) or m or moving(it):
                dve.wait_ge(sum_done, KD * r + m + it)
            ins = (nc.vector.tensor_copy(square_sum[:], square[:, m % 2]) if m == 0 and not moving(it) else
                   nc.vector.tensor_tensor(square_sum[:], square_sum[:], square[:, m % 2], ALU.add))
            ins.then_inc(sum_done, 1)

        def act_square(act, r, m, it=0):
            if r or m >= 2:
                act.wait_ge(sum_done, KD * r + m - 1 + it)
            nc.scalar.activation(square[:, m % 2], x[:, bass.ds(m + it, 1)].squeeze(1) if moving(it) else x[:, m],
                                 ACT.Square).then_inc(sq_done, 1)

        def pe_norm(pe, r):
            pe.wait_ge(sum_done, KD * (r + 1))
            nc.tensor.matmul(bank4[:, 0:T], ones, square_sum[:], start=True, stop=True).then_inc(sum_psum, 1)

        def act_norm(act, r):
            act.wait_ge(sum_psum, r + 1)
            nc.scalar.activation(rms[:], bank4[:, 0:T], ACT.Sqrt, bias=eps, scale=1.0 / D).then_inc(rms_done, 1)
            for k in range(KD):
                act.wait_ge(normed_done, KD * r + k + 1)
                nc.scalar.activation(hh[:, k], normed[:, k % 2], ACT.Copy).then_inc(normed_hi, 1)

        def dve_norm(dve, r):
            dve.wait_ge(rms_done, r + 1)
            nc.vector.reciprocal(rms[:], rms[:]).then_inc(rinv_done, 1)
            dve.wait_ge(rinv_done, r + 1)
            for k in range(KD):
                if KD * r + k >= 2:
                    dve.wait_ge(normed_split, KD * r + k - 1)
                nc.vector.scalar_tensor_tensor(normed[:, k % 2], x[:, k], gain[:, r * KD + k:r * KD + k + 1],
                                               rms[:], ALU.mult, ALU.mult).then_inc(normed_done, 1)

        def pool_norm(pool, r):
            for k in range(KD):
                pool.wait_ge(normed_hi, KD * r + k + 1)
                nc.gpsimd.tensor_tensor(hl[:, k], normed[:, k % 2], hh[:, k].bitcast(F32),
                                        ALU.subtract).then_inc(normed_split, 1)

        def act_fi_quad(act, ph, qq, it=0):
            q = ph.q0 + qq
            r = 0 if ph.q0 < QUADS // 2 else 1
            for j in range(4):
                act_ahead(act, q, j, it)
                if j % 2 == 0:
                    i = FT * r + 2 * qq + j // 2
                    act.wait_ge(pe_half, 4 * q + j + 1 + 4 * it)
                    if i >= 2:
                        act.wait_ge(out_of["dve"], ph.out0 + 2 * (2 * qq + j // 2) - 2 + 4 * it)
                    nc.scalar.activation(silu[:, j // 2], acc[j][:, 0:T], ACT.Silu).then_inc(silu_done, 1)

        def dve_fi_quad(dve, ph, qq, it=0):
            q = ph.q0 + qq
            r = 0 if ph.q0 < QUADS // 2 else 1
            for j in range(4):
                dve_ahead(dve, q, j, it)
                if j % 2 == 1:
                    i = FT * r + 2 * qq + j // 2
                    dve.wait_ge(pe_half, 4 * q + j + 1 + 4 * it)
                    dve.wait_ge(silu_done, i + 1 + 2 * it)
                    if i >= 2:
                        dve.wait_ge(u_split, i - 1 + 2 * it)
                    nc.vector.tensor_tensor(product[:, j // 2], silu[:, j // 2], acc[j][:, 0:T],
                                            ALU.mult).then_inc(out_of["dve"], 2)

        def pool_fi_quad(pool, ph, qq, it=0):
            r = 0 if ph.q0 < QUADS // 2 else 1
            for s in range(2):
                i = 2 * qq + s
                pool.wait_ge(out_of["dve"], ph.out0 + 2 * i + 2 + 4 * it)
                if not moving(it):
                    hi, lo = uh[:, i], ul[:, i]
                else:
                    hi, lo = (u[:, bass.ds(i + 2 * it, 1)].squeeze(1) for u in (uh, ul))
                nc.gpsimd.tensor_copy(hi, product[:, s]).then_inc(u_hi, 1)
                pool.wait_ge(u_hi, FT * r + i + 1 + 2 * it)
                nc.gpsimd.tensor_tensor(lo, product[:, s], hi.bitcast(F32), ALU.subtract).then_inc(u_split, 1)

        u_hi = sem("u_hi")

        def act_fo_quad(act, ph, m, it=0, norm=None):
            for j in range(4):
                act_ahead(act, ph.q0 + m, j, it)
            if norm is not None:
                act.wait_ge(out_of["dve"], ph.out0 + m + 1 + it)
                act_square(act, norm, m, it)

        def dve_add_x(dve, ph, m, factor, bank, it=0):
            xm = x[:, m] if not moving(it) else x[:, bass.ds(m + it, 1)].squeeze(1)
            nc.vector.scalar_tensor_tensor(xm, acc[bank][:, 0:T], factor, xm, ALU.mult,
                                           ALU.add).then_inc(out_of["dve"], 1)

        def dve_fo_quad(dve, ph, m, it=0, norm=None):
            for j in range(4):
                dve_ahead(dve, ph.q0 + m, j, it)
            dve.wait_ge(pe_half, 4 * (ph.q0 + m) + 4 + 4 * it)
            dve_add_x(dve, ph, m, 0.5, m % 2, it)
            if norm is not None:
                dve_sum_square(dve, norm, m, it)

        RR = [("qr", qr), ("kr", kr)]

        def act_rr_quad(act, ph, qq, which):
            for j in range(4):
                act_ahead(act, ph.q0 + qq, j)
                head = 2 * qq + j // 2
                act.wait_ge(pe_half, 4 * (ph.q0 + qq) + j + 1)
                n = RH * which + head
                if n >= 2:
                    act.wait_ge(rr_done, n - 1)
                    act.wait_ge(rr_pool, 3 * n - 3)
                nc.scalar.activation(pair[:, head % 2, j % 2], acc[j][:, 0:T], ACT.Copy,
                                     scale=1.0 if which == 0 else RQ ** -0.5).then_inc(out_of["act"], 1)

        def turn_head(eng, ops, ph, head, which):
            n = RH * which + head
            dst = RR[which][1]
            eng.wait_ge(out_of["act"], ph.out0 + 2 * head + 2)
            cos, sin = const("cos_r"), const("sin_r")
            if ops is nc.vector:
                step, p, q_, out, t0, op = rr_dve, 0, 1, 2 * head, 0, ALU.subtract
            else:
                step, p, q_, out, t0, op = rr_pool, 1, 0, 2 * head + 1, 2, ALU.add
            if n:
                if ops is nc.vector:
                    eng.wait_ge(rr_done, n)
                else:
                    eng.wait_ge(rr_pool, 3 * n)
            ops.tensor_tensor(turned[:, t0], pair[:, head % 2, p], cos, ALU.mult).then_inc(step, 1)
            ops.tensor_tensor(turned[:, t0 + 1], pair[:, head % 2, q_], sin, ALU.mult).then_inc(step, 1)
            if ops is nc.vector:
                eng.wait_ge(rr_dve, 2 * n + 2)
                ops.tensor_tensor(dst[:, out], turned[:, t0], turned[:, t0 + 1], op).then_inc(rr_done, 1)
            else:
                eng.wait_ge(rr_pool, 3 * n + 2)
                ops.tensor_tensor(dst[:, out], turned[:, t0], turned[:, t0 + 1], op).then_inc(rr_pool, 1)

        VKIND = {"vr": (vT_ret, v_ret, vs_ret, vr_turned, vr_out, vrs_out),
                 "v": (vT, v_tok, v_s, v_turned, v_out_sem, vs_out)}

        def act_v_tile(act, ph, t):
            src, _, small, turned_sem, _, small_out = VKIND[ph.kind]
            act.wait_ge(pe_half, 4 * ph.q0 + t + 1)
            if t >= 2:
                act.wait_ge(turned_sem, t - 1)
            nc.scalar.activation(src[:, t % 2], acc[t % 4][:, 0:T], ACT.Copy).then_inc(out_of["act"], 1)

        def act_v_small(act, ph, t):
            _, _, small, _, big_out, small_out = VKIND[ph.kind]
            act.wait_ge(big_out, t + 1)
            nc.scalar.activation(small[0:B, t * P:(t + 1) * P], aux45[0:B, t % 2, 256:256 + P],
                                 ACT.Copy).then_inc(small_out, 1)

        def dve_v_tile(dve, ph, t):
            _, big, _, turned_sem, big_out, _ = VKIND[ph.kind]
            dve.wait_ge(turned_sem, t + 1)
            nc.vector.tensor_copy(big[:, :, t * P:(t + 1) * P],
                                  aux45[:, t % 2, 0:256].rearrange("p (c f) -> p c f", c=2)).then_inc(big_out, 1)

        def pe_v_tile(pe, ph, t):
            src, _, _, turned_sem, big_out, small_out = VKIND[ph.kind]
            pe.wait_ge(out_of["act"], ph.out0 + t + 1)
            if t >= 2:
                pe.wait_ge(big_out, t - 1)
                pe.wait_ge(small_out, t - 1)
            nc.tensor.transpose(aux45[:, t % 2, 0:P], src[:, t % 2, 0:P], ident)
            nc.tensor.transpose(aux45[:, t % 2, P:2 * P], src[:, t % 2, P:S], ident)
            nc.tensor.transpose(aux45[0:B, t % 2, 256:256 + P], src[:, t % 2, S:T], ident).then_inc(turned_sem, 1)

        def decay(h, a, b):
            t0 = TABLES["decay"][0] + h * 2 * P
            return tab[:, t0 + a:t0 + b]

        def pe_ret_a(pe, h):
            if h:
                pe.wait_ge(kdec_done, 2 * h)
                pe.wait_ge(orms_done, h)
                pe.wait_ge(adec_done, 2 * h)
            for c in range(2):
                for p in range(2):
                    last = nc.tensor.transpose(bank5[:, (2 * c + p) * P:(2 * c + p + 1) * P],
                                               kr[:, 2 * h + p, c * P:(c + 1) * P], ident)
            last.then_inc(kt_psum, 1)
            for p in range(2):
                nc.tensor.matmul(bank4[:, 0:S], kr[:, 2 * h + p, 0:P], qr[:, 2 * h + p, 0:S],
                                 start=p == 0, stop=p == 1)
            for p in range(2):
                last = nc.tensor.matmul(bank4[:, S:S + P], kr[:, 2 * h + p, P:S], qr[:, 2 * h + p, P:S],
                                        start=p == 0, stop=p == 1)
            last.then_inc(a_psum, 1)

        def act_ret_k(act, h):
            act.wait_ge(kt_psum, h + 1)
            if h:
                act.wait_ge(snew_psum, h)
            for c in range(2):
                col = TABLES["kdec"][0] + 2 * h + c
                nc.scalar.activation(k_dec[:, c], bank5[:, c * 2 * P:(c + 1) * 2 * P], ACT.Copy,
                                     scale=tab[:, col:col + 1]).then_inc(kdec_done, 1)

        def dve_ret_a(dve, h):
            dve.wait_ge(a_psum, h + 1)
            if h:
                dve.wait_ge(o_psum, h)
            nc.vector.tensor_tensor(a_dec[:, 0:S], bank4[:, 0:S], decay(h, 0, S), ALU.mult).then_inc(adec_done, 1)
            nc.vector.tensor_tensor(a_dec[:, S:S + P], bank4[:, S:S + P], decay(h, 0, P),
                                    ALU.mult).then_inc(adec_done, 1)

        def pe_ret_o(pe, h):
            pe.wait_ge(adec_done, 2 * h + 2)
            if h:
                pe.wait_ge(snew_out, 2 * h)
            for e in range(4):
                out = aux67[:, e // 2, (e % 2) * S:(e % 2 + 1) * S]
                cols = slice(h * RV + e * P, h * RV + (e + 1) * P)
                nc.tensor.matmul(out, v_ret[:, 0, cols], a_dec[:, 0:S], start=True, stop=False)
                last = nc.tensor.matmul(out[:, P:S], v_ret[:, 1, cols], a_dec[:, S:S + P], start=False, stop=True)
            last.then_inc(o_psum, 1)

        def act_ret_o(act, h):
            act.wait_ge(o_psum, h + 1)
            if h:
                act.wait_ge(ob_done, h)
            src = aux67[:].rearrange("p c (e f) -> p (c e) f", e=2)
            nc.scalar.activation(o_ret[:], src, ACT.Copy).then_inc(o_out, 1)
            nc.scalar.activation(o_sq[:], src, ACT.Square).then_inc(osq_done, 1)

        def dve_ret_sum(dve, h):
            dve.wait_ge(osq_done, h + 1)
            if h:
                dve.wait_ge(oms_psum, h)
            nc.vector.tensor_reduce(o_sum[:], o_sq[:].rearrange("p e f -> p f e"), AX.X, ALU.add).then_inc(osum_done, 1)

        def pe_ret_sum(pe, h):
            pe.wait_ge(osum_done, h + 1)
            pe.wait_ge(kdec_done, 2 * h + 2)
            nc.tensor.matmul(bank5[:, 0:S], ones, o_sum[:], start=True, stop=True).then_inc(oms_psum, 1)

        def act_ret_rms(act, h):
            act.wait_ge(oms_psum, h + 1)
            if h:
                act.wait_ge(ob_done, h)
            nc.scalar.activation(o_rms[:], bank5[:, 0:S], ACT.Sqrt, bias=eps, scale=1.0 / RV).then_inc(orms_done, 1)

        def dve_ret_norm(dve, ph, h):
            dve.wait_ge(orms_done, h + 1)
            nc.vector.reciprocal(o_rms[:], o_rms[:]).then_inc(orinv_done, 1)
            dve.wait_ge(orinv_done, h + 1)
            nc.vector.tensor_tensor(o_ret[:], o_ret[:], o_rms[:].unsqueeze(1).to_broadcast([P, 4, S]),
                                    ALU.mult).then_inc(on_done, 1)
            dve.wait_ge(on_done, h + 1)
            dve.wait_ge(out_of["dve"], ph.out0 + 4 * h + 4)
            nc.vector.tensor_tensor(ob[:, 4 * h:4 * h + 4, 0:S], ob[:, 4 * h:4 * h + 4, 0:S], o_ret[:],
                                    ALU.mult).then_inc(ob_done, 1)

        def pe_ret_state(pe, h):
            pe.wait_ge(kdec_done, 2 * h + 2)
            pe.wait_ge(osq_done, h + 1)
            for p in range(2):
                for c in range(2):
                    last = nc.tensor.matmul(aux67[:, p], k_dec[:, c, p * P:(p + 1) * P],
                                            v_ret[:, c, h * RV:(h + 1) * RV], start=c == 0, stop=c == 1)
            last.then_inc(snew_psum, 1)

        def act_ret_state(act, h):
            act.wait_ge(snew_psum, h + 1)
            if h:
                act.wait_ge(ret_stored, 16 * h)
            for p in range(2):
                nc.scalar.activation(s_new[:, p], aux67[:, p], ACT.Copy).then_inc(snew_out, 1)

        def act_gr_tile(act, ph, t):
            act.wait_ge(pe_half, 4 * ph.q0 + t + 1)
            if t >= 2:
                act.wait_ge(out_of["dve"], ph.out0 + t - 1)
            nc.scalar.activation(sig[:, t % 2], acc[t % 4][:, 0:T], ACT.Sigmoid).then_inc(sig_done, 1)

        def dve_gr_tile(dve, ph, t):
            dve.wait_ge(sig_done, t + 1)
            nc.vector.tensor_tensor(ob[:, t], sig[:, t % 2], acc[t % 4][:, 0:T], ALU.mult).then_inc(out_of["dve"], 1)

        def qk_tile(t, it):
            return qk[:, t] if not moving(it) else qk[:, bass.ds(t + 4 * it, 1)].squeeze(1)

        def act_qk_evac(act, ph, qq, j, it=0):
            t = 4 * qq + j
            act.wait_ge(pe_half, 4 * ph.q0 + t + 1 + 4 * it)
            if t >= 2:
                act.wait_ge(qk_ms_psum, t - 1 + 4 * it)
            nc.scalar.activation(qk_sq[:, j % 2], acc[j][:, 0:T], ACT.Square).then_inc(qk_sq_done, 1)
            col = 3 * KD + (0 if t < AT else 1)
            nc.scalar.activation(qk_tile(t, it), acc[j][:, 0:T], ACT.Copy,
                                 scale=gain[:, col:col + 1]).then_inc(out_of["act"], 1)

        def pe_qk_ms(pe, t, it=0):
            pe.wait_ge(qk_sq_done, t + 1 + 4 * it)
            if t:
                pe.wait_ge(qk_rms_done, t + 4 * it)
            nc.tensor.matmul(bank4[:, 0:T], blocks, qk_sq[:, t % 2], start=True, stop=True).then_inc(qk_ms_psum, 1)

        def act_qk_rms(act, t, it=0):
            act.wait_ge(qk_ms_psum, t + 1 + 4 * it)
            if t >= 2:
                act.wait_ge(qk_normed, t - 1 + 4 * it)
            nc.scalar.activation(qk_rms[:, t % 2], bank4[:, 0:T], ACT.Sqrt, bias=eps,
                                 scale=1.0 / AE).then_inc(qk_rms_done, 1)

        def dve_qk_norm(dve, ph, t, it=0):
            dve.wait_ge(qk_rms_done, t + 1 + 4 * it)
            nc.vector.reciprocal(qk_rms[:, t % 2], qk_rms[:, t % 2]).then_inc(qk_rinv, 1)
            dve.wait_ge(qk_rinv, t + 1 + 4 * it)
            dve.wait_ge(out_of["act"], ph.out0 + t + 1 + 4 * it)
            if t >= 2:
                dve.wait_ge(qk_rot_psum, t - 1 + 4 * it)
                dve.wait_ge(qk_cos, t - 1 + 4 * it)
            nc.vector.tensor_tensor(qk_n[:, t % 2], qk_tile(t, it), qk_rms[:, t % 2], ALU.mult).then_inc(qk_normed, 1)

        def pe_qk_rot(pe, t, it=0):
            pe.wait_ge(qk_normed, t + 1 + 4 * it)
            if t:
                pe.wait_ge(qk_sin, t + 4 * it)
            nc.tensor.matmul(bank5[:, 0:T], turn, qk_n[:, t % 2], start=True, stop=True).then_inc(qk_rot_psum, 1)

        def pool_qk_rot(pool, t, it=0, step=4):
            pool.wait_ge(qk_normed, t + 1 + step * it)
            if t >= 2:
                pool.wait_ge(qk_done, t - 1 + step * it)
            nc.gpsimd.tensor_tensor(rot_c[:, t % 2], qk_n[:, t % 2], const("cos_a"), ALU.mult).then_inc(qk_cos, 1)

        def dve_qk_rot(dve, t, it=0):
            dve.wait_ge(qk_rot_psum, t + 1 + 4 * it)
            if t >= 2:
                dve.wait_ge(qk_done, t - 1 + 4 * it)
            nc.vector.tensor_tensor(rot_s[:, t % 2], bank5[:, 0:T], const("sin_a"), ALU.mult).then_inc(qk_sin, 1)
            dve.wait_ge(qk_sin, t + 1 + 4 * it)
            dve.wait_ge(qk_cos, t + 1 + 4 * it)
            nc.vector.tensor_tensor(qk_tile(t, it), rot_c[:, t % 2], rot_s[:, t % 2], ALU.add).then_inc(qk_done, 1)

        def col_b(t, c, b, it):
            return t[:, c, b:b + 1] if not moving(it) else t[:, c, bass.ds(b + it, 1)]

        def sp_state_load(sp, b, h, it=0):
            src = state_in[bass.ds(b + it, 1), h].squeeze(0) if moving(it) else state_in[b + it, h]
            src = src.rearrange("(p r) e -> p (r e)", r=2)
            if b:
                sp.wait_ge(state_stored[h], 16 * b + 16 * it)
            sp.dma_start(state[:, h], src).then_inc(state_in_sem[h], 16)

        def sp_state_store(sp, b, h, it=0):
            sp.wait_ge(os_psum, 4 * b + h + 1 + 4 * it)
            dst = state_out[b + it, h] if not moving(it) else state_out[bass.ds(b + it, 1), h].squeeze(0)
            sp.dma_start(dst.rearrange("(p r) e -> p (r e)", r=2), state[:, h]).then_inc(state_stored[h], 16)

        def dve_state_v(dve, b, h, it=0):
            s = 4 * b + h
            if s >= 2:
                dve.wait_ge(vb_psum, s - 1 + 4 * it)
            e0 = TABLES["ident"][0]
            onehot = tab[0:B, bass.ds(e0 + b + it, 1)] if moving(it) else tab[0:B, e0 + b:e0 + b + 1]
            nc.vector.tensor_scalar(v_mask[0:B, h % 2], vs_ret[0:B, h * RV:(h + 1) * RV], onehot, None,
                                    ALU.mult).then_inc(vmask_done, 1)

        def pe_state_v(pe, b, h, it=0):
            s = 4 * b + h
            pe.wait_ge(vmask_done, s + 1 + 4 * it)
            if s:
                pe.wait_ge(state_new, 2 * s + 8 * it)
            nc.tensor.matmul(bank6[:, :], ones[0:B, :], v_mask[0:B, h % 2], start=True, stop=True).then_inc(vb_psum, 1)

        def act_state(act, b, h, it=0):
            act.wait_ge(state_in_sem[h], 16 * (b + 1) + 16 * it)
            g0 = TABLES["gamma"][0] + h
            nc.scalar.activation(state[:, h], state[:, h], ACT.Copy, scale=tab[:, g0:g0 + 1]).then_inc(state_scaled, 1)

        def dve_state(dve, b, h, it=0):
            s = 4 * b + h
            dve.wait_ge(state_scaled, s + 1 + 4 * it)
            dve.wait_ge(vb_psum, s + 1 + 4 * it)
            for p in range(2):
                half = state[:, h, p * RV:(p + 1) * RV]
                nc.vector.scalar_tensor_tensor(half, bank6[:, :], col_b(kr_s, 2 * h + p, b, it), half,
                                               ALU.mult, ALU.add).then_inc(state_new, 1)

        def pe_state_o(pe, b, h, it=0):
            s = 4 * b + h
            pe.wait_ge(state_new, 2 * s + 2 + 8 * it)
            if s:
                pe.wait_ge(os_out, s + 4 * it)
            for e in range(4):
                for p in range(2):
                    last = nc.tensor.matmul(bank7[:, 8 * (h % 2) + e:8 * (h % 2) + e + 1],
                                            state[:, h, p * RV + e * P:p * RV + (e + 1) * P],
                                            col_b(qr_s, 2 * h + p, b, it), start=p == 0, stop=p == 1)
            last.then_inc(os_psum, 1)

        def act_state_o(act, b, h, it=0):
            s = 4 * b + h
            act.wait_ge(os_psum, s + 1 + 4 * it)
            dst = o_s[:, 4 * h:4 * h + 4, b] if not moving(it) else o_s[:, 4 * h:4 * h + 4, bass.ds(b + it, 1)].squeeze(2)
            nc.scalar.activation(dst, bank7[:, 8 * (h % 2):8 * (h % 2) + 4], ACT.Copy).then_inc(os_out, 1)

        def pe_scores(pe, i):
            h, qb = i // 2, i % 2
            if i:
                pe.wait_ge(att_masked, i)
            rows = slice((h % 2) * AE, (h % 2 + 1) * AE)
            keys = (qb + 1) * P
            for g in range(G):
                t = g * 4 + h // 2
                last = nc.tensor.matmul(aux45[:, g // 2, (g % 2) * S + (S - keys if qb == 0 else 0):
                                              (g % 2) * S + S],
                                        qk[rows, t, qb * P:(qb + 1) * P], qk[rows, AT + t, 0:keys],
                                        start=True, stop=True)
            last.then_inc(att_scores, 1)

        def att_view(t, qb):
            return t[:, :, P:2 * P] if qb == 0 else t

        def dve_scores(dve, i):
            qb = i % 2
            dve.wait_ge(att_scores, i + 1)
            if i:
                dve.wait_ge(att_turned, i)
            scores = aux45[:].rearrange("p c f -> p (c f)")[:, 0:G * S].rearrange("p (g k) -> p g k", g=G)
            mask = const("mask").rearrange("p (g k) -> p g k", g=G)
            nc.vector.tensor_tensor(att_view(prob[:], qb), att_view(scores, qb), att_view(mask, qb),
                                    ALU.add).then_inc(att_masked, 1)
            dve.wait_ge(att_masked, i + 1)
            nc.vector.tensor_reduce(att_m[:, 0:1], att_view(prob[:], qb), AX.XY, ALU.max).then_inc(att_step, 1)
            dve.wait_ge(att_step, 2 * i + 1)
            nc.vector.tensor_scalar(att_m[:, 1:2], att_m[:, 0:1], -SCALE, None, ALU.mult).then_inc(att_negmax, 1)

        att_step = sem("att_step")

        def act_exp(act, i):
            act.wait_ge(att_negmax, i + 1)
            view = att_view(prob[:], i % 2)
            nc.scalar.activation(view, view, ACT.Exp, bias=att_m[:, 1:2], scale=SCALE,
                                 accum_out=att_m[:, 2:3]).then_inc(att_exp, 1)

        def dve_prob(dve, i):
            dve.wait_ge(att_exp, i + 1)
            nc.vector.reciprocal(att_m[:, 3:4], att_m[:, 2:3]).then_inc(att_step, 1)
            dve.wait_ge(att_step, 2 * i + 2)
            view = att_view(prob[:], i % 2)
            nc.vector.tensor_scalar(view, view, att_m[:, 3:4], None, ALU.mult).then_inc(att_prob, 1)

        def att_blocks(i):
            return [(g, kb) for g in range(G) for kb in range(i % 2 + 1)]

        def turned_copies(i):
            return 3 * ((i + 1) // 2) + (i + 1) % 2

        def pe_turn(pe, i):
            pe.wait_ge(att_prob, i + 1)
            if i:
                pe.wait_ge(att_out, i)
            for n, (g, kb) in enumerate(att_blocks(i)):
                c = kb * P if i % 2 else P
                last = nc.tensor.transpose(aux67[:, n // 4, (n % 4) * P:(n % 4 + 1) * P], prob[:, g, c:c + P], ident)
            last.then_inc(att_turned, 1)

        def turned_copy(eng, i, part):
            n = len(att_blocks(i))
            a, b = (0, min(n, 4)) if part == 0 else (4, n)
            if a >= b:
                return
            eng.wait_ge(att_turned, i + 1)
            if i:
                eng.wait_ge(att_pv, i)
            src = aux67[:].rearrange("p c f -> p (c f)")[:, a * P:b * P]
            if part == 0:
                nc.scalar.activation(probT[:, a * P:b * P], src, ACT.Copy).then_inc(att_turned_out, 1)
            else:
                nc.vector.tensor_copy(probT[:, a * P:b * P], src).then_inc(att_turned_out, 1)

        def pe_pv(pe, i):
            h, qb = i // 2, i % 2
            pe.wait_ge(att_turned_out, turned_copies(i))
            blks = att_blocks(i)
            out = bank7[(h % 2) * AE:(h % 2 + 1) * AE, 256:256 + P]
            for n, (g, kb) in enumerate(blks):
                last = nc.tensor.matmul(out, v_tok[:, kb, g * AW + h * AE:g * AW + (h + 1) * AE],
                                        probT[:, n * P:(n + 1) * P], start=n == 0, stop=n == len(blks) - 1)
            last.then_inc(att_pv, 1)

        def act_pv(act, i):
            h, qb = i // 2, i % 2
            act.wait_ge(att_pv, i + 1)
            rows = slice((h % 2) * AE, (h % 2 + 1) * AE)
            nc.scalar.activation(oa[rows, h // 2, qb * P:(qb + 1) * P], bank7[rows, 256:256 + P],
                                 ACT.Copy).then_inc(att_out, 1)

        def sp_kv_load(sp, n, part):
            i = n % (B * G)
            b, g = i // G, i % G
            if n >= 3:
                m = n - 3
                if m < B * G:
                    sp.wait_ge(kq_done, 2 * m + 2)
                else:
                    sp.wait_ge(dec_v_done, m - B * G + 1)
            dil = GROUPS[g][1]
            src = caches[g][b].rearrange("(p d) c -> p d c", d=dil)[:, 0, part * AW:(part + 1) * AW]
            sp.dma_start(kv[:, n % 3], src).then_inc(kv_in[n % 3], 16)

        def pool_dec_q(pool, i):
            b, g = i // G, i % G
            if i:
                pool.wait_ge(qb_psum, i)
            e0 = TABLES["ident"][0]
            nc.gpsimd.tensor_scalar(q_mask[0:B, :], q_s[0:B, g * AW:(g + 1) * AW], tab[0:B, e0 + b:e0 + b + 1], None,
                                    ALU.mult).then_inc(qmask_done, 1)

        def pe_dec_q(pe, i):
            pe.wait_ge(qmask_done, i + 1)
            if i >= 2:
                pe.wait_ge(kq_done, 2 * (i - 2) + 1)
            nc.tensor.matmul(aux45[:, i % 2], ones[0:B, :], q_mask[0:B, :], start=True, stop=True).then_inc(qb_psum, 1)

        def dve_dec_k(dve, i):
            b, g = i // G, i % G
            dve.wait_ge(kv_in[i % 3], 16 * (i // 3 + 1))
            dve.wait_ge(qb_psum, i + 1)
            nc.vector.tensor_tensor(kv[:, i % 3], kv[:, i % 3], aux45[:, i % 2], ALU.mult).then_inc(kq_done, 1)
            dve.wait_ge(kq_done, 2 * i + 1)
            out = dec_s[:, g].rearrange("p (r n b) -> p n r b", r=2, b=B)[:, :, :, b]
            nc.vector.tensor_reduce(out, kv[:, i % 3].rearrange("p (n r e) -> p n r e", r=2, e=AE), AX.X,
                                    ALU.add).then_inc(kq_done, 1)

        def dve_dec_own(dve):
            nc.vector.tensor_tensor(qk_own[:], qk[:, 0:AT, S:T], qk[:, AT:2 * AT, S:T], ALU.mult).then_inc(dec_dve, 1)

        def pe_dec_scores(pe):
            pe.wait_ge(dec_dve, 1)
            pe.wait_ge(kq_done, 2 * B * G)
            for g in range(G):
                nc.tensor.transpose(bank6[0:64, g * P:(g + 1) * P], dec_s[:, g], ident)
            for g in range(G):
                for r in range(2):
                    last = nc.tensor.matmul(bank6[32 * r:32 * r + 32, G * P + g:G * P + g + 1],
                                            qk_own[:, 4 * g:4 * g + 4].rearrange("p n b -> p (n b)"),
                                            blocks[:, r * AE:r * AE + 1], start=True, stop=True)
            last.then_inc(dec_pe, 1)

        NK = G * P + G

        def dve_dec_max(dve):
            dve.wait_ge(dec_pe, 1)
            nc.vector.tensor_reduce(dec_m[0:64, 0:1], bank6[0:64, 0:NK], AX.X, ALU.max).then_inc(dec_dve, 1)
            dve.wait_ge(dec_dve, 2)
            nc.vector.tensor_scalar(dec_m[0:64, 1:2], dec_m[0:64, 0:1], -SCALE, None, ALU.mult).then_inc(dec_dve, 1)

        def act_dec_exp(act):
            act.wait_ge(dec_dve, 3)
            nc.scalar.activation(dec_p[0:64, :], bank6[0:64, 0:NK], ACT.Exp, bias=dec_m[0:64, 1:2], scale=SCALE,
                                 accum_out=dec_m[0:64, 2:3]).then_inc(dec_act, 1)

        def dve_dec_prob(dve):
            dve.wait_ge(dec_act, 1)
            nc.vector.reciprocal(dec_m[0:64, 3:4], dec_m[0:64, 2:3]).then_inc(dec_dve, 1)
            dve.wait_ge(dec_dve, 4)
            nc.vector.tensor_scalar(dec_p[0:64, :], dec_p[0:64, :], dec_m[0:64, 3:4], None,
                                    ALU.mult).then_inc(dec_dve, 1)
            dve.wait_ge(dec_dve, 5)
            for g in range(G):
                nc.vector.tensor_scalar(dec_diag[0:64, g], ident[0:64, 0:64], dec_p[0:64, G * P + g:G * P + g + 1],
                                        None, ALU.mult).then_inc(dec_dve, 1)

        def pe_dec_turn(pe):
            pe.wait_ge(dec_dve, 5 + G)
            for g in range(G):
                nc.tensor.transpose(bank5[:, g * 64:(g + 1) * 64], dec_p[0:64, g * P:(g + 1) * P], ident[0:64, 0:64])
            nc.tensor.matmul(bank4[0:B, 0:G * 64], const("rsel", 64), dec_diag[0:64].rearrange("p g r -> p (g r)"),
                             start=True, stop=True).then_inc(dec_pe, 1)

        def act_dec_turn(act):
            act.wait_ge(dec_pe, 2)
            nc.scalar.activation(dec_pT[:].rearrange("p g r -> p (g r)"), bank5[:, 0:G * 64],
                                 ACT.Copy).then_inc(dec_act, 1)
            nc.scalar.activation(dec_own[0:B].rearrange("p g r -> p (g r)"), bank4[0:B, 0:G * 64],
                                 ACT.Copy).then_inc(dec_act, 1)

        def pe_dec_own(pe):
            pe.wait_ge(dec_act, 3)
            for g in range(G):
                for n in range(4):
                    nc.tensor.matmul(bank7[:, n * 16:(n + 1) * 16].rearrange("p (r b) -> p r b", r=2),
                                     v_s[0:B, g * AW + n * P:g * AW + (n + 1) * P],
                                     dec_own[0:B, g].rearrange("p (r n b) -> p n r b", r=2, b=B)[:, n],
                                     start=g == 0 and n == 0, stop=False, skip_group_check=True)

        def pe_dec_v(pe, i):
            b, g = i // G, i % G
            n0 = B * G + i
            pe.wait_ge(kv_in[n0 % 3], 16 * (n0 // 3 + 1))
            for n in range(4):
                out = bank7[:, n * 16:(n + 1) * 16].rearrange("p (r b) -> p r b", r=2)[:, :, b]
                last = nc.tensor.matmul(out, kv[:, n0 % 3, n * P:(n + 1) * P],
                                        dec_pT[:, g].rearrange("p (r n b) -> p n r b", r=2, b=B)[:, n, :, b],
                                        start=False, stop=i == B * G - 1, skip_group_check=True)
            last.then_inc(dec_v_done, 1)

        def dve_dec_out(dve):
            dve.wait_ge(dec_v_done, B * G)
            for r in range(2):
                rows = slice(r * AE, (r + 1) * AE)
                nc.vector.tensor_copy(oa[rows, :, S:T],
                                      bank7[rows, 0:64].rearrange("p (n r b) -> p n r b", r=2, b=B)[:, :, r]
                                      ).then_inc(dec_dve, 1)
        DEC_DVE = 5 + G + 2

        fi1, fo1, p_qr, p_kr, p_vr, p_gr, p_qk, p_v, p_gb, p_pb, p_ga, p_pa, p_wo, fi2, fo2 = phases
        NSTATE_LOOP = p_qk.quads
        DEC_SLOTS = 4 * p_gb.quads

        block = ctx.enter_context(nc.Block())

        @block.sync
        def _(sp):
            sp.dma_start(x[:], xT).then_inc(const_in, 16)
            sp.dma_start(tab[:], tables).then_inc(const_in, 16)
            sp.dma_start(gain[:], gains).then_inc(const_in, 16)

            ROWS = 256
            pieces = []
            for g in (2, 1, 0):
                n = caches[g].shape[0] * caches[g].shape[1]
                src = caches[g].rearrange("b w c -> (b w) c")
                dst = kv_outs[g].rearrange("b w c -> (b w) c")
                for a in range(0, n, ROWS):
                    if a + ROWS < n:
                        pieces.append((dst, src, a, ROWS))
                    else:
                        pieces += [(dst, src, a, ROWS - 16), (dst, src, a + ROWS - 16, 15)]

            def roll(sp, c, it=0):
                dst, src, a, rows = pieces[c]
                if not moving(it):
                    sp.dma_start(dst[a:a + rows], src[a + 1:a + 1 + rows]).then_inc(rolled, 16)
                else:
                    sp.dma_start(dst[bass.ds(a + ROWS * it, rows)],
                                 src[bass.ds(a + 1 + ROWS * it, rows)]).then_inc(rolled, 16)

            with sp.Fori(0, fi1.quads + fo1.quads - 1) as it:
                sp.wait_ge(pe_half, 4 * it + 2)
                roll(sp, 0, 2 * it)
                roll(sp, 1, 2 * it)
            done = 2 * (fi1.quads + fo1.quads - 1)

            def roll_more(sp, n):
                nonlocal done
                for _ in range(n):
                    if done < len(pieces):
                        roll(sp, done)
                        done += 1

            for q in range(p_qr.q0, p_gr.q0 + p_gr.quads):
                sp.wait_ge(pe_half, 4 * q)
                roll_more(sp, 1)
                if q >= p_gr.q0 + 1:
                    h = q - p_gr.q0 - 1
                    sp.wait_ge(snew_out, 2 * h + 2)
                    sp.dma_start(ret_out[h].rearrange("(p r) e -> p (r e)", r=2),
                                 s_new[:].rearrange("p r e -> p (r e)")).then_inc(ret_stored, 16)
            sp.wait_ge(snew_out, 2 * RH)
            sp.dma_start(ret_out[RH - 1].rearrange("(p r) e -> p (r e)", r=2),
                         s_new[:].rearrange("p r e -> p (r e)")).then_inc(ret_stored, 16)
            for h in range(RH):
                sp_state_load(sp, 0, h)
            with sp.Fori(0, NSTATE_LOOP) as it:
                for h in range(RH):
                    sp_state_store(sp, 0, h, it)
                    sp_state_load(sp, 1, h, it)
            sp_state_done = NSTATE_LOOP
            for b in range(sp_state_done, B):
                for h in range(RH):
                    sp_state_store(sp, b, h)
                    if b + 1 < B:
                        sp_state_load(sp, b + 1, h)
            for h in range(RH):
                sp.wait_ge(state_stored[h], 16 * B)
            sp.wait_ge(qk_done, 2 * AT)
            sp.dma_start(kT_out, qk[:, AT:2 * AT]).then_inc(stored, 16)
            sp.wait_ge(v_out_sem, AT)
            sp.dma_start(v_out.rearrange("(c p) f -> p c f", c=2), v_tok[:]).then_inc(stored, 16)
            for n in range(2 * B * G):
                sp_kv_load(sp, n, n // (B * G))
                if n % 3 == 2:
                    roll_more(sp, 1)
            for q in range(p_pb.q0 + 2, p_wo.q0):
                sp.wait_ge(pe_half, 4 * q)
                roll_more(sp, 1)
            q = fi2.q0
            while done < len(pieces):
                sp.wait_ge(pe_half, 4 * q)
                roll_more(sp, 2)
                q += 1
            sp.wait_ge(rolled, 16 * len(pieces))
            sp.wait_ge(qks_out, 6)
            sp.wait_ge(vs_out, AT)
            for g in range(G):
                w = caches[g].shape[1]
                sp.dma_start(kv_outs[g][:, w - 1, 0:AW], k_s[0:B, g * AW:(g + 1) * AW]).then_inc(stored, 16)
                sp.dma_start(kv_outs[g][:, w - 1, AW:2 * AW], v_s[0:B, g * AW:(g + 1) * AW]).then_inc(stored, 16)
            for m in range(KD):
                sp.wait_ge(out_of["dve"], fo2.out0 + m + 1)
                sp.dma_start(yT[:, m], x[:, m]).then_inc(stored, 16)
            sp.wait_ge(stored, 16 * STORES)
            sp.wait_ge(ret_stored, 16 * RH)

        @block.scalar
        def _(act):
            load_unit(act, 0)
            load_unit(act, 1)
            act.wait_ge(const_in, 48)
            for m in range(KD):
                act_square(act, 0, m)
            hi_half(act, 0, 0)
            hi_half(act, 0, 1)
            act_norm(act, 0)
            hi_half(act, 0, 2)
            hi_half(act, 0, 3)
            act.wait_ge(lo_done, 2)
            load_unit(act, 2)

            def ffn(fi, fo, norm):
                act_fi_quad(act, fi, 0)
                with act.Fori(0, fi.quads - 3) as it:
                    act_fi_quad(act, fi, 1, it)
                for qq in range(fi.quads - 2, fi.quads):
                    act_fi_quad(act, fi, qq)
                with act.Fori(0, fo.quads // 2 - 1) as it:
                    for m in range(2):
                        act_fo_quad(act, fo, m, 2 * it, norm)
                for m in range(fo.quads - 2, fo.quads):
                    act_fo_quad(act, fo, m, 0, norm)

            ffn(fi1, fo1, 1)
            act_norm(act, 1)
            for which, ph in enumerate((p_qr, p_kr)):
                for qq in range(ph.quads):
                    act_rr_quad(act, ph, qq, which)
            for t in range(16):
                act_ahead(act, p_vr.q0 + t // 4, t % 4)
                act_v_tile(act, p_vr, t)
                if t:
                    act_v_small(act, p_vr, t - 1)
            act_v_small(act, p_vr, 15)
            act.wait_ge(rr_done, 2 * RH)
            act.wait_ge(rr_pool, 6 * RH)
            nc.scalar.activation(qr_s[:], qr[:, :, S:T], ACT.Copy).then_inc(rs_copied, 1)
            nc.scalar.activation(kr_s[:], kr[:, :, S:T], ACT.Copy).then_inc(rs_copied, 1)
            for h in range(RH):
                act_ret_k(act, h)
                for j in range(4):
                    act_ahead(act, p_gr.q0 + h, j)
                    act_gr_tile(act, p_gr, 4 * h + j)
                    if j == 0:
                        act_ret_o(act, h)
                    if j == 2:
                        act_ret_state(act, h)
                        act_ret_rms(act, h)

            def qk_quad(qq, b, it=0):
                for j in range(4):
                    act_ahead(act, p_qk.q0 + qq, j, it)
                    act_qk_evac(act, p_qk, qq, j, it)
                    act_state(act, b, j, it)
                    if j:
                        act_qk_rms(act, 4 * qq + j - 1, it)
                        act_state_o(act, b, j - 1, it)
                act_qk_rms(act, 4 * qq + 3, it)
                act_state_o(act, b, 3, it)

            qk_quad(0, 0)
            with act.Fori(0, p_qk.quads // 2 - 1) as it:
                qk_quad(1, 1, it)
            with act.Fori(0, p_qk.quads // 2) as it:
                qk_quad(3, 3, it)
            for t in range(AT):
                act_ahead(act, p_v.q0 + t // 4, t % 4)
                act_v_tile(act, p_v, t)
                if t < 8:
                    act_state(act, 6 + t // 4, t % 4)
                if t:
                    act_v_small(act, p_v, t - 1)
                if 1 <= t <= 8:
                    act_state_o(act, 6 + (t - 1) // 4, (t - 1) % 4)
            act_v_small(act, p_v, AT - 1)
            for n in range(6):
                act.wait_ge(qks_psum, n + 1)
                dst = (q_s[0:B, :] if n < 3 else k_s)[:, (n % 3) * AW:(n % 3 + 1) * AW]
                nc.scalar.activation(dst, aux67[0:B, n % 2], ACT.Copy).then_inc(qks_out, 1)
            act.wait_ge(os_out, B * RH)
            nc.scalar.activation(o_s2[:], o_s[:], ACT.Square).then_inc(small_act, 1)
            act.wait_ge(small_pe, 1)
            nc.scalar.activation(os_sum[:].rearrange("p h b -> p (h b)"), bank4[:, 0:RH * B], ACT.Sqrt, bias=eps,
                                 scale=1.0 / RV).then_inc(small_act, 1)
            act.wait_ge(small_step, 4)
            for h in range(RH):
                act.wait_ge(state_stored[h], 16 * B)
            for h in range(RH):
                nc.scalar.activation(obh[:, 4 * h:4 * h + 4], ob[:, 4 * h:4 * h + 4], ACT.Copy).then_inc(ob_hi, 1)
            act.wait_ge(ob_split, RH)
            for t in range(KD):
                act_ahead(act, p_gb.q0 + t // 4, t % 4)
                act.wait_ge(pe_half, 4 * p_gb.q0 + t + 1)
                nc.scalar.activation(gate_b[:, t], acc[t % 4][:, 0:T], ACT.Sigmoid).then_inc(out_of["act"], 1)
            act_dec_exp(act)
            act_dec_turn(act)
            for i in range(8):
                act_ahead(act, p_pb.q0 + i // 4, i % 4)

            def att(i):
                if i >= 1:
                    turned_copy(act, i - 1, 0)
                if i < 16:
                    act_exp(act, i)

            for i in range(8):
                att(i)
                if i >= 1:
                    act_pv(act, i - 1)
                act_ahead(act, p_pb.q0 + 2 + i // 4, i % 4)
            for t in range(KD):
                att(8 + t)
                act_pv(act, 7 + t)
                act_ahead(act, p_ga.q0 + t // 4, t % 4)
                act.wait_ge(pe_half, 4 * p_ga.q0 + t + 1)
                nc.scalar.activation(gate_a[:, t], acc[t % 4][:, 0:T], ACT.Sigmoid).then_inc(out_of["act"], 1)
            att(16)
            act_pv(act, 15)
            act.wait_ge(att_out, 16)
            act.wait_ge(dec_dve, DEC_DVE)
            nc.scalar.activation(oah[:], oa[:], ACT.Copy).then_inc(oa_hi, 1)
            for j in range(4):
                act_ahead(act, p_pa.q0, j)
                for m in (2 * j, 2 * j + 1):
                    act.wait_ge(merge_done, m + 1)
                    nc.scalar.activation(hh[:, m], merge[:, m % 2], ACT.Copy).then_inc(merge_hi, 1)
            for m in range(KD):
                act_ahead(act, p_wo.q0 + m // 4, m % 4)
                act.wait_ge(out_of["dve"], p_wo.out0 + m + 1)
                act_square(act, 2, m)
            act_norm(act, 2)
            ffn(fi2, fo2, None)

        @block.vector
        def _(dve):
            dve.wait_ge(const_in, 48)
            for m in range(KD):
                dve_sum_square(dve, 0, m)
            lo_half(dve, 0, 0)
            lo_half(dve, 0, 1)
            dve_norm(dve, 0)
            lo_half(dve, 0, 2)
            lo_half(dve, 0, 3)

            def ffn(fi, fo, norm):
                dve_fi_quad(dve, fi, 0)
                with dve.Fori(0, fi.quads - 3) as it:
                    dve_fi_quad(dve, fi, 1, it)
                for qq in range(fi.quads - 2, fi.quads):
                    dve_fi_quad(dve, fi, qq)
                start = 0
                if norm is not None:
                    for m in range(2):
                        dve_fo_quad(dve, fo, m, 0, norm)
                    start = 2
                with dve.Fori(0, (fo.quads - 2 - start) // 2) as it:
                    for m in range(start, start + 2):
                        dve_fo_quad(dve, fo, m, 2 * it, norm)
                for m in range(fo.quads - 2, fo.quads):
                    dve_fo_quad(dve, fo, m, 0, norm)

            ffn(fi1, fo1, 1)
            dve_norm(dve, 1)
            for which, ph in enumerate((p_qr, p_kr)):
                for t in range(2 * RH):
                    dve_ahead(dve, ph.q0 + t // 4, t % 4)
                    if t % 2:
                        turn_head(dve, nc.vector, ph, t // 2, which)
            for t in range(16):
                dve_ahead(dve, p_vr.q0 + t // 4, t % 4)
                if t:
                    dve_v_tile(dve, p_vr, t - 1)
            dve_v_tile(dve, p_vr, 15)
            for h in range(RH):
                dve_ret_a(dve, h)
                for j in range(4):
                    dve_ahead(dve, p_gr.q0 + h, j)
                    dve_gr_tile(dve, p_gr, 4 * h + j)
                    if j == 1:
                        dve_ret_sum(dve, h)
                dve_ret_norm(dve, p_gr, h)

            def qk_quad(qq, b, it=0):
                for j in range(4):
                    dve_state_v(dve, b, j, it)
                    dve_ahead(dve, p_qk.q0 + qq, j, it)
                    dve_state(dve, b, j, it)
                    if j:
                        dve_qk_norm(dve, p_qk, 4 * qq + j - 1, it)
                    if j >= 2:
                        dve_qk_rot(dve, 4 * qq + j - 2, it)
                dve_qk_norm(dve, p_qk, 4 * qq + 3, it)
                dve_qk_rot(dve, 4 * qq + 2, it)
                dve_qk_rot(dve, 4 * qq + 3, it)

            qk_quad(0, 0)
            with dve.Fori(0, p_qk.quads - 1) as it:
                qk_quad(1, 1, it)
            for t in range(AT):
                if t < 8:
                    dve_state_v(dve, 6 + t // 4, t % 4)
                dve_ahead(dve, p_v.q0 + t // 4, t % 4)
                if t < 8:
                    dve_state(dve, 6 + t // 4, t % 4)
                if t:
                    dve_v_tile(dve, p_v, t - 1)
            dve_v_tile(dve, p_v, AT - 1)
            dve.wait_ge(small_act, 1)
            nc.vector.tensor_reduce(os_sum[:], o_s2[:].rearrange("p (h e) b -> p h b e", e=4), AX.X,
                                    ALU.add).then_inc(small_step, 1)
            dve.wait_ge(small_act, 2)
            nc.vector.reciprocal(os_sum[:], os_sum[:]).then_inc(small_step, 1)
            dve.wait_ge(small_step, 2)
            nc.vector.tensor_tensor(o_s[:].rearrange("p (h e) b -> p h e b", e=4),
                                    o_s[:].rearrange("p (h e) b -> p h e b", e=4),
                                    os_sum[:].unsqueeze(2).to_broadcast([P, RH, 4, B]), ALU.mult).then_inc(small_step, 1)
            dve.wait_ge(small_step, 3)
            nc.vector.tensor_tensor(ob[:, :, S:T], ob[:, :, S:T], o_s[:], ALU.mult).then_inc(small_step, 1)
            dve_dec_own(dve)
            for t in range(KD):
                dve_ahead(dve, p_gb.q0 + t // 4, t % 4)
                for i in range(3 * t, 3 * t + 3):
                    dve_dec_k(dve, i)
            dve_dec_max(dve)
            dve_dec_prob(dve)

            def pb_tile(m):
                dve.wait_ge(pe_half, 4 * p_pb.q0 + 2 * m + 2)
                nc.vector.tensor_tensor(gate_b[:, m], gate_b[:, m], acc[m % 4][:, 0:T],
                                        ALU.mult).then_inc(out_of["dve"], 1)

            dve.wait_ge(out_of["act"], p_gb.out0 + KD)
            for i in range(8):
                dve_ahead(dve, p_pb.q0 + i // 4, i % 4)
                if i % 2:
                    pb_tile(i // 2)
            dve_dec_out(dve)

            def att(i):
                if i >= 1:
                    turned_copy(dve, i - 1, 1)
                if i < 16:
                    dve_scores(dve, i)
                    dve_prob(dve, i)

            for i in range(8):
                att(i)
                dve_ahead(dve, p_pb.q0 + 2 + i // 4, i % 4)
                if i % 2:
                    pb_tile(4 + i // 2)
            for t in range(KD):
                att(8 + t)
                dve_ahead(dve, p_ga.q0 + t // 4, t % 4)
            att(16)
            dve.wait_ge(oa_hi, 1)
            nc.vector.tensor_tensor(oal[:], oa[:], oah[:].bitcast(F32), ALU.subtract).then_inc(oa_split, 1)
            dve.wait_ge(out_of["act"], p_ga.out0 + KD)
            for j in range(4):
                dve_ahead(dve, p_pa.q0, j)
                for m in (2 * j, 2 * j + 1):
                    dve.wait_ge(pe_half, 4 * p_pa.q0 + j + 1)
                    if m >= 2:
                        dve.wait_ge(merge_done, m - 1)
                    nc.vector.tensor_tensor(merge_a[:, m % 2], gate_a[:, m], acc[m % 4][:, 0:T],
                                            ALU.mult).then_inc(out_of["dve"], 1)
            for m in range(KD):
                dve_ahead(dve, p_wo.q0 + m // 4, m % 4)
                dve.wait_ge(pe_half, 4 * p_wo.q0 + m + 1)
                dve_add_x(dve, p_wo, m, 1.0, m % 4)
                dve_sum_square(dve, 2, m)
            dve_norm(dve, 2)
            ffn(fi2, fo2, None)

        @block.gpsimd
        def _(pool):
            def ffn(fi):
                with pool.Fori(0, fi.quads) as it:
                    pool_fi_quad(pool, fi, 0, it)

            pool_norm(pool, 0)
            ffn(fi1)
            pool_norm(pool, 1)
            for which, ph in enumerate((p_qr, p_kr)):
                for h in range(RH):
                    turn_head(pool, nc.gpsimd, ph, h, which)

            for t in range(2):
                pool_qk_rot(pool, t)
            with pool.Fori(0, AT - 1) as it:
                for t in range(2, 4):
                    pool_qk_rot(pool, t, it, 2)
            for h in range(RH):
                pool.wait_ge(ob_hi, h + 1)
                nc.gpsimd.tensor_tensor(obl[:, 4 * h:4 * h + 4], ob[:, 4 * h:4 * h + 4],
                                        obh[:, 4 * h:4 * h + 4].bitcast(F32), ALU.subtract).then_inc(ob_split, 1)
            pool.wait_ge(qks_out, 3)
            for i in range(B * G):
                pool_dec_q(pool, i)
            for m in range(KD):
                pool.wait_ge(out_of["dve"], p_pa.out0 + m + 1)
                if m >= 2:
                    pool.wait_ge(merge_split, m - 1)
                nc.gpsimd.tensor_tensor(merge[:, m % 2], merge_a[:, m % 2], gate_b[:, m], ALU.add).then_inc(merge_done, 1)
                pool.wait_ge(merge_hi, m + 1)
                nc.gpsimd.tensor_tensor(hl[:, m], merge[:, m % 2], hh[:, m].bitcast(F32),
                                        ALU.subtract).then_inc(merge_split, 1)
            pool_norm(pool, 2)
            ffn(fi2)

        @block.tensor
        def _(pe):
            def ffn(fi, fo, r):
                pe_enter(pe, fi)
                norm = (normed_split, KD * r)
                pe_wide_first(fi, norm)
                with pe.Fori(0, fi.quads - 1) as it:
                    for j in range(4):
                        pe_wide_half(pe, fi, 1, j, it)
                with pe.Fori(0, fo.quads // 2) as it:
                    for m in range(2):
                        pe_fo_quad(pe, fo, m, m, 2 * it)

            def pe_wide_first(ph, norm):
                for j in range(4):
                    pe_wide_half(pe, ph, 0, j, 0, norm if j == 0 else None)

            pe.wait_ge(const_in, 48)
            pe_norm(pe, 0)
            ffn(fi1, fo1, 0)
            pe_norm(pe, 1)
            for ph in (p_qr, p_kr):
                pe_enter(pe, ph)
                for qq in range(ph.quads):
                    for j in range(4):
                        pe_wide_half(pe, ph, qq, j, 0, (normed_split, KD) if ph is p_qr and qq == 0 and j == 0 else None)
            for t in range(16):
                pe_wide_half(pe, p_vr, t // 4, t % 4)
                if t:
                    pe_v_tile(pe, p_vr, t - 1)
            pe_v_tile(pe, p_vr, 15)
            pe_enter(pe, p_gr)
            pe.wait_ge(rr_done, 2 * RH)
            pe.wait_ge(rr_pool, 6 * RH)
            pe.wait_ge(vr_out, 16)
            pe.wait_ge(vrs_out, 16)
            pe_ret_a(pe, 0)
            for h in range(RH):
                pe_wide_half(pe, p_gr, h, 0)
                pe_ret_o(pe, h)
                pe_wide_half(pe, p_gr, h, 1)
                pe_ret_state(pe, h)
                pe_wide_half(pe, p_gr, h, 2)
                pe_ret_sum(pe, h)
                pe_wide_half(pe, p_gr, h, 3)
                if h + 1 < RH:
                    pe_ret_a(pe, h + 1)
            pe_enter(pe, p_qk)
            pe.wait_ge(orms_done, RH)
            pe.wait_ge(adec_done, 2 * RH)
            pe.wait_ge(snew_out, 2 * RH)

            def qk_quad(qq, b, it=0):
                t = 4 * qq
                for j in range(4):
                    pe_wide_half(pe, p_qk, qq, j, it)
                    if j:
                        pe_state_o(pe, b, j - 1, it)
                    pe_state_v(pe, b, j, it)
                    if j:
                        pe_qk_ms(pe, t + j - 1, it)
                    if j >= 2:
                        pe_qk_rot(pe, t + j - 2, it)
                pe_qk_ms(pe, t + 3, it)
                pe_qk_rot(pe, t + 2, it)
                pe_state_o(pe, b, 3, it)
                pe_qk_rot(pe, t + 3, it)

            qk_quad(0, 0)
            with pe.Fori(0, p_qk.quads - 1) as it:
                qk_quad(1, 1, it)
            pe_enter(pe, p_v)
            pe.wait_ge(qk_rms_done, 2 * AT)
            pe.wait_ge(qk_sin, 2 * AT)
            for t in range(AT):
                pe_wide_half(pe, p_v, t // 4, t % 4)
                if t < 8:
                    pe_state_v(pe, 6 + t // 4, t % 4)
                if t:
                    pe_v_tile(pe, p_v, t - 1)
                if 1 <= t <= 8:
                    pe_state_o(pe, 6 + (t - 1) // 4, (t - 1) % 4)
            pe_v_tile(pe, p_v, AT - 1)
            pe.wait_ge(qk_done, 2 * AT)
            pe.wait_ge(os_out, B * RH)
            for n in range(6):
                if n >= 2:
                    pe.wait_ge(qks_out, n - 1)
                for i in range(4):
                    last = nc.tensor.transpose(aux67[0:B, n % 2, i * P:(i + 1) * P], qk[:, 4 * n + i, S:T], ident)
                last.then_inc(qks_psum, 1)
            pe.wait_ge(small_step, 1)
            pe.wait_ge(v_out_sem, AT)
            pe.wait_ge(vs_out, AT)
            nc.tensor.matmul(bank4[:, 0:RH * B], ones, os_sum[:].rearrange("p h b -> p (h b)"), start=True,
                             stop=True).then_inc(small_pe, 1)
            for t in range(KD):
                pe_wide_half(pe, p_gb, t // 4, t % 4)
                if t == 0:
                    pe.wait_ge(small_act, 2)
                for i in range(3 * t, 3 * t + 3):
                    pe_dec_q(pe, i)
            pe.wait_ge(qks_out, 6)
            pe_enter(pe, p_pb)
            pe.wait_ge(ob_split, RH)

            def pb_half(i, midway=None):
                m = i // 2
                pe_wait_half(pe, p_pb.q0 + i // 4, i % 4)
                if i % 2 == 0:
                    pe_wait_acc(pe, p_pb, m, 4)
                for t in range(8):
                    if t == 5 and midway:
                        midway()
                    k = 8 * (i % 2) + t
                    last = three_passes(acc[m % 4][:, 0:T], i % 4, t, obh[:, k], obl[:, k], k == 0, k == 15)
                last.then_inc(pe_half, 1)

            pb_half(0)
            pe_dec_scores(pe)
            pb_half(1)
            pb_half(2)
            pe_dec_turn(pe)
            pb_half(3)
            pe_dec_own(pe)
            for i in range(4, 8):
                for v in range(6 * (i - 4), 6 * (i - 4) + 6):
                    pe_dec_v(pe, v)
                pb_half(i)
            pe.wait_ge(dec_dve, DEC_DVE)

            def att(i):
                if i >= 1:
                    pe_turn(pe, i - 1)
                if i < 16:
                    pe_scores(pe, i)

            for i in range(8):
                att(i)
                pb_half(8 + i, (lambda n=i - 1: pe_pv(pe, n)) if i else None)
            pe_enter(pe, p_ga)
            for t in range(KD):
                att(8 + t)
                pe_wide_half(pe, p_ga, t // 4, t % 4, midway=lambda n=7 + t: pe_pv(pe, n))
            att(16)
            pe_pv(pe, 15)
            pe_enter(pe, p_pa)
            pe.wait_ge(oa_split, 1)
            for j in range(4):
                pe_wait_half(pe, p_pa.q0, j)
                for m in (2 * j, 2 * j + 1):
                    pe_wait_acc(pe, p_pa, m, 4)
                    for k in range(4):
                        last = three_passes(acc[m % 4][:, 0:T], j, 4 * (m % 2) + k, oah[:, k], oal[:, k],
                                            k == 0, k == 3)
                last.then_inc(pe_half, 1)
            for m in range(KD):
                pe_wide_half(pe, p_wo, m // 4, m % 4, 0, (merge_split, 0) if m == 0 else None)
            pe_norm(pe, 2)
            ffn(fi2, fo2, 2)


def tiles_of(w, order):
    return [w[k * P:(k + 1) * P, cols] for k, cols in order]


def unit_array(w, orders):
    return np.stack([np.concatenate(tiles_of(w, order), axis=1) for order in orders])


def weight_units(i):
    def cols(a, step=1):
        return slice(a, a + P * step, step)

    def wide(w, starts, kt=KD):
        return unit_array(w, [[(k, c) for c in starts[n:n + 2] for k in range(kt)] for n in range(0, len(starts), 2)])

    def ffn_in(w):
        return wide(w, [cols(o + t * P) for t in range(FT) for o in (0, DFF)])

    def ffn_out(w):
        return unit_array(w, [[(k, cols(m * P)) for k in range(h * 11, h * 11 + 11)] for m in range(KD) for h in range(2)])

    w = i["w_in"][0]
    at = np.cumsum([0, G * AW, G * AW, G * AW, RH * RQ, RH * RQ, RH * RV, RH * RV, D, D])
    qa, ka, va, qr, kr, vr, gr, ga, gb = (int(a) for a in at[:9])

    def run(start, n):
        return [cols(start + t * P) for t in range(n)]

    def halves(start):
        return [cols(start + h * RQ + p, 2) for h in range(RH) for p in range(2)]

    pb = unit_array(i["w_pb"][0], [[(k, cols(m * P)) for k in range(16)] for m in range(KD)])
    pa = unit_array(i["w_pa"][0], [[(k, cols(m * P)) for m in range(n, n + 4) for k in range(4)] for n in (0, 4)])
    w16 = np.concatenate([
        ffn_in(i["ffn1_in"][0]), wide(w, halves(qr)), wide(w, halves(kr)), wide(w, run(vr, 16)), wide(w, run(gr, 16)),
        wide(w, run(qa, AT) + run(ka, AT)), wide(w, run(va, AT)), wide(w, run(gb, KD)), pb, wide(w, run(ga, KD)), pa,
        wide(i["w_o"][0], run(0, KD)), ffn_in(i["ffn2_in"][0])])
    w11 = np.concatenate([ffn_out(i["ffn1_out"][0]), ffn_out(i["ffn2_out"][0])])
    return w16, w11


def kernel(**inputs):
    import concourse.bacc as bacc
    from concourse.bass_utils import run_bass_kernel_spmd

    i = {k: np.asarray(v) for k, v in inputs.items()}
    tokens = np.concatenate([i["x_prompt"][0], i["x_sample"][:, 0]])
    xT = np.ascontiguousarray(tokens.T.reshape(KD, P, T).transpose(1, 0, 2))
    norms = [i[n][0].reshape(KD, P).T for n in ("ffn1_norm", "mix_norm", "ffn2_norm")]
    heads = [np.tile(i[n][0], 2)[:, None] for n in ("a_q_norm", "a_k_norm")]
    w16, w11 = weight_units(i)
    caches = [i[f"cache_kv_a{g}"][0].reshape(B, -1, 2 * AW) for g in range(G)]
    arrays = {"xT": xT, "tables": build_tables(), "gains": np.ascontiguousarray(np.concatenate(norms + heads, axis=1)),
              "w16": w16, "w11": w11, "cache0": caches[0], "cache1": caches[1], "cache2": caches[2],
              "state_in": i["state_ret"][0]}
    outs = {"yT": (P, KD, T), "kT_out": (P, AT, T), "v_out": (S, G * AW), "ret_out": (RH, RQ, RV),
            "kv0_out": caches[0].shape, "kv1_out": caches[1].shape, "kv2_out": caches[2].shape,
            "state_out": (B, RH, RQ, RV)}
    nc = bacc.Bacc("TRN2", target_bir_lowering=False, num_devices=1)
    args = [nc.dram_tensor(n, a.shape, mybir.dt.from_np(a.dtype), kind="ExternalInput").ap() for n, a in arrays.items()]
    args += [nc.dram_tensor(n, s, F32, kind="ExternalOutput").ap() for n, s in outs.items()]
    trunk_step(nc, *args)
    r = run_bass_kernel_spmd(nc, [arrays], core_ids=[0]).results[0]

    y = r["yT"].transpose(2, 1, 0).reshape(T, D)
    k = r["kT_out"].transpose(2, 1, 0).reshape(T, G, AH, AE)[:S]
    v = r["v_out"].reshape(S, G, AH, AE)
    prompt = []
    for g, (window, _) in enumerate(GROUPS):
        keep = min(window, S)
        prompt.append(np.stack([k[S - keep:, g], v[S - keep:, g]], axis=1)[None, None])
    sample = [r[f"kv{g}_out"].reshape(i[f"cache_kv_a{g}"].shape) for g in range(G)]
    return (y[None, :S], y[S:, None], *prompt, r["ret_out"][None, None], *sample, r["state_out"][None])
```

```python
from contextlib import ExitStack

import numpy as np

import concourse.bass as bass
from concourse import mybir

F32 = mybir.dt.float32
F32R = mybir.dt.float32r
ALU = mybir.AluOpType
ACT = mybir.ActivationFunctionType
AX = mybir.AxisListType

P = 128
D = 1024
KD = D // P
S = 256
B = 8
T = S + B
PAST = 2048
DFF = ((8 * D // 3 + P - 1) // P) * P
FT = DFF // P
GROUPS = ((128, 1), (512, 4), (2048, 16))
G = len(GROUPS)
AH, AE = 8, 64
AW = AH * AE
AT = G * AW // P
RH, RQ, RV = 4, 256, 512
EPS = 1e-6
NEG = -1e30
SCALE = AE ** -0.5
PICK = 32 + B

PHASES = [
    ("fi", 11, 4, "dve"), ("fo", 8, 1, "dve"), ("qr", 2, 4, "act"), ("kr", 2, 4, "act"), ("vr", 4, 4, "act"),
    ("gr", 4, 4, "dve"), ("qk", 6, 4, "act"), ("v", 3, 4, "act"), ("gb", 2, 4, "act"), ("pb", 4, 2, "dve"),
    ("ga", 2, 4, "act"), ("pa", 1, 8, "dve"), ("wo", 2, 4, "dve"), ("fi", 11, 4, "dve"), ("fo", 8, 1, "dve"),
]
FO_HALVES = (6, 5, 6, 5)


def moving(it):
    return not isinstance(it, int)


class Phase:

    def __init__(self, index):
        self.kind, self.quads, self.per_quad, self.owner = PHASES[index]
        self.q0 = sum(p[1] for p in PHASES[:index])
        self.out0 = sum(p[1] * p[2] for p in PHASES[:index] if p[3] == self.owner)
        self.previous = PHASES[index - 1][3] if index else self.owner
        self.previous_out = sum(p[1] * p[2] for p in PHASES[:index] if p[3] == self.previous)


QUADS = sum(p[1] for p in PHASES)
KIND_OF = [p[0] for p in PHASES for _ in range(p[1])]


def half_tiles(q, j):
    return FO_HALVES[j] if KIND_OF[q] == "fo" else 8


def half_offset(q, j):
    return (0 if j % 2 == 0 else half_tiles(q, j - 1)) * P


TABLES = {}
_at = 0
for _name, _n in (("cos_a", T), ("sin_a", T), ("cos_r", T), ("sin_r", T), ("mask", G * 2 * P), ("decay", RH * 2 * P),
                  ("ident", P), ("ones", P), ("blocks", P), ("turn", P), ("spread", P), ("kdec", RH * 2), ("gamma", RH),
                  ("rsel", B), ("pick", B), ("eps", 1)):
    TABLES[_name] = (_at, _at + _n)
    _at += _n
NTAB = _at
NGAIN = 3 * KD + 2


def build_tables():
    tab = np.zeros((P, NTAB), np.float32)

    def put(name, value):
        a, b = TABLES[name]
        value = np.asarray(value, np.float32)
        tab[:value.shape[0], a:b] = value.reshape(value.shape[0], b - a)

    pos = np.concatenate([np.arange(S), np.full(B, PAST)]).astype(np.float32)
    half = AE // 8
    inv = (np.float32(500000.0) ** (-np.arange(half, dtype=np.float32) / np.float32(half))).astype(np.float32)
    ang = (pos[None, :] * inv[:, None]).astype(np.float32).astype(np.float64)
    cos_a, sin_a = np.ones((P, T)), np.zeros((P, T))
    turn = np.zeros((P, P))
    for base in (0, AE):
        for r in range(2):
            cos_a[base + r * half:base + (r + 1) * half] = np.cos(ang)
            sin_a[base + r * half:base + (r + 1) * half] = np.sin(ang)
        for i in range(half):
            turn[base + half + i, base + i] = -1.0
            turn[base + i, base + half + i] = 1.0
    put("cos_a", cos_a)
    put("sin_a", sin_a)
    put("turn", turn)
    put("spread", np.arange(P)[:, None] % 32 == 16 * (np.arange(P)[None, :] // AE))
    inv_r = (np.float32(1.0) / np.float32(10000.0) ** np.linspace(0.0, 1.0, P, dtype=np.float32)).astype(np.float32)
    ang_r = (pos[None, :] * inv_r[:, None]).astype(np.float32).astype(np.float64)
    put("cos_r", np.cos(ang_r))
    put("sin_r", np.sin(ang_r))
    mask = np.zeros((P, G, 2, P))
    qi, kj = np.arange(P)[:, None], np.arange(P)[None, :]
    for g, (_, dil) in enumerate(GROUPS):
        for block, dist in ((0, P + qi - kj), (1, qi - kj)):
            ok = (dist >= 0) & (dist % dil == 0) & (dist // dil <= P)
            mask[:, g, block] = np.where(ok, 0.0, NEG)
    put("mask", mask)
    gamma = 1.0 - 2.0 ** (-5.0 - np.arange(RH))
    decay = np.zeros((P, RH, 2, P))
    j, i = np.arange(P)[:, None], np.arange(P)[None, :]
    for h in range(RH):
        decay[:, h, 0] = np.where(i >= j, gamma[h] ** np.maximum(i - j, 0), 0.0)
        decay[:, h, 1] = gamma[h] ** (P + i - j)
    put("decay", decay)
    put("ident", np.eye(P))
    put("ones", np.ones((P, P)))
    put("blocks", np.kron(np.eye(2), np.ones((AE, AE))))
    kdec = np.zeros((P, RH, 2))
    for h in range(RH):
        for c in range(2):
            kdec[:, h, c] = gamma[h] ** (S - 1 - c * P - np.arange(P))
    put("kdec", kdec)
    put("gamma", np.broadcast_to(gamma, (P, RH)))
    put("rsel", (np.arange(64)[:, None] % B == np.arange(B)[None, :]))
    put("pick", (np.arange(PICK)[:, None] % 32 == np.arange(B)[None, :]))
    put("eps", np.full((P, 1), EPS))
    return tab


def trunk_step(nc, xT, tables, gains, w16, w11, cache0, cache1, cache2, state_in,
               yT, kT_out, v_out, ret_out, kv0_out, kv1_out, kv2_out, state_out):
    caches, kv_outs = (cache0, cache1, cache2), (kv0_out, kv1_out, kv2_out)

    with ExitStack() as ctx:
        base = 16512
        place = {"at": base}

        def fixed(name, shape, dtype=F32):
            t = nc.alloc_sbuf_tensor_at(name, [P] + shape, dtype, offset=place["at"])
            place["at"] += (int(np.prod(shape)) * 4 + 31) // 32 * 32
            return t

        x = fixed("x", [KD, T])
        hh = fixed("hh", [KD, T], F32R)
        hl = fixed("hl", [KD, T], F32R)
        raw = [fixed(f"raw{i}", [16 * P]) for i in range(2)]
        wh = [fixed(f"wh{i}", [8 * P], F32R) for i in range(4)]
        wl = [fixed(f"wl{i}", [8 * P], F32R) for i in range(4)]
        tab = fixed("tab", [NTAB])
        gain = fixed("gain", [NGAIN])
        square = fixed("square", [2, T])
        square_sum = fixed("square_sum", [T])
        rms = fixed("rms", [T])
        normed = square
        qr_s = fixed("qr_s", [2 * RH, B])
        kr_s = fixed("kr_s", [2 * RH, B])
        o_s = fixed("o_s", [RH * 4, B])
        o_s2 = fixed("o_s2", [RH * 4, B])
        os_sum = fixed("os_sum", [RH, B])
        pick = fixed("pick", [B], F32R)
        picked = fixed("picked", [1], F32R)
        arena = place["at"]

        def at(name, offset, shape, dtype=F32):
            return nc.alloc_sbuf_tensor_at(name, [P] + shape, dtype, offset=arena + offset)

        uh = at("uh", 0, [FT, T], F32R)
        ul = at("ul", 23232, [FT, T], F32R)
        silu = at("silu", 46464, [2, T])
        product = at("product", 48576, [2, T])
        v_ret = at("v_ret", 0, [2, RH * RV])
        vs_ret = at("vs_ret", 16384, [RH * RV])
        ob = at("ob", 24576, [RH * 4, T])
        qr = at("qr", 41472, [2 * RH, T])
        kr = at("kr", 49920, [2 * RH, T])
        pair = at("pair", 58368, [2, 2, T])
        turned = at("turned", 62592, [4, T])
        vT_ret = at("vT_ret", 66816, [2, T])
        sig = at("sig", 68928, [2, T])
        a_dec = at("a_dec", 71040, [3 * P])
        k_dec = at("k_dec", 72576, [2, RQ])
        o_ret = at("o_ret", 74624, [4, S])
        o_sq = at("o_sq", 78720, [4, S])
        o_sum = at("o_sum", 82816, [S])
        o_rms = at("o_rms", 83840, [S])
        s_new = at("s_new", 112256, [2, RV])
        state = at("state", 0, [4, 2 * RV])
        qk = at("qk", 41472, [2 * AT, T])
        v_tok = at("v_tok", 66816, [2, G * AW])
        vk_s = at("vk_s", 79104, [G * AW])
        v_s, k_s = vk_s[0:B, :], vk_s[32:32 + B, :]
        q_hl = at("q_hl", 85248, [G * AW], F32R)
        qk_sq = at("qk_sq", 91392, [2, T])
        qk_rms = at("qk_rms", 93504, [T])
        qk_rinv = at("qk_rinv", 94560, [T])
        rot_s = at("rot_s", 95616, [2, T])
        rot_c = at("rot_c", 97728, [2, T])
        vr_hl = at("vr_hl", 99840, [RH * RV], F32R)
        vT = at("vT", 108032, [4, T])
        obh = at("obh", 0, [RH * 4, T], F32R)
        dec_s = at("dec_s", 16896, [G, 64])
        dec_p = at("dec_p", 17664, [G * P + G])
        dec_pT = at("dec_pT", 19232, [G, 64])
        dec_own = at("dec_own", 20000, [G, 64])
        dec_diag = at("dec_diag", 20768, [G, 64])
        qk_own = at("qk_own", 21536, [AT, B])
        dec_m = at("dec_m", 21920, [4])
        att_m = at("att_m", 21952, [4])
        gate_b = at("gate_b", 24576, [KD, T])
        gate_a = at("gate_a", 33024, [KD, T])
        oa = at("oa", 85248, [4, T])
        kv = at("kv", 91392, [3, AW])
        prob = at("prob", 91392, [G, 2 * P])
        probT = at("probT", 94464, [6 * P])
        obl = at("obl", 99584, [RH * 4, T], F32R)
        oah = at("oah", 41472, [4, T], F32R)
        oal = at("oal", 45696, [4, T], F32R)
        merge_a = at("merge_a", 91392, [2, T])
        merge = at("merge", 93504, [2, T])

        def const(name, rows=P):
            a, b = TABLES[name]
            return tab[0:rows, a:b]

        ident, ones, blocks, turn = const("ident"), const("ones"), const("blocks"), const("turn")
        eps = const("eps")

        acc = [ctx.enter_context(nc.psum_tensor(f"acc{i}", [P, 512], F32)) for i in range(4)]
        aux45 = ctx.enter_context(nc.psum_tensor("aux45", [P, 2, 512], F32))
        aux67 = ctx.enter_context(nc.psum_tensor("aux67", [P, 2, 512], F32))
        bank4, bank5, bank6, bank7 = aux45[:, 0], aux45[:, 1], aux67[:, 0], aux67[:, 1]

        def sem(name):
            return ctx.enter_context(nc.semaphore(name))

        const_in = sem("const_in")
        raw_in = [sem("raw_in0"), sem("raw_in1")]
        hi_done, lo_done = sem("hi_done"), sem("lo_done")
        pe_half = sem("pe_half")
        out_of = {"act": sem("acc_out_act"), "dve": sem("acc_out_dve")}
        silu_done, u_split = sem("silu_done"), sem("u_split")
        sq_done, sum_done, sum_psum = sem("sq_done"), sem("sum_done"), sem("sum_psum")
        rms_done, rinv_done = sem("rms_done"), sem("rinv_done")
        normed_done, normed_hi, normed_split = sem("normed_done"), sem("normed_hi"), sem("normed_split")
        rr_dve, rr_pool, rr_done = sem("rr_dve"), sem("rr_pool"), sem("rr_done")
        rs_copied = sem("rs_copied")
        vr_turned, vr_out, vrs_out = sem("vr_turned"), sem("vr_out"), sem("vrs_out")
        sig_done = sem("sig_done")
        kt_psum, kdec_done = sem("kt_psum"), sem("kdec_done")
        a_psum, adec_done = sem("a_psum"), sem("adec_done")
        o_psum, o_out, osq_done, osum_done = sem("o_psum"), sem("o_out"), sem("osq_done"), sem("osum_done")
        oms_psum, orms_done, orinv_done, on_done, ob_done = (
            sem("oms_psum"), sem("orms_done"), sem("orinv_done"), sem("on_done"), sem("ob_done"))
        snew_psum, snew_out, ret_stored = sem("snew_psum"), sem("snew_out"), sem("ret_stored")
        cleared, pick_done, picked_done = sem("cleared"), sem("pick_done"), sem("picked_done")
        qk_sq_done, qk_ms_psum, qk_rms_done, qk_rinv_done = (
            sem("qk_sq_done"), sem("qk_ms_psum"), sem("qk_rms_done"), sem("qk_rinv_done"))
        qk_rot_psum, qk_sin, qk_cos, qk_turned, qk_spread, qk_done = (
            sem("qk_rot_psum"), sem("qk_sin"), sem("qk_cos"), sem("qk_turned"), sem("qk_spread"), sem("qk_done"))
        state_in_sem = [sem(f"state_in{i}") for i in range(4)]
        state_stored = [sem(f"state_stored{i}") for i in range(4)]
        vr_hi, vr_lo, vb_psum, state_scaled, state_new = (
            sem("vr_hi"), sem("vr_lo"), sem("vb_psum"), sem("state_scaled"), sem("state_new"))
        os_psum, os_out = sem("os_psum"), sem("os_out")
        v_turned, v_out_sem, vs_out = sem("v_turned"), sem("v_tok_out"), sem("v_s_out")
        qks_psum, qks_out, qs_lo = sem("qks_psum"), sem("qks_out"), sem("qs_lo")
        small_step = sem("small_step")
        small_act = sem("small_act")
        small_pe = sem("small_pe")
        ob_hi, ob_split = sem("ob_hi"), sem("ob_split")
        kv_in = [sem(f"kv_in{i}") for i in range(3)]
        qb_psum, kq_done = sem("qb_psum"), sem("kq_done")
        dec_pe, dec_dve, dec_act, dec_v_done = sem("dec_pe"), sem("dec_dve"), sem("dec_act"), sem("dec_v_done")
        att_scores, att_masked, att_negmax = sem("att_scores"), sem("att_masked"), sem("att_negmax")
        att_exp, att_rinv, att_prob = sem("att_exp"), sem("att_rinv"), sem("att_prob")
        att_turned, att_turned_out = sem("att_turned"), sem("att_turned_out")
        att_pv, att_out = sem("att_pv"), sem("att_out")
        oa_hi, oa_split = sem("oa_hi"), sem("oa_split")
        merge_a_done, merge_done, merge_hi, merge_split = (
            sem("merge_a_done"), sem("merge_done"), sem("merge_hi"), sem("merge_split"))
        rolled = sem("rolled")
        stored = sem("stored")
        STORES = 1 + 1 + KD + 2 * G

        phases = [Phase(i) for i in range(len(PHASES))]
        unit16 = {}
        for q in range(QUADS):
            for s in range(2):
                n = 2 * q + s
                kind = "11" if KIND_OF[q] == "fo" else "16"
                unit16[n] = (kind, sum(1 for v in unit16.values() if v[0] == kind))

        def load_unit(act, n, it=0):
            kind, index = unit16[n]
            src, cols = (w16, 16 * P) if kind == "16" else (w11, 11 * P)
            act.dma_start(raw[n % 2][:, 0:cols], src[index + 2 * it]).then_inc(raw_in[n % 2], 16)

        def hi_half(act, q, j, it=0):
            n = half_tiles(q, j) * P
            off = half_offset(q, j)
            act.wait_ge(raw_in[j // 2], 16 * (q + 1) + 16 * it)
            if q >= 1:
                act.wait_ge(pe_half, 4 * (q - 1) + j + 1 + 4 * it)
            nc.scalar.activation(wh[j][:, 0:n], raw[j // 2][:, off:off + n], ACT.Copy).then_inc(hi_done, 1)

        def lo_half(dve, q, j, it=0):
            n = half_tiles(q, j) * P
            off = half_offset(q, j)
            dve.wait_ge(hi_done, 4 * q + j + 1 + 4 * it)
            nc.vector.tensor_tensor(wl[j][:, 0:n], raw[j // 2][:, off:off + n], wh[j][:, 0:n].bitcast(F32),
                                    ALU.subtract).then_inc(lo_done, 1)

        def act_ahead(act, q, j, it=0):
            if q + 1 < QUADS:
                hi_half(act, q + 1, j, it)
            if j == 0 and q + 1 < QUADS:
                act.wait_ge(lo_done, 4 * q + 4 + 4 * it)
                load_unit(act, 2 * (q + 1) + 1, it)
            if j == 2 and q + 2 < QUADS:
                act.wait_ge(lo_done, 4 * (q + 1) + 2 + 4 * it)
                load_unit(act, 2 * (q + 2), it)

        def dve_ahead(dve, q, j, it=0):
            if q + 1 < QUADS:
                lo_half(dve, q + 1, j, it)

        def three_passes(out, j, t, xh, xl, first, last, skip=False):
            w_hi, w_lo = wh[j][:, t * P:(t + 1) * P], wl[j][:, t * P:(t + 1) * P]
            nc.tensor.matmul(out, w_hi, xh, start=first, stop=False)
            nc.tensor.matmul(out, w_hi, xl, start=False, stop=False)
            return nc.tensor.matmul(out, w_lo, xh, start=False, stop=last)

        def pe_wait_half(pe, q, j, it=0):
            pe.wait_ge(lo_done, 4 * q + j + 1 + 4 * it)

        def pe_wait_acc(pe, ph, local, keep, it=0):
            value = ph.out0 + local - keep + 1
            if value > 0:
                pe.wait_ge(out_of[ph.owner], value + ph.per_quad * it)

        def pe_enter(pe, ph):
            if ph.previous != ph.owner and ph.q0:
                pe.wait_ge(out_of[ph.previous], ph.previous_out)

        def pe_wide_half(pe, ph, qq, j, it=0, wait_x=None, midway=None):
            pe_wait_half(pe, ph.q0 + qq, j, it)
            pe_wait_acc(pe, ph, 4 * qq + j, 4, it)
            for k in range(KD):
                if wait_x is not None:
                    pe.wait_ge(wait_x[0], wait_x[1] + k + 1)
                if k == 5 and midway:
                    midway()
                last = three_passes(acc[j][:, 0:T], j, k, hh[:, k], hl[:, k], k == 0, k == KD - 1)
            last.then_inc(pe_half, 1)

        def pe_fo_quad(pe, ph, m, bank, it=0):
            r = 0 if ph.q0 < QUADS // 2 else 1
            pe_wait_acc(pe, ph, m, 2, it)
            k = 0
            for j in range(4):
                pe_wait_half(pe, ph.q0 + m, j, it)
                pe.wait_ge(u_split, FT * r + k + FO_HALVES[j])
                for t in range(FO_HALVES[j]):
                    last = three_passes(acc[bank][:, 0:T], j, t, uh[:, k], ul[:, k], k == 0, k == FT - 1)
                    k += 1
                last.then_inc(pe_half, 1)

        def dve_sum_square(dve, r, m, it=0):
            dve.wait_ge(sq_done, KD * r + m + 1 + it)
            if not isinstance(m, int) or m or moving(it):
                dve.wait_ge(sum_done, KD * r + m + it)
            ins = (nc.vector.tensor_copy(square_sum[:], square[:, m % 2]) if m == 0 and not moving(it) else
                   nc.vector.tensor_tensor(square_sum[:], square_sum[:], square[:, m % 2], ALU.add))
            ins.then_inc(sum_done, 1)

        def act_square(act, r, m, it=0):
            if r or m >= 2:
                act.wait_ge(sum_done, KD * r + m - 1 + it)
            nc.scalar.activation(square[:, m % 2], x[:, bass.ds(m + it, 1)].squeeze(1) if moving(it) else x[:, m],
                                 ACT.Square).then_inc(sq_done, 1)

        def pe_norm(pe, r):
            pe.wait_ge(sum_done, KD * (r + 1))
            nc.tensor.matmul(bank4[:, 0:T], ones, square_sum[:], start=True, stop=True).then_inc(sum_psum, 1)

        def act_norm(act, r):
            act.wait_ge(sum_psum, r + 1)
            nc.scalar.activation(rms[:], bank4[:, 0:T], ACT.Sqrt, bias=eps, scale=1.0 / D).then_inc(rms_done, 1)
            for k in range(KD):
                act.wait_ge(normed_done, KD * r + k + 1)
                nc.scalar.activation(hh[:, k], normed[:, k % 2], ACT.Copy).then_inc(normed_hi, 1)

        def dve_norm(dve, r):
            dve.wait_ge(rms_done, r + 1)
            nc.vector.reciprocal(rms[:], rms[:]).then_inc(rinv_done, 1)
            dve.wait_ge(rinv_done, r + 1)
            for k in range(KD):
                if KD * r + k >= 2:
                    dve.wait_ge(normed_split, KD * r + k - 1)
                nc.vector.scalar_tensor_tensor(normed[:, k % 2], x[:, k], gain[:, r * KD + k:r * KD + k + 1],
                                               rms[:], ALU.mult, ALU.mult).then_inc(normed_done, 1)

        def pool_norm(pool, r):
            for k in range(KD):
                pool.wait_ge(normed_hi, KD * r + k + 1)
                nc.gpsimd.tensor_tensor(hl[:, k], normed[:, k % 2], hh[:, k].bitcast(F32),
                                        ALU.subtract).then_inc(normed_split, 1)

        def act_fi_quad(act, ph, qq, it=0):
            q = ph.q0 + qq
            r = 0 if ph.q0 < QUADS // 2 else 1
            for j in range(4):
                act_ahead(act, q, j, it)
                if j % 2 == 0:
                    i = FT * r + 2 * qq + j // 2
                    act.wait_ge(pe_half, 4 * q + j + 1 + 4 * it)
                    if i >= 2:
                        act.wait_ge(out_of["dve"], ph.out0 + 2 * (2 * qq + j // 2) - 2 + 4 * it)
                    nc.scalar.activation(silu[:, j // 2], acc[j][:, 0:T], ACT.Silu).then_inc(silu_done, 1)

        def dve_fi_quad(dve, ph, qq, it=0):
            q = ph.q0 + qq
            r = 0 if ph.q0 < QUADS // 2 else 1
            for j in range(4):
                dve_ahead(dve, q, j, it)
                if j % 2 == 1:
                    i = FT * r + 2 * qq + j // 2
                    dve.wait_ge(pe_half, 4 * q + j + 1 + 4 * it)
                    dve.wait_ge(silu_done, i + 1 + 2 * it)
                    if i >= 2:
                        dve.wait_ge(u_split, i - 1 + 2 * it)
                    nc.vector.tensor_tensor(product[:, j // 2], silu[:, j // 2], acc[j][:, 0:T],
                                            ALU.mult).then_inc(out_of["dve"], 2)

        def pool_fi_quad(pool, ph, qq, it=0):
            r = 0 if ph.q0 < QUADS // 2 else 1
            for s in range(2):
                i = 2 * qq + s
                pool.wait_ge(out_of["dve"], ph.out0 + 2 * i + 2 + 4 * it)
                if not moving(it):
                    hi, lo = uh[:, i], ul[:, i]
                else:
                    hi, lo = (u[:, bass.ds(i + 2 * it, 1)].squeeze(1) for u in (uh, ul))
                nc.gpsimd.tensor_copy(hi, product[:, s]).then_inc(u_hi, 1)
                pool.wait_ge(u_hi, FT * r + i + 1 + 2 * it)
                nc.gpsimd.tensor_tensor(lo, product[:, s], hi.bitcast(F32), ALU.subtract).then_inc(u_split, 1)

        u_hi = sem("u_hi")

        def act_fo_quad(act, ph, m, it=0, norm=None):
            for j in range(4):
                act_ahead(act, ph.q0 + m, j, it)
            if norm is not None:
                act.wait_ge(out_of["dve"], ph.out0 + m + 1 + it)
                act_square(act, norm, m, it)

        def dve_add_x(dve, ph, m, factor, bank, it=0):
            xm = x[:, m] if not moving(it) else x[:, bass.ds(m + it, 1)].squeeze(1)
            nc.vector.scalar_tensor_tensor(xm, acc[bank][:, 0:T], factor, xm, ALU.mult,
                                           ALU.add).then_inc(out_of["dve"], 1)

        def dve_fo_quad(dve, ph, m, it=0, norm=None):
            for j in range(4):
                dve_ahead(dve, ph.q0 + m, j, it)
            dve.wait_ge(pe_half, 4 * (ph.q0 + m) + 4 + 4 * it)
            dve_add_x(dve, ph, m, 0.5, m % 2, it)
            if norm is not None:
                dve_sum_square(dve, norm, m, it)

        RR = [("qr", qr), ("kr", kr)]

        def act_rr_quad(act, ph, qq, which):
            for j in range(4):
                act_ahead(act, ph.q0 + qq, j)
                head = 2 * qq + j // 2
                act.wait_ge(pe_half, 4 * (ph.q0 + qq) + j + 1)
                n = RH * which + head
                if n >= 2:
                    act.wait_ge(rr_done, n - 1)
                    act.wait_ge(rr_pool, 3 * n - 3)
                nc.scalar.activation(pair[:, head % 2, j % 2], acc[j][:, 0:T], ACT.Copy,
                                     scale=1.0 if which == 0 else RQ ** -0.5).then_inc(out_of["act"], 1)

        def turn_head(eng, ops, ph, head, which):
            n = RH * which + head
            dst = RR[which][1]
            eng.wait_ge(out_of["act"], ph.out0 + 2 * head + 2)
            cos, sin = const("cos_r"), const("sin_r")
            if ops is nc.vector:
                step, p, q_, out, t0, op = rr_dve, 0, 1, 2 * head, 0, ALU.subtract
            else:
                step, p, q_, out, t0, op = rr_pool, 1, 0, 2 * head + 1, 2, ALU.add
            if n:
                if ops is nc.vector:
                    eng.wait_ge(rr_done, n)
                else:
                    eng.wait_ge(rr_pool, 3 * n)
            ops.tensor_tensor(turned[:, t0], pair[:, head % 2, p], cos, ALU.mult).then_inc(step, 1)
            ops.tensor_tensor(turned[:, t0 + 1], pair[:, head % 2, q_], sin, ALU.mult).then_inc(step, 1)
            if ops is nc.vector:
                eng.wait_ge(rr_dve, 2 * n + 2)
                ops.tensor_tensor(dst[:, out], turned[:, t0], turned[:, t0 + 1], op).then_inc(rr_done, 1)
            else:
                eng.wait_ge(rr_pool, 3 * n + 2)
                ops.tensor_tensor(dst[:, out], turned[:, t0], turned[:, t0 + 1], op).then_inc(rr_pool, 1)

        VKIND = {"vr": (vT_ret, 2, v_ret, vs_ret, vr_turned, vr_out, vrs_out),
                 "v": (vT, 4, v_tok, v_s, v_turned, v_out_sem, vs_out)}

        def act_v_tile(act, ph, t):
            src, ring, _, _, turned_sem, _, _ = VKIND[ph.kind]
            act.wait_ge(pe_half, 4 * ph.q0 + t + 1)
            if t >= ring:
                act.wait_ge(turned_sem, t - ring + 1)
            nc.scalar.activation(src[:, t % ring], acc[t % 4][:, 0:T], ACT.Copy).then_inc(out_of["act"], 1)

        def act_v_small(act, ph, t):
            _, _, _, small, _, big_out, small_out = VKIND[ph.kind]
            act.wait_ge(big_out, t + 1)
            nc.scalar.activation(small[0:B, t * P:(t + 1) * P], aux45[0:B, t % 2, 256:256 + P],
                                 ACT.Copy).then_inc(small_out, 1)

        def dve_v_tile(dve, ph, t):
            _, _, big, _, turned_sem, big_out, _ = VKIND[ph.kind]
            dve.wait_ge(turned_sem, t + 1)
            nc.vector.tensor_copy(big[:, :, t * P:(t + 1) * P],
                                  aux45[:, t % 2, 0:256].rearrange("p (c f) -> p c f", c=2)).then_inc(big_out, 1)

        def pe_v_tile(pe, ph, t):
            src, ring, _, _, turned_sem, big_out, small_out = VKIND[ph.kind]
            pe.wait_ge(out_of["act"], ph.out0 + t + 1)
            if t >= 2:
                pe.wait_ge(big_out, t - 1)
                pe.wait_ge(small_out, t - 1)
            nc.tensor.transpose(aux45[:, t % 2, 0:P], src[:, t % ring, 0:P], ident)
            nc.tensor.transpose(aux45[:, t % 2, P:2 * P], src[:, t % ring, P:S], ident)
            nc.tensor.transpose(aux45[0:B, t % 2, 256:256 + P], src[:, t % ring, S:T], ident).then_inc(turned_sem, 1)

        def decay(h, a, b):
            t0 = TABLES["decay"][0] + h * 2 * P
            return tab[:, t0 + a:t0 + b]

        def pe_ret_a(pe, h):
            if h:
                pe.wait_ge(kdec_done, 2 * h)
                pe.wait_ge(orms_done, h)
                pe.wait_ge(adec_done, 2 * h)
            for c in range(2):
                for p in range(2):
                    last = nc.tensor.transpose(bank5[:, (2 * c + p) * P:(2 * c + p + 1) * P],
                                               kr[:, 2 * h + p, c * P:(c + 1) * P], ident)
            last.then_inc(kt_psum, 1)
            for p in range(2):
                nc.tensor.matmul(bank4[:, 0:S], kr[:, 2 * h + p, 0:P], qr[:, 2 * h + p, 0:S],
                                 start=p == 0, stop=p == 1)
            for p in range(2):
                last = nc.tensor.matmul(bank4[:, S:S + P], kr[:, 2 * h + p, P:S], qr[:, 2 * h + p, P:S],
                                        start=p == 0, stop=p == 1)
            last.then_inc(a_psum, 1)

        def act_ret_k(act, h):
            act.wait_ge(kt_psum, h + 1)
            if h:
                act.wait_ge(snew_psum, h)
            for c in range(2):
                col = TABLES["kdec"][0] + 2 * h + c
                nc.scalar.activation(k_dec[:, c], bank5[:, c * 2 * P:(c + 1) * 2 * P], ACT.Copy,
                                     scale=tab[:, col:col + 1]).then_inc(kdec_done, 1)

        def dve_ret_a(dve, h):
            dve.wait_ge(a_psum, h + 1)
            if h:
                dve.wait_ge(o_psum, h)
            nc.vector.tensor_tensor(a_dec[:, 0:S], bank4[:, 0:S], decay(h, 0, S), ALU.mult).then_inc(adec_done, 1)
            nc.vector.tensor_tensor(a_dec[:, S:S + P], bank4[:, S:S + P], decay(h, 0, P),
                                    ALU.mult).then_inc(adec_done, 1)

        def pe_ret_o(pe, h):
            pe.wait_ge(adec_done, 2 * h + 2)
            if h:
                pe.wait_ge(snew_out, 2 * h)
            for e in range(4):
                out = aux67[:, e // 2, (e % 2) * S:(e % 2 + 1) * S]
                cols = slice(h * RV + e * P, h * RV + (e + 1) * P)
                nc.tensor.matmul(out, v_ret[:, 0, cols], a_dec[:, 0:S], start=True, stop=False)
                last = nc.tensor.matmul(out[:, P:S], v_ret[:, 1, cols], a_dec[:, S:S + P], start=False, stop=True)
            last.then_inc(o_psum, 1)

        def act_ret_o(act, h):
            act.wait_ge(o_psum, h + 1)
            if h:
                act.wait_ge(ob_done, h)
            src = aux67[:].rearrange("p c (e f) -> p (c e) f", e=2)
            nc.scalar.activation(o_ret[:], src, ACT.Copy).then_inc(o_out, 1)
            nc.scalar.activation(o_sq[:], src, ACT.Square).then_inc(osq_done, 1)

        def dve_ret_sum(dve, h):
            dve.wait_ge(osq_done, h + 1)
            if h:
                dve.wait_ge(oms_psum, h)
            nc.vector.tensor_reduce(o_sum[:], o_sq[:].rearrange("p e f -> p f e"), AX.X, ALU.add).then_inc(osum_done, 1)

        def pe_ret_sum(pe, h):
            pe.wait_ge(osum_done, h + 1)
            pe.wait_ge(kdec_done, 2 * h + 2)
            nc.tensor.matmul(bank5[:, 0:S], ones, o_sum[:], start=True, stop=True).then_inc(oms_psum, 1)

        def act_ret_rms(act, h):
            act.wait_ge(oms_psum, h + 1)
            if h:
                act.wait_ge(ob_done, h)
            nc.scalar.activation(o_rms[:], bank5[:, 0:S], ACT.Sqrt, bias=eps, scale=1.0 / RV).then_inc(orms_done, 1)

        def dve_ret_norm(dve, ph, h):
            dve.wait_ge(orms_done, h + 1)
            nc.vector.reciprocal(o_rms[:], o_rms[:]).then_inc(orinv_done, 1)
            dve.wait_ge(orinv_done, h + 1)
            nc.vector.tensor_tensor(o_ret[:], o_ret[:], o_rms[:].unsqueeze(1).to_broadcast([P, 4, S]),
                                    ALU.mult).then_inc(on_done, 1)
            dve.wait_ge(on_done, h + 1)
            dve.wait_ge(out_of["dve"], ph.out0 + 4 * h + 4)
            nc.vector.tensor_tensor(ob[:, 4 * h:4 * h + 4, 0:S], ob[:, 4 * h:4 * h + 4, 0:S], o_ret[:],
                                    ALU.mult).then_inc(ob_done, 1)

        def pe_ret_state(pe, h):
            pe.wait_ge(kdec_done, 2 * h + 2)
            pe.wait_ge(osq_done, h + 1)
            for p in range(2):
                for c in range(2):
                    last = nc.tensor.matmul(aux67[:, p], k_dec[:, c, p * P:(p + 1) * P],
                                            v_ret[:, c, h * RV:(h + 1) * RV], start=c == 0, stop=c == 1)
            last.then_inc(snew_psum, 1)

        def act_ret_state(act, h):
            act.wait_ge(snew_psum, h + 1)
            if h:
                act.wait_ge(ret_stored, 16 * h)
            for p in range(2):
                nc.scalar.activation(s_new[:, p], aux67[:, p], ACT.Copy).then_inc(snew_out, 1)

        def act_gr_tile(act, ph, t):
            act.wait_ge(pe_half, 4 * ph.q0 + t + 1)
            if t >= 2:
                act.wait_ge(out_of["dve"], ph.out0 + t - 1)
            nc.scalar.activation(sig[:, t % 2], acc[t % 4][:, 0:T], ACT.Sigmoid).then_inc(sig_done, 1)

        def dve_gr_tile(dve, ph, t):
            dve.wait_ge(sig_done, t + 1)
            nc.vector.tensor_tensor(ob[:, t], sig[:, t % 2], acc[t % 4][:, 0:T], ALU.mult).then_inc(out_of["dve"], 1)

        def qk_tile(t, it):
            return qk[:, t] if not moving(it) else qk[:, bass.ds(t + 4 * it, 1)].squeeze(1)

        def act_qk_evac(act, ph, qq, j, it=0):
            t = 4 * qq + j
            act.wait_ge(pe_half, 4 * ph.q0 + t + 1 + 4 * it)
            if t >= 2:
                act.wait_ge(qk_ms_psum, t - 1 + 4 * it)
            nc.scalar.activation(qk_sq[:, j % 2], acc[j][:, 0:T], ACT.Square).then_inc(qk_sq_done, 1)
            col = 3 * KD + (0 if t < AT else 1)
            nc.scalar.activation(qk_tile(t, it), acc[j][:, 0:T], ACT.Copy,
                                 scale=gain[:, col:col + 1]).then_inc(out_of["act"], 1)

        def pe_qk_ms(pe, t, it=0):
            pe.wait_ge(qk_sq_done, t + 1 + 4 * it)
            if t >= 4 and t % 4 == 0:
                pe.wait_ge(qk_rms_done, t // 4 + it)
            if t:
                pe.wait_ge(os_out, t + 4 * it)
            j = t % 4
            nc.tensor.matmul(bank7[32 * j:32 * j + 32, 128:128 + T],
                             blocks[:, 0:P:4], qk_sq[:, t % 2],
                             start=True, stop=True).then_inc(qk_ms_psum, 1)

        def act_qk_rms(act, quad, it=0):
            act.wait_ge(qk_ms_psum, 4 * quad + 4 + 4 * it)
            if quad:
                act.wait_ge(qk_rinv_done, quad + it)
            nc.scalar.activation(qk_rms[:], bank7[:, 128:128 + T], ACT.Sqrt, bias=eps,
                                 scale=1.0 / AE).then_inc(qk_rms_done, 1)

        def dve_qk_rinv(dve, quad, it=0):
            dve.wait_ge(qk_rms_done, quad + 1 + it)
            if quad:
                dve.wait_ge(qk_spread, 4 * quad + 4 * it)
            nc.vector.reciprocal(qk_rinv[:], qk_rms[:]).then_inc(qk_rinv_done, 1)

        def pe_qk_rot(pe, ph, t, it=0):
            pe.wait_ge(out_of["act"], ph.out0 + t + 1 + 4 * it)
            if t:
                pe.wait_ge(qk_sin, t + 4 * it)
            nc.tensor.matmul(bank4[:, 0:T], turn, qk_tile(t, it), start=True, stop=True).then_inc(qk_rot_psum, 1)

        def pool_qk_rot(pool, ph, t):
            pool.wait_ge(out_of["act"], ph.out0 + t + 1)
            nc.gpsimd.tensor_tensor(rot_c[:, t % 2], qk[:, t], const("cos_a"), ALU.mult).then_inc(qk_cos, 1)
            pool.wait_ge(qk_sin, t + 1)
            pool.wait_ge(qk_cos, t + 1)
            nc.gpsimd.tensor_tensor(qk[:, t], rot_c[:, t % 2], rot_s[:, t % 2], ALU.add).then_inc(qk_turned, 1)

        def dve_qk_sin(dve, t, it=0):
            dve.wait_ge(qk_rot_psum, t + 1 + 4 * it)
            if t >= 2:
                dve.wait_ge(qk_turned, t - 1 + 4 * it)
            nc.vector.tensor_tensor(rot_s[:, t % 2], bank4[:, 0:T], const("sin_a"), ALU.mult).then_inc(qk_sin, 1)

        def pe_qk_spread(pe, t, it=0):
            pe.wait_ge(qk_rinv_done, t // 4 + 1 + it)
            if t:
                pe.wait_ge(qk_done, t + 4 * it)
            j = t % 4
            rows = slice(32 * j, 32 * j + 32)
            nc.tensor.matmul(bank5[:, 0:T], const("spread")[rows], qk_rinv[rows], start=True, stop=True).then_inc(qk_spread, 1)

        def dve_qk_norm(dve, t, it=0):
            dve.wait_ge(qk_spread, t + 1 + 4 * it)
            dve.wait_ge(qk_turned, t + 1 + 4 * it)
            nc.vector.tensor_tensor(qk_tile(t, it), qk_tile(t, it), bank5[:, 0:T], ALU.mult).then_inc(qk_done, 1)

        def sp_state_load(sp, b, h, it=0):
            src = state_in[bass.ds(b + it, 1), h].squeeze(0) if moving(it) else state_in[b + it, h]
            src = src.rearrange("(p r) e -> p (r e)", r=2)
            if b:
                sp.wait_ge(state_stored[h], 16 * b + 16 * it)
            sp.dma_start(state[:, h], src).then_inc(state_in_sem[h], 16)

        def sp_state_store(sp, b, h, it=0):
            sp.wait_ge(os_psum, 4 * b + h + 1 + 4 * it)
            dst = state_out[b + it, h] if not moving(it) else state_out[bass.ds(b + it, 1), h].squeeze(0)
            sp.dma_start(dst.rearrange("(p r) e -> p (r e)", r=2), state[:, h]).then_inc(state_stored[h], 16)

        def act_pick(act, b, it=0):
            if b:
                act.wait_ge(vb_psum, RH * b + RH * it)
            nc.scalar.activation(picked[0:PICK], pick[0:PICK, bass.ds(b + it, 1)] if moving(it) else
                                 pick[0:PICK, b:b + 1], ACT.Copy).then_inc(picked_done, 1)

        def pe_state_v(pe, b, h, it=0):
            s = 4 * b + h
            pe.wait_ge(picked_done, b + 1 + it)
            if s:
                pe.wait_ge(state_new, 2 * s + 8 * it)
            nc.tensor.matmul(bank6[:, :], picked[0:PICK, 0:1].to_broadcast([PICK, P]),
                             vr_hl[0:PICK, h * RV:(h + 1) * RV], start=True, stop=True).then_inc(vb_psum, 1)

        def act_state(act, b, h, it=0):
            act.wait_ge(state_in_sem[h], 16 * (b + 1) + 16 * it)
            g0 = TABLES["gamma"][0] + h
            nc.scalar.activation(state[:, h], state[:, h], ACT.Copy, scale=tab[:, g0:g0 + 1]).then_inc(state_scaled, 1)

        def dve_state(dve, b, h, it=0):
            s = 4 * b + h
            dve.wait_ge(state_scaled, s + 1 + 4 * it)
            dve.wait_ge(vb_psum, s + 1 + 4 * it)
            for p in range(2):
                half = state[:, h, p * RV:(p + 1) * RV]
                nc.vector.scalar_tensor_tensor(half, bank6[:, :], kr_s[:, 2 * h + p, bass.ds(b + it, 1)] if moving(it) else kr_s[:, 2 * h + p, b:b + 1], half,
                                               ALU.mult, ALU.add).then_inc(state_new, 1)

        def pe_state_o(pe, b, h, it=0):
            s = 4 * b + h
            pe.wait_ge(state_new, 2 * s + 2 + 8 * it)
            if s:
                pe.wait_ge(os_out, s + 4 * it)
            for e in range(4):
                c = 32 * (h % 2) + B * e
                for p in range(2):
                    last = nc.tensor.matmul(bank7[:, c:c + B], state[:, h, p * RV + e * P:p * RV + (e + 1) * P],
                                            qr_s[:, 2 * h + p], start=p == 0, stop=p == 1)
            last.then_inc(os_psum, 1)

        def act_state_o(act, b, h, it=0):
            s = 4 * b + h
            act.wait_ge(os_psum, s + 1 + 4 * it)
            own = bank7[:, 32 * (h % 2):32 * (h % 2) + 32].rearrange("p (e b) -> p e b", e=4)
            if moving(it):
                src, dst = (v[:, :, bass.ds(b + it, 1)].squeeze(2) for v in (own, o_s[:, 4 * h:4 * h + 4]))
            else:
                src, dst = own[:, :, b], o_s[:, 4 * h:4 * h + 4, b]
            nc.scalar.activation(dst, src, ACT.Copy).then_inc(os_out, 1)

        def pe_scores(pe, i):
            h, qb = i // 2, i % 2
            if i:
                pe.wait_ge(att_masked, i)
            rows = slice((h % 2) * AE, (h % 2 + 1) * AE)
            keys = (qb + 1) * P
            for g in range(G):
                t = g * 4 + h // 2
                last = nc.tensor.matmul(aux45[:, g // 2, (g % 2) * S + (S - keys if qb == 0 else 0):
                                              (g % 2) * S + S],
                                        qk[rows, t, qb * P:(qb + 1) * P], qk[rows, AT + t, 0:keys],
                                        start=True, stop=True)
            last.then_inc(att_scores, 1)

        def att_view(t, qb):
            return t[:, :, P:2 * P] if qb == 0 else t

        def dve_scores(dve, i):
            qb = i % 2
            dve.wait_ge(att_scores, i + 1)
            if i:
                dve.wait_ge(att_turned, i)
            scores = aux45[:].rearrange("p c f -> p (c f)")[:, 0:G * S].rearrange("p (g k) -> p g k", g=G)
            mask = const("mask").rearrange("p (g k) -> p g k", g=G)
            nc.vector.tensor_tensor(att_view(prob[:], qb), att_view(scores, qb), att_view(mask, qb),
                                    ALU.add).then_inc(att_masked, 1)
            dve.wait_ge(att_masked, i + 1)
            nc.vector.tensor_reduce(att_m[:, 0:1], att_view(prob[:], qb), AX.XY, ALU.max).then_inc(att_step, 1)
            dve.wait_ge(att_step, 2 * i + 1)
            nc.vector.tensor_scalar(att_m[:, 1:2], att_m[:, 0:1], -SCALE, None, ALU.mult).then_inc(att_negmax, 1)

        att_step = sem("att_step")

        def act_exp(act, i):
            act.wait_ge(att_negmax, i + 1)
            view = att_view(prob[:], i % 2)
            nc.scalar.activation(view, view, ACT.Exp, bias=att_m[:, 1:2], scale=SCALE,
                                 accum_out=att_m[:, 2:3]).then_inc(att_exp, 1)

        def dve_prob(dve, i):
            dve.wait_ge(att_exp, i + 1)
            nc.vector.reciprocal(att_m[:, 3:4], att_m[:, 2:3]).then_inc(att_step, 1)
            dve.wait_ge(att_step, 2 * i + 2)
            view = att_view(prob[:], i % 2)
            nc.vector.tensor_scalar(view, view, att_m[:, 3:4], None, ALU.mult).then_inc(att_prob, 1)

        def att_blocks(i):
            return [(g, kb) for g in range(G) for kb in range(i % 2 + 1)]

        def turned_copies(i):
            return 3 * ((i + 1) // 2) + (i + 1) % 2

        def pe_turn(pe, i):
            pe.wait_ge(att_prob, i + 1)
            if i:
                pe.wait_ge(att_out, i)
            for n, (g, kb) in enumerate(att_blocks(i)):
                c = kb * P if i % 2 else P
                last = nc.tensor.transpose(aux67[:, n // 4, (n % 4) * P:(n % 4 + 1) * P], prob[:, g, c:c + P], ident)
            last.then_inc(att_turned, 1)

        def turned_copy(eng, i, part):
            n = len(att_blocks(i))
            a, b = (0, min(n, 4)) if part == 0 else (4, n)
            if a >= b:
                return
            eng.wait_ge(att_turned, i + 1)
            if i:
                eng.wait_ge(att_pv, i)
            src = aux67[:].rearrange("p c f -> p (c f)")[:, a * P:b * P]
            if part == 0:
                nc.scalar.activation(probT[:, a * P:b * P], src, ACT.Copy).then_inc(att_turned_out, 1)
            else:
                nc.vector.tensor_copy(probT[:, a * P:b * P], src).then_inc(att_turned_out, 1)

        def pe_pv(pe, i):
            h, qb = i // 2, i % 2
            pe.wait_ge(att_turned_out, turned_copies(i))
            blks = att_blocks(i)
            out = bank7[(h % 2) * AE:(h % 2 + 1) * AE, 256:256 + P]
            for n, (g, kb) in enumerate(blks):
                last = nc.tensor.matmul(out, v_tok[:, kb, g * AW + h * AE:g * AW + (h + 1) * AE],
                                        probT[:, n * P:(n + 1) * P], start=n == 0, stop=n == len(blks) - 1)
            last.then_inc(att_pv, 1)

        def act_pv(act, i):
            h, qb = i // 2, i % 2
            act.wait_ge(att_pv, i + 1)
            rows = slice((h % 2) * AE, (h % 2 + 1) * AE)
            nc.scalar.activation(oa[rows, h // 2, qb * P:(qb + 1) * P], bank7[rows, 256:256 + P],
                                 ACT.Copy).then_inc(att_out, 1)

        def sp_kv_load(sp, n, part):
            i = n % (B * G)
            b, g = i // G, i % G
            if n >= 3:
                m = n - 3
                if m < B * G:
                    sp.wait_ge(kq_done, 2 * m + 2)
                else:
                    sp.wait_ge(dec_v_done, m - B * G + 1)
            dil = GROUPS[g][1]
            src = caches[g][b].rearrange("(p d) c -> p d c", d=dil)[:, 0, part * AW:(part + 1) * AW]
            sp.dma_start(kv[:, n % 3], src).then_inc(kv_in[n % 3], 16)

        def pe_dec_q(pe, i):
            b, g = i // G, i % G
            if i >= 2:
                pe.wait_ge(kq_done, 2 * (i - 2) + 1)
            nc.tensor.matmul(aux67[:, i % 2], pick[0:PICK, b:b + 1].to_broadcast([PICK, P]),
                             q_hl[0:PICK, g * AW:(g + 1) * AW], start=True, stop=True).then_inc(qb_psum, 1)

        def dve_dec_k(dve, i):
            b, g = i // G, i % G
            dve.wait_ge(kv_in[i % 3], 16 * (i // 3 + 1))
            dve.wait_ge(qb_psum, i + 1)
            nc.vector.tensor_tensor(kv[:, i % 3], kv[:, i % 3], aux67[:, i % 2], ALU.mult).then_inc(kq_done, 1)
            dve.wait_ge(kq_done, 2 * i + 1)
            out = dec_s[:, g].rearrange("p (r n b) -> p n r b", r=2, b=B)[:, :, :, b]
            nc.vector.tensor_reduce(out, kv[:, i % 3].rearrange("p (n r e) -> p n r e", r=2, e=AE), AX.X,
                                    ALU.add).then_inc(kq_done, 1)

        def dve_dec_own(dve):
            nc.vector.tensor_tensor(qk_own[:], qk[:, 0:AT, S:T], qk[:, AT:2 * AT, S:T], ALU.mult).then_inc(dec_dve, 1)

        def pe_dec_scores(pe):
            pe.wait_ge(dec_dve, 1)
            pe.wait_ge(kq_done, 2 * B * G)
            for g in range(G):
                nc.tensor.transpose(bank6[0:64, g * P:(g + 1) * P], dec_s[:, g], ident)
            for g in range(G):
                for r in range(2):
                    last = nc.tensor.matmul(bank6[32 * r:32 * r + 32, G * P + g:G * P + g + 1],
                                            qk_own[:, 4 * g:4 * g + 4].rearrange("p n b -> p (n b)"),
                                            blocks[:, r * AE:r * AE + 1], start=True, stop=True)
            last.then_inc(dec_pe, 1)

        NK = G * P + G

        def dve_dec_max(dve):
            dve.wait_ge(dec_pe, 1)
            nc.vector.tensor_reduce(dec_m[0:64, 0:1], bank6[0:64, 0:NK], AX.X, ALU.max).then_inc(dec_dve, 1)
            dve.wait_ge(dec_dve, 2)
            nc.vector.tensor_scalar(dec_m[0:64, 1:2], dec_m[0:64, 0:1], -SCALE, None, ALU.mult).then_inc(dec_dve, 1)

        def act_dec_exp(act):
            act.wait_ge(dec_dve, 3)
            nc.scalar.activation(dec_p[0:64, :], bank6[0:64, 0:NK], ACT.Exp, bias=dec_m[0:64, 1:2], scale=SCALE,
                                 accum_out=dec_m[0:64, 2:3]).then_inc(dec_act, 1)

        def dve_dec_prob(dve):
            dve.wait_ge(dec_act, 1)
            nc.vector.reciprocal(dec_m[0:64, 3:4], dec_m[0:64, 2:3]).then_inc(dec_dve, 1)
            dve.wait_ge(dec_dve, 4)
            nc.vector.tensor_scalar(dec_p[0:64, :], dec_p[0:64, :], dec_m[0:64, 3:4], None,
                                    ALU.mult).then_inc(dec_dve, 1)
            dve.wait_ge(dec_dve, 5)
            for g in range(G):
                nc.vector.tensor_scalar(dec_diag[0:64, g], ident[0:64, 0:64], dec_p[0:64, G * P + g:G * P + g + 1],
                                        None, ALU.mult).then_inc(dec_dve, 1)

        def pe_dec_turn(pe):
            pe.wait_ge(dec_dve, 5 + G)
            for g in range(G):
                nc.tensor.transpose(bank5[:, g * 64:(g + 1) * 64], dec_p[0:64, g * P:(g + 1) * P], ident[0:64, 0:64])
            nc.tensor.matmul(bank4[0:B, 0:G * 64], const("rsel", 64), dec_diag[0:64].rearrange("p g r -> p (g r)"),
                             start=True, stop=True).then_inc(dec_pe, 1)

        def act_dec_turn(act):
            act.wait_ge(dec_pe, 2)
            nc.scalar.activation(dec_pT[:].rearrange("p g r -> p (g r)"), bank5[:, 0:G * 64],
                                 ACT.Copy).then_inc(dec_act, 1)
            nc.scalar.activation(dec_own[0:B].rearrange("p g r -> p (g r)"), bank4[0:B, 0:G * 64],
                                 ACT.Copy).then_inc(dec_act, 1)

        def pe_dec_own(pe):
            pe.wait_ge(dec_act, 3)
            for g in range(G):
                for n in range(4):
                    nc.tensor.matmul(bank7[:, n * 16:(n + 1) * 16].rearrange("p (r b) -> p r b", r=2),
                                     v_s[0:B, g * AW + n * P:g * AW + (n + 1) * P],
                                     dec_own[0:B, g].rearrange("p (r n b) -> p n r b", r=2, b=B)[:, n],
                                     start=g == 0 and n == 0, stop=False, skip_group_check=True)

        def pe_dec_v(pe, i):
            b, g = i // G, i % G
            n0 = B * G + i
            pe.wait_ge(kv_in[n0 % 3], 16 * (n0 // 3 + 1))
            for n in range(4):
                out = bank7[:, n * 16:(n + 1) * 16].rearrange("p (r b) -> p r b", r=2)[:, :, b]
                last = nc.tensor.matmul(out, kv[:, n0 % 3, n * P:(n + 1) * P],
                                        dec_pT[:, g].rearrange("p (r n b) -> p n r b", r=2, b=B)[:, n, :, b],
                                        start=False, stop=i == B * G - 1, skip_group_check=True)
            last.then_inc(dec_v_done, 1)

        def dve_dec_out(dve):
            dve.wait_ge(dec_v_done, B * G)
            for r in range(2):
                rows = slice(r * AE, (r + 1) * AE)
                nc.vector.tensor_copy(oa[rows, :, S:T],
                                      bank7[rows, 0:64].rearrange("p (n r b) -> p n r b", r=2, b=B)[:, :, r]
                                      ).then_inc(dec_dve, 1)
        DEC_DVE = 5 + G + 2

        fi1, fo1, p_qr, p_kr, p_vr, p_gr, p_qk, p_v, p_gb, p_pb, p_ga, p_pa, p_wo, fi2, fo2 = phases
        NSTATE_LOOP = p_qk.quads
        V_TURNED = {3: (0,), 4: (1,), 5: (2, 3), 6: (4, 5), 7: (6,), 8: (7,), 9: (8,), 10: (9,), 11: (10,)}
        QK_LAST = {0: (19,), 1: (20, 21), 2: (22, 23)}
        SMALL_AT = QKS_AT = 9

        block = ctx.enter_context(nc.Block())

        @block.sync
        def _(sp):
            sp.dma_start(x[:], xT).then_inc(const_in, 16)
            sp.dma_start(tab[:], tables).then_inc(const_in, 16)
            sp.dma_start(gain[:], gains).then_inc(const_in, 16)

            ROWS = 256
            pieces = []
            for g in (2, 1, 0):
                n = caches[g].shape[0] * caches[g].shape[1]
                src = caches[g].rearrange("b w c -> (b w) c")
                dst = kv_outs[g].rearrange("b w c -> (b w) c")
                for a in range(0, n, ROWS):
                    if a + ROWS < n:
                        pieces.append((dst, src, a, ROWS))
                    else:
                        pieces += [(dst, src, a, ROWS - 16), (dst, src, a + ROWS - 16, 15)]

            def roll(sp, c, it=0):
                dst, src, a, rows = pieces[c]
                if not moving(it):
                    sp.dma_start(dst[a:a + rows], src[a + 1:a + 1 + rows]).then_inc(rolled, 16)
                else:
                    sp.dma_start(dst[bass.ds(a + ROWS * it, rows)],
                                 src[bass.ds(a + 1 + ROWS * it, rows)]).then_inc(rolled, 16)

            first = 4 * (fi1.quads + fo1.quads) // 3
            with sp.Fori(0, first) as it:
                sp.wait_ge(pe_half, 3 * it + 2)
                roll(sp, 0, it)
            done = first

            def roll_more(sp, n):
                nonlocal done
                for _ in range(n):
                    if done < len(pieces):
                        roll(sp, done)
                        done += 1

            for q in range(p_qr.q0, p_gr.q0 + p_gr.quads):
                sp.wait_ge(pe_half, 4 * q)
                roll_more(sp, 2 if KIND_OF[q] == "gr" else 1)
                if q >= p_gr.q0 + 1:
                    h = q - p_gr.q0 - 1
                    sp.wait_ge(snew_out, 2 * h + 2)
                    sp.dma_start(ret_out[h].rearrange("(p r) e -> p (r e)", r=2),
                                 s_new[:].rearrange("p r e -> p (r e)")).then_inc(ret_stored, 16)
            sp.wait_ge(snew_out, 2 * RH)
            sp.dma_start(ret_out[RH - 1].rearrange("(p r) e -> p (r e)", r=2),
                         s_new[:].rearrange("p r e -> p (r e)")).then_inc(ret_stored, 16)
            for h in range(RH):
                sp_state_load(sp, 0, h)
            with sp.Fori(0, NSTATE_LOOP) as it:
                for h in range(RH):
                    sp_state_store(sp, 0, h, it)
                    sp_state_load(sp, 1, h, it)
            sp_state_done = NSTATE_LOOP
            for b in range(sp_state_done, B):
                for h in range(RH):
                    sp_state_store(sp, b, h)
                    if b + 1 < B:
                        sp_state_load(sp, b + 1, h)
            sp.wait_ge(qk_done, 2 * AT)
            sp.dma_start(kT_out, qk[:, AT:2 * AT]).then_inc(stored, 16)
            for n in range(2 * B * G):
                sp_kv_load(sp, n, n // (B * G))
                if n == 5:
                    sp.wait_ge(v_out_sem, AT)
                    sp.dma_start(v_out.rearrange("(c p) f -> p c f", c=2), v_tok[:]).then_inc(stored, 16)
                if n % 3 == 2:
                    roll_more(sp, 1)
            for q in range(p_pb.q0 + 2, p_wo.q0):
                sp.wait_ge(pe_half, 4 * q)
                roll_more(sp, 2)
            paced = 4 * fi2.q0
            while done < len(pieces):
                sp.wait_ge(pe_half, paced)
                roll_more(sp, 1)
                paced += 3
            sp.wait_ge(rolled, 16 * len(pieces))
            sp.wait_ge(qks_out, 6)
            sp.wait_ge(vs_out, AT)
            for g in range(G):
                w = caches[g].shape[1]
                sp.dma_start(kv_outs[g][:, w - 1, 0:AW], k_s[0:B, g * AW:(g + 1) * AW]).then_inc(stored, 16)
                sp.dma_start(kv_outs[g][:, w - 1, AW:2 * AW], v_s[0:B, g * AW:(g + 1) * AW]).then_inc(stored, 16)
            for m in range(KD):
                sp.wait_ge(out_of["dve"], fo2.out0 + m + 1)
                sp.dma_start(yT[:, m], x[:, m]).then_inc(stored, 16)
            sp.wait_ge(stored, 16 * STORES)
            sp.wait_ge(ret_stored, 16 * RH)

        @block.scalar
        def _(act):
            load_unit(act, 0)
            load_unit(act, 1)
            act.wait_ge(const_in, 48)
            for m in range(KD):
                act_square(act, 0, m)
            hi_half(act, 0, 0)
            hi_half(act, 0, 1)
            act_norm(act, 0)
            hi_half(act, 0, 2)
            hi_half(act, 0, 3)
            act.wait_ge(lo_done, 2)
            load_unit(act, 2)

            def ffn(fi, fo, norm):
                act_fi_quad(act, fi, 0)
                with act.Fori(0, fi.quads - 3) as it:
                    act_fi_quad(act, fi, 1, it)
                for qq in range(fi.quads - 2, fi.quads):
                    act_fi_quad(act, fi, qq)
                with act.Fori(0, fo.quads // 2 - 1) as it:
                    for m in range(2):
                        act_fo_quad(act, fo, m, 2 * it, norm)
                for m in range(fo.quads - 2, fo.quads):
                    act_fo_quad(act, fo, m, 0, norm)

            ffn(fi1, fo1, 1)
            act_norm(act, 1)
            for which, ph in enumerate((p_qr, p_kr)):
                for qq in range(ph.quads):
                    act_rr_quad(act, ph, qq, which)
            for t in range(16):
                act_ahead(act, p_vr.q0 + t // 4, t % 4)
                act_v_tile(act, p_vr, t)
                if t:
                    act_v_small(act, p_vr, t - 1)
            act_v_small(act, p_vr, 15)
            act.wait_ge(rr_done, 2 * RH)
            act.wait_ge(rr_pool, 6 * RH)
            nc.scalar.activation(qr_s[:], qr[:, :, S:T], ACT.Copy).then_inc(rs_copied, 1)
            nc.scalar.activation(kr_s[:], kr[:, :, S:T], ACT.Copy).then_inc(rs_copied, 1)
            act.wait_ge(cleared, 2)
            act.wait_ge(vrs_out, 16)
            nc.scalar.activation(vr_hl[0:B], vs_ret[0:B], ACT.Copy).then_inc(vr_hi, 1)
            nc.scalar.activation(pick[0:PICK], const("pick", PICK), ACT.Copy).then_inc(pick_done, 1)
            act.wait_ge(pick_done, 1)
            act_pick(act, 0)
            for h in range(RH):
                act_ret_k(act, h)
                for j in range(4):
                    act_ahead(act, p_gr.q0 + h, j)
                    act_gr_tile(act, p_gr, 4 * h + j)
                    if j == 0:
                        act_ret_o(act, h)
                    if j == 2:
                        act_ret_state(act, h)
                        act_ret_rms(act, h)

            def qk_quad(qq, it=0):
                for j in range(4):
                    if j == 0 and qq:
                        act_qk_rms(act, qq - 1, it)
                    act_ahead(act, p_qk.q0 + qq, j, it)
                    act_qk_evac(act, p_qk, qq, j, it)
                    act_state(act, qq, j, it)
                    if qq or j:
                        act_state_o(act, qq if j else qq - 1, (j - 1) % 4, it)
                act_pick(act, qq + 1, it)

            qk_quad(0)
            with act.Fori(0, AT // 4 - 1) as it:
                qk_quad(1, it)
            with act.Fori(0, AT // 4) as it:
                qk_quad(AT // 4, it)
            act.wait_ge(ret_stored, 16 * RH)
            for t in range(AT):
                if t == 0:
                    act_qk_rms(act, p_qk.quads - 1)
                act_ahead(act, p_v.q0 + t // 4, t % 4)
                act_v_tile(act, p_v, t)
                s = RH * NSTATE_LOOP + t
                if s < B * RH:
                    act_state(act, s // 4, s % 4)
                if s <= B * RH:
                    act_state_o(act, (s - 1) // 4, (s - 1) % 4)
                if s % 4 == 3 and s < B * RH - 1:
                    act_pick(act, s // 4 + 1)
                for i in V_TURNED.get(t, ()):
                    act_v_small(act, p_v, i)
                if t == SMALL_AT:
                    act.wait_ge(os_out, B * RH)
                    nc.scalar.activation(o_s2[:], o_s[:], ACT.Square).then_inc(small_act, 1)
                if t == SMALL_AT + 1:
                    act.wait_ge(small_pe, 1)
                    nc.scalar.activation(os_sum[:].rearrange("p h b -> p (h b)"), bank4[:, 0:RH * B], ACT.Sqrt,
                                         bias=eps, scale=1.0 / RV).then_inc(small_act, 1)
                if t >= QKS_AT:
                    for n in range(2 * (t - QKS_AT), 2 * (t - QKS_AT) + 2):
                        act.wait_ge(qks_psum, n + 1)
                        dst = (q_hl[0:B, :] if n < 3 else k_s)[:, (n % 3) * AW:(n % 3 + 1) * AW]
                        nc.scalar.activation(dst, aux67[0:B, n % 2], ACT.Copy).then_inc(qks_out, 1)

            def split_ob(h):
                nc.scalar.activation(obh[:, 4 * h:4 * h + 4], ob[:, 4 * h:4 * h + 4], ACT.Copy).then_inc(ob_hi, 1)

            act.wait_ge(small_step, 4)
            for h in range(RH):
                act.wait_ge(state_stored[h], 16 * B)
            split_ob(0)
            for t in range(KD):
                act_ahead(act, p_gb.q0 + t // 4, t % 4)
                if t == 0:
                    act_v_small(act, p_v, AT - 1)
                if t < 3:
                    split_ob(t + 1)
                act.wait_ge(pe_half, 4 * p_gb.q0 + t + 1)
                act.wait_ge(ob_split, 1 + t // 4)
                nc.scalar.activation(gate_b[:, t], acc[t % 4][:, 0:T], ACT.Sigmoid).then_inc(out_of["act"], 1)
            act_dec_exp(act)
            act_dec_turn(act)
            for i in range(8):
                act_ahead(act, p_pb.q0 + i // 4, i % 4)

            def att(i):
                if i >= 1:
                    turned_copy(act, i - 1, 0)
                if i < 16:
                    act_exp(act, i)

            for i in range(8):
                att(i)
                if i >= 1:
                    act_pv(act, i - 1)
                act_ahead(act, p_pb.q0 + 2 + i // 4, i % 4)
            for t in range(KD):
                att(8 + t)
                act_pv(act, 7 + t)
                act_ahead(act, p_ga.q0 + t // 4, t % 4)
                act.wait_ge(pe_half, 4 * p_ga.q0 + t + 1)
                nc.scalar.activation(gate_a[:, t], acc[t % 4][:, 0:T], ACT.Sigmoid).then_inc(out_of["act"], 1)
            att(16)
            act_pv(act, 15)
            act.wait_ge(att_out, 16)
            act.wait_ge(dec_dve, DEC_DVE)
            nc.scalar.activation(oah[:], oa[:], ACT.Copy).then_inc(oa_hi, 1)
            for j in range(4):
                act_ahead(act, p_pa.q0, j)
                for m in (2 * j, 2 * j + 1):
                    act.wait_ge(merge_done, m + 1)
                    nc.scalar.activation(hh[:, m], merge[:, m % 2], ACT.Copy).then_inc(merge_hi, 1)
            for m in range(KD):
                act_ahead(act, p_wo.q0 + m // 4, m % 4)
                act.wait_ge(out_of["dve"], p_wo.out0 + m + 1)
                act_square(act, 2, m)
            act_norm(act, 2)
            ffn(fi2, fo2, None)

        @block.vector
        def _(dve):
            dve.wait_ge(const_in, 48)
            for m in range(KD):
                dve_sum_square(dve, 0, m)
            lo_half(dve, 0, 0)
            lo_half(dve, 0, 1)
            dve_norm(dve, 0)
            lo_half(dve, 0, 2)
            lo_half(dve, 0, 3)

            def ffn(fi, fo, norm):
                dve_fi_quad(dve, fi, 0)
                with dve.Fori(0, fi.quads - 3) as it:
                    dve_fi_quad(dve, fi, 1, it)
                for qq in range(fi.quads - 2, fi.quads):
                    dve_fi_quad(dve, fi, qq)
                start = 0
                if norm is not None:
                    for m in range(2):
                        dve_fo_quad(dve, fo, m, 0, norm)
                    start = 2
                with dve.Fori(0, (fo.quads - 2 - start) // 2) as it:
                    for m in range(start, start + 2):
                        dve_fo_quad(dve, fo, m, 2 * it, norm)
                for m in range(fo.quads - 2, fo.quads):
                    dve_fo_quad(dve, fo, m, 0, norm)

            ffn(fi1, fo1, 1)
            dve_norm(dve, 1)
            for which, ph in enumerate((p_qr, p_kr)):
                for t in range(2 * RH):
                    dve_ahead(dve, ph.q0 + t // 4, t % 4)
                    if t % 2:
                        turn_head(dve, nc.vector, ph, t // 2, which)
            for t in range(16):
                dve_ahead(dve, p_vr.q0 + t // 4, t % 4)
                if t:
                    dve_v_tile(dve, p_vr, t - 1)
            dve_v_tile(dve, p_vr, 15)
            dve.wait_ge(vr_hi, 1)
            nc.vector.tensor_tensor(vr_hl[32:PICK], vs_ret[0:B], vr_hl[0:B].bitcast(F32), ALU.subtract).then_inc(vr_lo, 1)
            for h in range(RH):
                dve_ret_a(dve, h)
                for j in range(4):
                    dve_ahead(dve, p_gr.q0 + h, j)
                    dve_gr_tile(dve, p_gr, 4 * h + j)
                    if j == 1:
                        dve_ret_sum(dve, h)
                dve_ret_norm(dve, p_gr, h)

            def qk_quad(qq, it=0):
                for j in range(4):
                    t = 4 * qq + j
                    dve_state(dve, qq, j, it)
                    dve_ahead(dve, p_qk.q0 + qq, j, it)
                    if t:
                        dve_qk_sin(dve, t - 1, it)
                    if j == 0 and qq:
                        dve_qk_rinv(dve, qq - 1, it)
                    if t >= 5:
                        dve_qk_norm(dve, t - 5, it)

            qk_quad(0)
            qk_quad(1)
            with dve.Fori(0, p_qk.quads - 2) as it:
                qk_quad(2, it)
            for t in range(AT):
                s = RH * NSTATE_LOOP + t
                if s < B * RH:
                    dve_state(dve, s // 4, s % 4)
                dve_ahead(dve, p_v.q0 + t // 4, t % 4)
                if t == 0:
                    dve_qk_sin(dve, 2 * AT - 1)
                    dve_qk_rinv(dve, p_qk.quads - 1)
                for i in QK_LAST.get(t, ()):
                    dve_qk_norm(dve, i)
                for i in V_TURNED.get(t, ()):
                    dve_v_tile(dve, p_v, i)
                if t == SMALL_AT:
                    dve.wait_ge(small_act, 1)
                    nc.vector.tensor_reduce(os_sum[:], o_s2[:].rearrange("p (h e) b -> p h b e", e=4), AX.X,
                                            ALU.add).then_inc(small_step, 1)
                if t >= QKS_AT:
                    for n in range(2 * (t - QKS_AT), min(3, 2 * (t - QKS_AT) + 2)):
                        dve.wait_ge(qks_out, n + 1)
                        cols = slice(n * AW, (n + 1) * AW)
                        nc.vector.tensor_tensor(q_hl[32:PICK, cols], aux67[0:B, n % 2], q_hl[0:B, cols].bitcast(F32),
                                                ALU.subtract).then_inc(qs_lo, 1)
            dve.wait_ge(small_act, 2)
            nc.vector.reciprocal(os_sum[:], os_sum[:]).then_inc(small_step, 1)
            dve.wait_ge(small_step, 2)
            nc.vector.tensor_tensor(o_s[:].rearrange("p (h e) b -> p h e b", e=4),
                                    o_s[:].rearrange("p (h e) b -> p h e b", e=4),
                                    os_sum[:].unsqueeze(2).to_broadcast([P, RH, 4, B]), ALU.mult).then_inc(small_step, 1)
            dve.wait_ge(small_step, 3)
            nc.vector.tensor_tensor(ob[:, :, S:T], ob[:, :, S:T], o_s[:], ALU.mult).then_inc(small_step, 1)
            dve_dec_own(dve)
            for t in range(KD):
                dve_ahead(dve, p_gb.q0 + t // 4, t % 4)
                if t == 0:
                    dve_v_tile(dve, p_v, AT - 1)
                for i in range(3 * t, 3 * t + 3):
                    dve_dec_k(dve, i)
            dve_dec_max(dve)
            dve_dec_prob(dve)

            def pb_tile(m):
                dve.wait_ge(pe_half, 4 * p_pb.q0 + 2 * m + 2)
                nc.vector.tensor_tensor(gate_b[:, m], gate_b[:, m], acc[m % 4][:, 0:T],
                                        ALU.mult).then_inc(out_of["dve"], 1)

            dve.wait_ge(out_of["act"], p_gb.out0 + KD)
            for i in range(8):
                dve_ahead(dve, p_pb.q0 + i // 4, i % 4)
                if i % 2:
                    pb_tile(i // 2)
            dve_dec_out(dve)

            def att(i):
                if i >= 1:
                    turned_copy(dve, i - 1, 1)
                if i < 16:
                    dve_scores(dve, i)
                    dve_prob(dve, i)

            for i in range(8):
                att(i)
                dve_ahead(dve, p_pb.q0 + 2 + i // 4, i % 4)
                if i % 2:
                    pb_tile(4 + i // 2)
            for t in range(KD):
                att(8 + t)
                dve_ahead(dve, p_ga.q0 + t // 4, t % 4)
            att(16)
            dve.wait_ge(oa_hi, 1)
            nc.vector.tensor_tensor(oal[:], oa[:], oah[:].bitcast(F32), ALU.subtract).then_inc(oa_split, 1)
            dve.wait_ge(out_of["act"], p_ga.out0 + KD)
            for j in range(4):
                dve_ahead(dve, p_pa.q0, j)
                for m in (2 * j, 2 * j + 1):
                    dve.wait_ge(pe_half, 4 * p_pa.q0 + j + 1)
                    if m >= 2:
                        dve.wait_ge(merge_done, m - 1)
                    nc.vector.tensor_tensor(merge_a[:, m % 2], gate_a[:, m], acc[m % 4][:, 0:T],
                                            ALU.mult).then_inc(out_of["dve"], 1)
            for m in range(KD):
                dve_ahead(dve, p_wo.q0 + m // 4, m % 4)
                dve.wait_ge(pe_half, 4 * p_wo.q0 + m + 1)
                dve_add_x(dve, p_wo, m, 1.0, m % 4)
                dve_sum_square(dve, 2, m)
            dve_norm(dve, 2)
            ffn(fi2, fo2, None)

        @block.gpsimd
        def _(pool):
            def ffn(fi):
                with pool.Fori(0, fi.quads) as it:
                    pool_fi_quad(pool, fi, 0, it)

            pool_norm(pool, 0)
            nc.gpsimd.memset(vr_hl[0:PICK].bitcast(F32), 0.0).then_inc(cleared, 1)
            nc.gpsimd.memset(q_hl[0:PICK].bitcast(F32), 0.0).then_inc(cleared, 1)
            ffn(fi1)
            pool_norm(pool, 1)
            for which, ph in enumerate((p_qr, p_kr)):
                for h in range(RH):
                    turn_head(pool, nc.gpsimd, ph, h, which)

            for t in range(2 * AT):
                pool_qk_rot(pool, p_qk, t)
            for h in range(RH):
                pool.wait_ge(ob_hi, h + 1)
                nc.gpsimd.tensor_tensor(obl[:, 4 * h:4 * h + 4], ob[:, 4 * h:4 * h + 4],
                                        obh[:, 4 * h:4 * h + 4].bitcast(F32), ALU.subtract).then_inc(ob_split, 1)
            for m in range(KD):
                pool.wait_ge(out_of["dve"], p_pa.out0 + m + 1)
                if m >= 2:
                    pool.wait_ge(merge_split, m - 1)
                nc.gpsimd.tensor_tensor(merge[:, m % 2], merge_a[:, m % 2], gate_b[:, m], ALU.add).then_inc(merge_done, 1)
                pool.wait_ge(merge_hi, m + 1)
                nc.gpsimd.tensor_tensor(hl[:, m], merge[:, m % 2], hh[:, m].bitcast(F32),
                                        ALU.subtract).then_inc(merge_split, 1)
            pool_norm(pool, 2)
            ffn(fi2)

        @block.tensor
        def _(pe):
            def ffn(fi, fo, r):
                pe_enter(pe, fi)
                norm = (normed_split, KD * r)
                pe_wide_first(fi, norm)
                with pe.Fori(0, fi.quads - 1) as it:
                    for j in range(4):
                        pe_wide_half(pe, fi, 1, j, it)
                with pe.Fori(0, fo.quads // 2) as it:
                    for m in range(2):
                        pe_fo_quad(pe, fo, m, m, 2 * it)

            def pe_wide_first(ph, norm):
                for j in range(4):
                    pe_wide_half(pe, ph, 0, j, 0, norm if j == 0 else None)

            pe.wait_ge(const_in, 48)
            pe_norm(pe, 0)
            ffn(fi1, fo1, 0)
            pe_norm(pe, 1)
            for ph in (p_qr, p_kr):
                pe_enter(pe, ph)
                for qq in range(ph.quads):
                    for j in range(4):
                        pe_wide_half(pe, ph, qq, j, 0, (normed_split, KD) if ph is p_qr and qq == 0 and j == 0 else None)
            for t in range(16):
                pe_wide_half(pe, p_vr, t // 4, t % 4)
                if t:
                    pe_v_tile(pe, p_vr, t - 1)
            pe_v_tile(pe, p_vr, 15)
            pe_enter(pe, p_gr)
            pe.wait_ge(rr_done, 2 * RH)
            pe.wait_ge(rr_pool, 6 * RH)
            pe.wait_ge(vr_out, 16)
            pe.wait_ge(vrs_out, 16)
            pe_ret_a(pe, 0)
            for h in range(RH):
                pe_wide_half(pe, p_gr, h, 0)
                pe_ret_o(pe, h)
                pe_wide_half(pe, p_gr, h, 1)
                pe_ret_state(pe, h)
                pe_wide_half(pe, p_gr, h, 2)
                pe_ret_sum(pe, h)
                pe_wide_half(pe, p_gr, h, 3)
                if h + 1 < RH:
                    pe_ret_a(pe, h + 1)
            pe_enter(pe, p_qk)
            pe.wait_ge(orms_done, RH)
            pe.wait_ge(adec_done, 2 * RH)
            pe.wait_ge(snew_out, 2 * RH)
            pe.wait_ge(vr_lo, 1)

            def qk_quad(qq, it=0):
                for j in range(4):
                    t = 4 * qq + j
                    pe_wide_half(pe, p_qk, qq, j, it)
                    if t:
                        pe_qk_ms(pe, t - 1, it)
                    pe_state_v(pe, qq, j, it)
                    if t:
                        pe_qk_rot(pe, p_qk, t - 1, it)
                    if t >= 5:
                        pe_qk_spread(pe, t - 5, it)
                    if j == 0 and qq:
                        pe.wait_ge(qk_rms_done, qq + it)
                    if t:
                        pe_state_o(pe, qq if j else qq - 1, (j - 1) % 4, it)

            qk_quad(0)
            qk_quad(1)
            with pe.Fori(0, p_qk.quads - 2) as it:
                qk_quad(2, it)
            pe_enter(pe, p_v)
            for t in range(AT):
                pe_wide_half(pe, p_v, t // 4, t % 4)
                s = RH * NSTATE_LOOP + t
                if t == 0:
                    pe_qk_ms(pe, 2 * AT - 1)
                if s < B * RH:
                    pe_state_v(pe, s // 4, s % 4)
                if t == 0:
                    pe_qk_rot(pe, p_qk, 2 * AT - 1)
                for i in QK_LAST.get(t, ()):
                    pe_qk_spread(pe, i)
                if t == 0:
                    pe.wait_ge(qk_rms_done, p_qk.quads)
                if s <= B * RH:
                    pe_state_o(pe, (s - 1) // 4, (s - 1) % 4)
                for i in V_TURNED.get(t, ()):
                    if i == 0:
                        pe.wait_ge(qk_sin, 2 * AT)
                        pe.wait_ge(qk_done, 2 * AT)
                    if i == AT - 2:
                        pe.wait_ge(small_act, 2)
                    pe_v_tile(pe, p_v, i)
                if t == SMALL_AT + 1:
                    pe.wait_ge(small_step, 1)
                    pe.wait_ge(v_out_sem, AT - 3)
                    pe.wait_ge(vs_out, AT - 3)
                    nc.tensor.matmul(bank4[:, 0:RH * B], ones, os_sum[:].rearrange("p h b -> p (h b)"), start=True,
                                     stop=True).then_inc(small_pe, 1)
                if t >= QKS_AT:
                    for n in range(2 * (t - QKS_AT), 2 * (t - QKS_AT) + 2):
                        if n == 0:
                            pe.wait_ge(os_out, B * RH)
                        if n >= 2:
                            pe.wait_ge(qks_out, n - 1)
                            pe.wait_ge(qs_lo, min(3, n - 1))
                        for i in range(4):
                            last = nc.tensor.transpose(aux67[0:B, n % 2, i * P:(i + 1) * P], qk[:, 4 * n + i, S:T], ident)
                        last.then_inc(qks_psum, 1)
            for t in range(KD):
                pe_wide_half(pe, p_gb, t // 4, t % 4)
                if t == 0:
                    pe_v_tile(pe, p_v, AT - 1)
                    pe.wait_ge(qks_out, 6)
                    pe.wait_ge(qs_lo, 3)
                for i in range(3 * t, 3 * t + 3):
                    pe_dec_q(pe, i)
            pe.wait_ge(qks_out, 6)
            pe_enter(pe, p_pb)
            pe.wait_ge(ob_split, RH)

            def pb_half(i, midway=None):
                m = i // 2
                pe_wait_half(pe, p_pb.q0 + i // 4, i % 4)
                if i % 2 == 0:
                    pe_wait_acc(pe, p_pb, m, 4)
                for t in range(8):
                    if t == 5 and midway:
                        midway()
                    k = 8 * (i % 2) + t
                    last = three_passes(acc[m % 4][:, 0:T], i % 4, t, obh[:, k], obl[:, k], k == 0, k == 15)
                last.then_inc(pe_half, 1)

            pb_half(0)
            pe_dec_scores(pe)
            pb_half(1)
            pb_half(2)
            pe_dec_turn(pe)
            pb_half(3)
            pe_dec_own(pe)
            for i in range(4, 8):
                for v in range(6 * (i - 4), 6 * (i - 4) + 6):
                    pe_dec_v(pe, v)
                pb_half(i)
            pe.wait_ge(dec_dve, DEC_DVE)

            def att(i):
                if i >= 1:
                    pe_turn(pe, i - 1)
                if i < 16:
                    pe_scores(pe, i)

            for i in range(8):
                att(i)
                pb_half(8 + i, (lambda n=i - 1: pe_pv(pe, n)) if i else None)
            pe_enter(pe, p_ga)
            for t in range(KD):
                att(8 + t)
                pe_wide_half(pe, p_ga, t // 4, t % 4, midway=lambda n=7 + t: pe_pv(pe, n))
            att(16)
            pe_pv(pe, 15)
            pe_enter(pe, p_pa)
            pe.wait_ge(oa_split, 1)
            for j in range(4):
                pe_wait_half(pe, p_pa.q0, j)
                for m in (2 * j, 2 * j + 1):
                    pe_wait_acc(pe, p_pa, m, 4)
                    for k in range(4):
                        last = three_passes(acc[m % 4][:, 0:T], j, 4 * (m % 2) + k, oah[:, k], oal[:, k],
                                            k == 0, k == 3)
                last.then_inc(pe_half, 1)
            for m in range(KD):
                pe_wide_half(pe, p_wo, m // 4, m % 4, 0, (merge_split, 0) if m == 0 else None)
            pe_norm(pe, 2)
            ffn(fi2, fo2, 2)


def tiles_of(w, order):
    return [w[k * P:(k + 1) * P, cols] for k, cols in order]


def unit_array(w, orders):
    return np.stack([np.concatenate(tiles_of(w, order), axis=1) for order in orders])


def weight_units(i):
    def cols(a, step=1):
        return slice(a, a + P * step, step)

    def wide(w, starts, kt=KD):
        return unit_array(w, [[(k, c) for c in starts[n:n + 2] for k in range(kt)] for n in range(0, len(starts), 2)])

    def ffn_in(w):
        return wide(w, [cols(o + t * P) for t in range(FT) for o in (0, DFF)])

    def ffn_out(w):
        return unit_array(w, [[(k, cols(m * P)) for k in range(h * 11, h * 11 + 11)] for m in range(KD) for h in range(2)])

    w = i["w_in"][0]
    at = np.cumsum([0, G * AW, G * AW, G * AW, RH * RQ, RH * RQ, RH * RV, RH * RV, D, D])
    qa, ka, va, qr, kr, vr, gr, ga, gb = (int(a) for a in at[:9])

    def run(start, n):
        return [cols(start + t * P) for t in range(n)]

    def halves(start):
        return [cols(start + h * RQ + p, 2) for h in range(RH) for p in range(2)]

    pb = unit_array(i["w_pb"][0], [[(k, cols(m * P)) for k in range(16)] for m in range(KD)])
    pa = unit_array(i["w_pa"][0], [[(k, cols(m * P)) for m in range(n, n + 4) for k in range(4)] for n in (0, 4)])
    w16 = np.concatenate([
        ffn_in(i["ffn1_in"][0]), wide(w, halves(qr)), wide(w, halves(kr)), wide(w, run(vr, 16)), wide(w, run(gr, 16)),
        wide(w, run(qa, AT) + run(ka, AT)), wide(w, run(va, AT)), wide(w, run(gb, KD)), pb, wide(w, run(ga, KD)), pa,
        wide(i["w_o"][0], run(0, KD)), ffn_in(i["ffn2_in"][0])])
    w11 = np.concatenate([ffn_out(i["ffn1_out"][0]), ffn_out(i["ffn2_out"][0])])
    return w16, w11


def kernel(**inputs):
    import concourse.bacc as bacc
    from concourse.bass_utils import run_bass_kernel_spmd

    i = {k: np.asarray(v) for k, v in inputs.items()}
    tokens = np.concatenate([i["x_prompt"][0], i["x_sample"][:, 0]])
    xT = np.ascontiguousarray(tokens.T.reshape(KD, P, T).transpose(1, 0, 2))
    norms = [i[n][0].reshape(KD, P).T for n in ("ffn1_norm", "mix_norm", "ffn2_norm")]
    heads = [np.tile(i[n][0], 2)[:, None] for n in ("a_q_norm", "a_k_norm")]
    w16, w11 = weight_units(i)
    caches = [i[f"cache_kv_a{g}"][0].reshape(B, -1, 2 * AW) for g in range(G)]
    arrays = {"xT": xT, "tables": build_tables(), "gains": np.ascontiguousarray(np.concatenate(norms + heads, axis=1)),
              "w16": w16, "w11": w11, "cache0": caches[0], "cache1": caches[1], "cache2": caches[2],
              "state_in": i["state_ret"][0]}
    outs = {"yT": (P, KD, T), "kT_out": (P, AT, T), "v_out": (S, G * AW), "ret_out": (RH, RQ, RV),
            "kv0_out": caches[0].shape, "kv1_out": caches[1].shape, "kv2_out": caches[2].shape,
            "state_out": (B, RH, RQ, RV)}
    nc = bacc.Bacc("TRN2", target_bir_lowering=False, num_devices=1)
    args = [nc.dram_tensor(n, a.shape, mybir.dt.from_np(a.dtype), kind="ExternalInput").ap() for n, a in arrays.items()]
    args += [nc.dram_tensor(n, s, F32, kind="ExternalOutput").ap() for n, s in outs.items()]
    trunk_step(nc, *args)
    r = run_bass_kernel_spmd(nc, [arrays], core_ids=[0]).results[0]

    y = r["yT"].transpose(2, 1, 0).reshape(T, D)
    k = r["kT_out"].transpose(2, 1, 0).reshape(T, G, AH, AE)[:S]
    v = r["v_out"].reshape(S, G, AH, AE)
    prompt = []
    for g, (window, _) in enumerate(GROUPS):
        keep = min(window, S)
        prompt.append(np.stack([k[S - keep:, g], v[S - keep:, g]], axis=1)[None, None])
    sample = [r[f"kv{g}_out"].reshape(i[f"cache_kv_a{g}"].shape) for g in range(G)]
    return (y[None, :S], y[S:, None], *prompt, r["ret_out"][None, None], *sample, r["state_out"][None])
```

```python
from contextlib import ExitStack

import numpy as np

import concourse.bass as bass
from concourse import mybir

F32 = mybir.dt.float32
F32R = mybir.dt.float32r
ALU = mybir.AluOpType
ACT = mybir.ActivationFunctionType
AX = mybir.AxisListType

P = 128
D = 1024
KD = D // P
S = 256
B = 8
T = S + B
PAST = 2048
DFF = ((8 * D // 3 + P - 1) // P) * P
FT = DFF // P
GROUPS = ((128, 1), (512, 4), (2048, 16))
G = len(GROUPS)
AH, AE = 8, 64
AW = AH * AE
AT = G * AW // P
RH, RQ, RV = 4, 256, 512
EPS = 1e-6
NEG = -1e30
SCALE = AE ** -0.5
PICK = 32 + B

PHASES = [
    ("fi", 11, 4, "dve"), ("fo", 8, 1, "dve"), ("qr", 2, 4, "act"), ("kr", 2, 4, "act"), ("vr", 4, 4, "act"),
    ("gr", 4, 4, "dve"), ("qk", 6, 4, "act"), ("v", 3, 4, "act"), ("gb", 2, 4, "act"), ("pb", 4, 2, "dve"),
    ("ga", 2, 4, "act"), ("pa", 1, 8, "dve"), ("wo", 2, 4, "dve"), ("fi", 11, 4, "dve"), ("fo", 8, 1, "dve"),
]
FO_HALVES = (6, 5, 6, 5)


def moving(it):
    return not isinstance(it, int)


class Phase:

    def __init__(self, index):
        self.kind, self.quads, self.per_quad, self.owner = PHASES[index]
        self.q0 = sum(p[1] for p in PHASES[:index])
        self.out0 = sum(p[1] * p[2] for p in PHASES[:index] if p[3] == self.owner)
        self.previous = PHASES[index - 1][3] if index else self.owner
        self.previous_out = sum(p[1] * p[2] for p in PHASES[:index] if p[3] == self.previous)


QUADS = sum(p[1] for p in PHASES)
KIND_OF = [p[0] for p in PHASES for _ in range(p[1])]


def half_tiles(q, j):
    return FO_HALVES[j] if KIND_OF[q] == "fo" else 8


def half_offset(q, j):
    return (0 if j % 2 == 0 else half_tiles(q, j - 1)) * P


TABLES = {}
_at = 0
for _name, _n in (("eps", 1), ("ones", P), ("cos_a", T), ("sin_a", T), ("cos_r", T), ("sin_r", T),
                  ("decay", RH * 2 * P), ("mask", G * 2 * P), ("ident", P), ("blocks", P), ("turn", P), ("spread", P), ("kdec", RH * 2), ("gamma", RH),
                  ("rsel", B), ("pick", B), ("own_head", AH), ("own_seq", B)):
    TABLES[_name] = (_at, _at + _n)
    _at += _n
NTAB = _at
EARLY = TABLES["ones"][1]
NGAIN = 3 * KD + 2


def build_tables():
    tab = np.zeros((P, NTAB), np.float32)

    def put(name, value):
        a, b = TABLES[name]
        value = np.asarray(value, np.float32)
        tab[:value.shape[0], a:b] = value.reshape(value.shape[0], b - a)

    pos = np.concatenate([np.arange(S), np.full(B, PAST)]).astype(np.float32)
    half = AE // 8
    inv = (np.float32(500000.0) ** (-np.arange(half, dtype=np.float32) / np.float32(half))).astype(np.float32)
    ang = (pos[None, :] * inv[:, None]).astype(np.float32).astype(np.float64)
    cos_a, sin_a = np.ones((P, T)), np.zeros((P, T))
    turn = np.zeros((P, P))
    for base in (0, AE):
        for r in range(2):
            cos_a[base + r * half:base + (r + 1) * half] = np.cos(ang)
            sin_a[base + r * half:base + (r + 1) * half] = np.sin(ang)
        for i in range(half):
            turn[base + half + i, base + i] = -1.0
            turn[base + i, base + half + i] = 1.0
    put("cos_a", cos_a)
    put("sin_a", sin_a)
    put("turn", turn)
    put("spread", np.arange(P)[:, None] % 32 == 16 * (np.arange(P)[None, :] // AE))
    inv_r = (np.float32(1.0) / np.float32(10000.0) ** np.linspace(0.0, 1.0, P, dtype=np.float32)).astype(np.float32)
    ang_r = (pos[None, :] * inv_r[:, None]).astype(np.float32).astype(np.float64)
    put("cos_r", np.cos(ang_r))
    put("sin_r", np.sin(ang_r))
    mask = np.zeros((P, G, 2, P))
    qi, kj = np.arange(P)[:, None], np.arange(P)[None, :]
    for g, (_, dil) in enumerate(GROUPS):
        for block, dist in ((0, P + qi - kj), (1, qi - kj)):
            ok = (dist >= 0) & (dist % dil == 0) & (dist // dil <= P)
            mask[:, g, block] = np.where(ok, 0.0, NEG)
    put("mask", mask)
    gamma = 1.0 - 2.0 ** (-5.0 - np.arange(RH))
    decay = np.zeros((P, RH, 2, P))
    j, i = np.arange(P)[:, None], np.arange(P)[None, :]
    for h in range(RH):
        decay[:, h, 0] = np.where(i >= j, gamma[h] ** np.maximum(i - j, 0), 0.0)
        decay[:, h, 1] = gamma[h] ** (P + i - j)
    put("decay", decay)
    put("ident", np.eye(P))
    put("ones", np.ones((P, P)))
    put("blocks", np.kron(np.eye(2), np.ones((AE, AE))))
    kdec = np.zeros((P, RH, 2))
    for h in range(RH):
        for c in range(2):
            kdec[:, h, c] = gamma[h] ** (S - 1 - c * P - np.arange(P))
    put("kdec", kdec)
    put("gamma", np.broadcast_to(gamma, (P, RH)))
    put("rsel", (np.arange(64)[:, None] % B == np.arange(B)[None, :]))
    row = np.arange(P)
    head = 2 * (row % 16 // 4) + row % 32 // 16
    put("own_head", (np.arange(AH)[None, :] == head[:, None]) & (row % 4 == row // 32)[:, None])
    put("own_seq", np.arange(B)[None, :] % 4 == row[:, None] // 32)
    put("pick", (np.arange(PICK)[:, None] % 32 == np.arange(B)[None, :]))
    put("eps", np.full((P, 1), EPS))
    return tab


def trunk_step(nc, xT, tables, gains, w16, w11, cache0, cache1, cache2, state_in,
               yT, kT_out, v_out, ret_out, kv0_out, kv1_out, kv2_out, state_out):
    caches, kv_outs = (cache0, cache1, cache2), (kv0_out, kv1_out, kv2_out)

    with ExitStack() as ctx:
        base = 16512
        place = {"at": base}

        def fixed(name, shape, dtype=F32):
            t = nc.alloc_sbuf_tensor_at(name, [P] + shape, dtype, offset=place["at"])
            place["at"] += (int(np.prod(shape)) * 4 + 31) // 32 * 32
            return t

        x = fixed("x", [KD, T])
        hh = fixed("hh", [KD, T], F32R)
        hl = fixed("hl", [KD, T], F32R)
        raw = [fixed(f"raw{i}", [8 * P]) for i in range(4)]
        wh = [fixed(f"wh{i}", [8 * P], F32R) for i in range(4)]
        wl = [fixed(f"wl{i}", [8 * P], F32R) for i in range(4)]
        tab = fixed("tab", [NTAB])
        gain = fixed("gain", [NGAIN])
        square = fixed("square", [2, T])
        square_sum = fixed("square_sum", [T])
        rms = fixed("rms", [T])
        normed = square
        qr_s = fixed("qr_s", [2 * RH, B])
        kr_s = fixed("kr_s", [2 * RH, B])
        o_s = fixed("o_s", [RH * 4, B])
        o_s2 = fixed("o_s2", [RH * 4, B])
        os_sum = fixed("os_sum", [RH, B])
        pick = fixed("pick", [B], F32R)
        picked = fixed("picked", [1], F32R)
        arena = place["at"]

        def at(name, offset, shape, dtype=F32):
            return nc.alloc_sbuf_tensor_at(name, [P] + shape, dtype, offset=arena + offset)

        uh = at("uh", 0, [FT, T], F32R)
        ul = at("ul", 23232, [FT, T], F32R)
        silu = at("silu", 46464, [2, T])
        product = at("product", 48576, [2, T])
        v_ret = at("v_ret", 0, [2, RH * RV])
        vs_ret = at("vs_ret", 16384, [RH * RV])
        ob = at("ob", 24576, [RH * 4, T])
        qr = at("qr", 41472, [2 * RH, T])
        kr = at("kr", 49920, [2 * RH, T])
        pair = at("pair", 58368, [2, 2, T])
        turned = at("turned", 62592, [4, T])
        vT_ret = at("vT_ret", 66816, [2, T])
        sig = at("sig", 68928, [2, T])
        a_dec = at("a_dec", 71040, [3 * P])
        k_dec = at("k_dec", 72576, [2, RQ])
        o_ret = at("o_ret", 74624, [4, S])
        o_sq = at("o_sq", 78720, [4, S])
        o_sum = at("o_sum", 82816, [S])
        o_rms = at("o_rms", 83840, [S])
        s_new = at("s_new", 112256, [2, RV])
        state = at("state", 0, [4, 2 * RV])
        qk = at("qk", 41472, [2 * AT, T])
        v_tok = at("v_tok", 66816, [2, G * AW])
        vk_s = at("vk_s", 79104, [G * AW])
        v_s, k_s = vk_s[0:B, :], vk_s[32:32 + B, :]
        q_hl = at("q_hl", 85248, [G * AW], F32R)
        qk_sq = at("qk_sq", 91392, [2, T])
        qk_rms = at("qk_rms", 93504, [T])
        qk_rinv = at("qk_rinv", 94560, [T])
        rot_s = at("rot_s", 95616, [2, T])
        rot_c = at("rot_c", 97728, [2, T])
        vr_hl = at("vr_hl", 99840, [RH * RV], F32R)
        vT = at("vT", 108032, [4, T])
        obh = at("obh", 0, [RH * 4, T], F32R)
        dec_s = at("dec_s", 16896, [G, 64])
        dec_p = at("dec_p", 17664, [G * P + G])
        dec_pT = at("dec_pT", 19232, [G, 64])
        dec_own = at("dec_own", 20000, [G, 64])
        dec_diag = at("dec_diag", 20768, [G, 64])
        qk_own = at("qk_own", 21536, [AT, B])
        dec_m = at("dec_m", 21920, [4])
        att_m = at("att_m", 21952, [2, 4])
        q_spread = at("q_spread", 21984, [AW])
        probT = at("probT", 16896, [6 * P])
        gate_b = at("gate_b", 24576, [KD, T])
        gate_a = at("gate_a", 33024, [KD, T])
        kv = at("kv", 91392, [4, AW])
        v_own = at("v_own", 85248, [2, AW])
        prob = at("prob", 85248, [2, G, 2 * P])
        obl = at("obl", 99584, [RH * 4, T], F32R)
        oah = at("oah", 99584, [4, T], F32R)
        oal = at("oal", 103808, [4, T], F32R)
        merge_a = at("merge_a", 91392, [2, T])
        merge = at("merge", 93504, [2, T])

        def const(name, rows=P):
            a, b = TABLES[name]
            return tab[0:rows, a:b]

        ident, ones, blocks, turn = const("ident"), const("ones"), const("blocks"), const("turn")
        eps = const("eps")
        oa_at = TABLES["cos_r"][0]
        oa = tab[:, oa_at:oa_at + 4 * T].rearrange("p (n t) -> p n t", n=4)

        acc = [ctx.enter_context(nc.psum_tensor(f"acc{i}", [P, 512], F32)) for i in range(4)]
        aux45 = ctx.enter_context(nc.psum_tensor("aux45", [P, 2, 512], F32))
        aux67 = ctx.enter_context(nc.psum_tensor("aux67", [P, 2, 512], F32))
        bank4, bank5, bank6, bank7 = aux45[:, 0], aux45[:, 1], aux67[:, 0], aux67[:, 1]

        def sem(name):
            return ctx.enter_context(nc.semaphore(name))

        x_in = [sem("x_in0"), sem("x_in1")]
        const_in = sem("const_in")
        tab_in = sem("tab_in")
        raw_in = [sem(f"raw_in{i}") for i in range(4)]
        hi_done, lo_done = sem("hi_done"), sem("lo_done")
        pe_half = sem("pe_half")
        out_of = {"act": sem("acc_out_act"), "dve": sem("acc_out_dve")}
        silu_done, u_split, u_hi = sem("silu_done"), sem("u_split"), sem("u_hi")
        sq_done, sum_done, sum_psum = sem("sq_done"), sem("sum_done"), sem("sum_psum")
        rms_done, rinv_done = sem("rms_done"), sem("rinv_done")
        normed_done, normed_hi = sem("normed_done"), sem("normed_hi")
        normed_lo = [sem("normed_lo_dve"), sem("normed_lo_pool")]
        rr_dve, rr_pool, rr_done = sem("rr_dve"), sem("rr_pool"), sem("rr_done")
        rs_copied = sem("rs_copied")
        vr_turned, vr_out, vrs_out = sem("vr_turned"), sem("vr_out"), sem("vrs_out")
        sig_done = sem("sig_done")
        kt_psum, kdec_done = sem("kt_psum"), sem("kdec_done")
        a_psum, adec_done = sem("a_psum"), sem("adec_done")
        o_psum, o_out, osq_done, osum_done = sem("o_psum"), sem("o_out"), sem("osq_done"), sem("osum_done")
        oms_psum, orms_done, orinv_done, on_done, ob_done = (
            sem("oms_psum"), sem("orms_done"), sem("orinv_done"), sem("on_done"), sem("ob_done"))
        snew_psum, snew_out, ret_stored = sem("snew_psum"), sem("snew_out"), sem("ret_stored")
        cleared, pick_done, picked_done = sem("cleared"), sem("pick_done"), sem("picked_done")
        qk_sq_done, qk_ms_psum, qk_rms_done, qk_rinv_done = (
            sem("qk_sq_done"), sem("qk_ms_psum"), sem("qk_rms_done"), sem("qk_rinv_done"))
        qk_rot_psum, qk_sin, qk_cos, qk_turned, qk_spread, qk_done = (
            sem("qk_rot_psum"), sem("qk_sin"), sem("qk_cos"), sem("qk_turned"), sem("qk_spread"), sem("qk_done"))
        state_in_sem = [sem(f"state_in{i}") for i in range(4)]
        state_stored = [sem(f"state_stored{i}") for i in range(4)]
        vr_hi, vr_lo, vb_psum, state_scaled, state_new = (
            sem("vr_hi"), sem("vr_lo"), sem("vb_psum"), sem("state_scaled"), sem("state_new"))
        os_psum, os_out = sem("os_psum"), sem("os_out")
        v_turned, v_out_sem, vs_out = sem("v_turned"), sem("v_tok_out"), sem("v_s_out")
        qks_psum, qks_out, qs_lo = sem("qks_psum"), sem("qks_out"), sem("qs_lo")
        small_step = sem("small_step")
        small_act = sem("small_act")
        small_pe = sem("small_pe")
        ob_hi, ob_split = sem("ob_hi"), sem("ob_split")
        kv_in = [sem(f"kv_in{i}") for i in range(4)]
        att_step = sem("att_step")
        qb_psum, kq_done = sem("qb_psum"), sem("kq_done")
        q_copied = sem("q_copied")
        kq_mul = [sem("kq_mul_dve"), sem("kq_mul_pool")]
        dec_pe, dec_dve, dec_act, dec_v_done, v_own_done = sem("dec_pe"), sem("dec_dve"), sem("dec_act"), sem("dec_v_done"), sem("v_own_done")
        att_scores, att_masked, att_negmax = sem("att_scores"), sem("att_masked"), sem("att_negmax")
        att_exp, att_prob = sem("att_exp"), sem("att_prob")
        att_turned, att_turned_out = sem("att_turned"), sem("att_turned_out")
        att_pv, att_out = sem("att_pv"), sem("att_out")
        oa_hi, oa_split = sem("oa_hi"), sem("oa_split")
        gate_done, merge_done, merge_hi = sem("gate_done"), sem("merge_done"), sem("merge_hi")
        merge_lo = [sem("merge_lo_pool"), sem("merge_lo_dve")]
        rolled = sem("rolled")
        stored = sem("stored")
        STORES = 1 + 1 + KD + 2 * G

        phases = [Phase(i) for i in range(len(PHASES))]
        unit16 = {}
        for q in range(QUADS):
            for s in range(2):
                n = 2 * q + s
                kind = "11" if KIND_OF[q] == "fo" else "16"
                unit16[n] = (kind, sum(1 for v in unit16.values() if v[0] == kind))

        def load_half(act, q, j, it=0):
            kind, index = unit16[2 * q + j // 2]
            off, n = half_offset(q, j), half_tiles(q, j) * P
            src = (w16 if kind == "16" else w11)[index + 2 * it]
            act.dma_start(raw[j][:, 0:n], src[:, off:off + n]).then_inc(raw_in[j], 16)

        def hi_half(act, q, j, it=0):
            n = half_tiles(q, j) * P
            act.wait_ge(raw_in[j], 16 * (q + 1) + 16 * it)
            if q >= 1:
                act.wait_ge(pe_half, 4 * (q - 1) + j + 1 + 4 * it)
            nc.scalar.activation(wh[j][:, 0:n], raw[j][:, 0:n], ACT.Copy).then_inc(hi_done, 1)

        def lo_half(dve, q, j, it=0):
            n = half_tiles(q, j) * P
            dve.wait_ge(hi_done, 4 * q + j + 1 + 4 * it)
            nc.vector.tensor_tensor(wl[j][:, 0:n], raw[j][:, 0:n], wh[j][:, 0:n].bitcast(F32),
                                    ALU.subtract).then_inc(lo_done, 1)

        def act_ahead(act, q, j, it=0):
            if q + 1 < QUADS:
                hi_half(act, q + 1, j, it)
            n = 4 * (q + 1) + j
            q_next, j_next = (n + 3) // 4, (n + 3) % 4
            if q_next < QUADS:
                act.wait_ge(lo_done, n + 4 * it)
                load_half(act, q_next, j_next, it)

        def dve_ahead(dve, q, j, it=0):
            if q + 1 < QUADS:
                lo_half(dve, q + 1, j, it)

        def three_passes(out, j, t, xh, xl, first, last, skip=False):
            w_hi, w_lo = wh[j][:, t * P:(t + 1) * P], wl[j][:, t * P:(t + 1) * P]
            nc.tensor.matmul(out, w_hi, xh, start=first, stop=False)
            nc.tensor.matmul(out, w_hi, xl, start=False, stop=False)
            return nc.tensor.matmul(out, w_lo, xh, start=False, stop=last)

        def pe_wait_half(pe, q, j, it=0):
            pe.wait_ge(lo_done, 4 * q + j + 1 + 4 * it)

        def pe_wait_acc(pe, ph, local, keep, it=0):
            if local < keep and ph.q0 and ph.previous != ph.owner:
                behind = (2 if KIND_OF[ph.q0 - 1] == "fo" else keep) - 1 - local
                if behind >= 0:
                    pe.wait_ge(out_of[ph.previous], ph.previous_out - behind)
                return
            value = ph.out0 + local - keep + 1
            if value > 0:
                pe.wait_ge(out_of[ph.owner], value + ph.per_quad * it)

        def normed_tile(pe, r):
            return lambda k: pe.wait_ge(normed_lo[k % 2], KD // 2 * r + k // 2 + 1)

        def pe_wide_half(pe, ph, qq, j, it=0, wait_x=None, between=None):
            pe_wait_half(pe, ph.q0 + qq, j, it)
            pe_wait_acc(pe, ph, 4 * qq + j, 4, it)
            for k in range(KD):
                if wait_x is not None:
                    wait_x(k)
                for step in (between or {}).get(k, ()):
                    step()
                last = three_passes(acc[j][:, 0:T], j, k, hh[:, k], hl[:, k], k == 0, k == KD - 1)
            last.then_inc(pe_half, 1)

        def pe_fo_quad(pe, ph, m, bank, it=0):
            r = 0 if ph.q0 < QUADS // 2 else 1
            pe_wait_acc(pe, ph, m, 2, it)
            k = 0
            for j in range(4):
                pe_wait_half(pe, ph.q0 + m, j, it)
                pe.wait_ge(u_split, FT * r + k + FO_HALVES[j])
                for t in range(FO_HALVES[j]):
                    last = three_passes(acc[bank][:, 0:T], j, t, uh[:, k], ul[:, k], k == 0, k == FT - 1)
                    k += 1
                last.then_inc(pe_half, 1)

        def dve_sum_square(dve, r, m, it=0):
            dve.wait_ge(sq_done, KD * r + m + 1 + it)
            if not isinstance(m, int) or m or moving(it):
                dve.wait_ge(sum_done, KD * r + m + it)
            ins = (nc.vector.tensor_copy(square_sum[:], square[:, m % 2]) if m == 0 and not moving(it) else
                   nc.vector.tensor_tensor(square_sum[:], square_sum[:], square[:, m % 2], ALU.add))
            ins.then_inc(sum_done, 1)

        def act_square(act, r, m, it=0):
            if r or m >= 2:
                act.wait_ge(sum_done, KD * r + m - 1 + it)
            nc.scalar.activation(square[:, m % 2], x[:, bass.ds(m + it, 1)].squeeze(1) if moving(it) else x[:, m],
                                 ACT.Square).then_inc(sq_done, 1)

        def pe_norm(pe, r):
            pe.wait_ge(sum_done, KD * (r + 1))
            nc.tensor.matmul(bank4[:, 0:T], ones, square_sum[:], start=True, stop=True).then_inc(sum_psum, 1)

        def act_norm(act, r):
            act.wait_ge(sum_psum, r + 1)
            nc.scalar.activation(rms[:], bank4[:, 0:T], ACT.Sqrt, bias=eps, scale=1.0 / D).then_inc(rms_done, 1)
            for k in range(KD):
                act.wait_ge(normed_done, KD * r + k + 1)
                nc.scalar.activation(hh[:, k], normed[:, k % 2], ACT.Copy).then_inc(normed_hi, 1)

        def dve_norm(dve, r):
            dve.wait_ge(rms_done, r + 1)
            nc.vector.reciprocal(rms[:], rms[:]).then_inc(rinv_done, 1)
            dve.wait_ge(rinv_done, r + 1)

            def low_part(k):
                dve.wait_ge(normed_hi, KD * r + k + 1)
                nc.vector.tensor_tensor(hl[:, k], normed[:, k % 2], hh[:, k].bitcast(F32),
                                        ALU.subtract).then_inc(normed_lo[0], 1)

            for k in range(KD):
                if k >= 2:
                    dve.wait_ge(normed_lo[k % 2], KD // 2 * r + k // 2)
                nc.vector.scalar_tensor_tensor(normed[:, k % 2], x[:, k], gain[:, r * KD + k:r * KD + k + 1],
                                               rms[:], ALU.mult, ALU.mult).then_inc(normed_done, 1)
                if k % 2:
                    low_part(k - 1)

        def pool_norm(pool, r):
            for k in range(1, KD, 2):
                pool.wait_ge(normed_hi, KD * r + k + 1)
                nc.gpsimd.tensor_tensor(hl[:, k], normed[:, k % 2], hh[:, k].bitcast(F32),
                                        ALU.subtract).then_inc(normed_lo[1], 1)

        def act_fi_quad(act, ph, qq, it=0):
            q = ph.q0 + qq
            r = 0 if ph.q0 < QUADS // 2 else 1
            for j in range(4):
                if j % 2 == 0:
                    i = FT * r + 2 * qq + j // 2
                    act.wait_ge(pe_half, 4 * q + j + 1 + 4 * it)
                    if i >= 2:
                        act.wait_ge(out_of["dve"], ph.out0 + 2 * (2 * qq + j // 2) - 2 + 4 * it)
                    nc.scalar.activation(silu[:, j // 2], acc[j][:, 0:T], ACT.Silu).then_inc(silu_done, 1)
                act_ahead(act, q, j, it)

        def dve_fi_quad(dve, ph, qq, it=0):
            q = ph.q0 + qq
            r = 0 if ph.q0 < QUADS // 2 else 1
            for j in range(4):
                if j % 2 == 1:
                    i = FT * r + 2 * qq + j // 2
                    dve.wait_ge(pe_half, 4 * q + j + 1 + 4 * it)
                    dve.wait_ge(silu_done, i + 1 + 2 * it)
                    if i >= 2:
                        dve.wait_ge(u_split, i - 1 + 2 * it)
                    nc.vector.tensor_tensor(product[:, j // 2], silu[:, j // 2], acc[j][:, 0:T],
                                            ALU.mult).then_inc(out_of["dve"], 2)
                dve_ahead(dve, q, j, it)

        def pool_fi_quad(pool, ph, qq, it=0):
            r = 0 if ph.q0 < QUADS // 2 else 1
            for s in range(2):
                i = 2 * qq + s
                pool.wait_ge(out_of["dve"], ph.out0 + 2 * i + 2 + 4 * it)
                if not moving(it):
                    hi, lo = uh[:, i], ul[:, i]
                else:
                    hi, lo = (u[:, bass.ds(i + 2 * it, 1)].squeeze(1) for u in (uh, ul))
                nc.gpsimd.tensor_copy(hi, product[:, s]).then_inc(u_hi, 1)
                pool.wait_ge(u_hi, FT * r + i + 1 + 2 * it)
                nc.gpsimd.tensor_tensor(lo, product[:, s], hi.bitcast(F32), ALU.subtract).then_inc(u_split, 1)

        def act_fo_quad(act, ph, m, it=0, norm=None):
            for j in range(4):
                if j == (2 if m == KD - 1 else 3) and norm is not None:
                    act.wait_ge(out_of["dve"], ph.out0 + m + 1 + it)
                    act_square(act, norm, m, it)
                    if m == KD - 1:
                        act_norm(act, norm)
                act_ahead(act, ph.q0 + m, j, it)

        def dve_add_x(dve, ph, m, factor, bank, it=0):
            xm = x[:, m] if not moving(it) else x[:, bass.ds(m + it, 1)].squeeze(1)
            nc.vector.scalar_tensor_tensor(xm, acc[bank][:, 0:T], factor, xm, ALU.mult,
                                           ALU.add).then_inc(out_of["dve"], 1)

        def dve_fo_quad(dve, ph, m, it=0, norm=None):
            for j in range(4):
                if j == (2 if m == KD - 1 and norm is not None else 3):
                    dve.wait_ge(pe_half, 4 * (ph.q0 + m) + 4 + 4 * it)
                    dve_add_x(dve, ph, m, 0.5, m % 2, it)
                    if norm is not None:
                        dve_sum_square(dve, norm, m, it)
                        if m == KD - 1:
                            dve_norm(dve, norm)
                dve_ahead(dve, ph.q0 + m, j, it)

        RR = [("qr", qr), ("kr", kr)]

        def act_rr_quad(act, ph, qq, which):
            for j in range(4):
                act_ahead(act, ph.q0 + qq, j)
                head = 2 * qq + j // 2
                act.wait_ge(pe_half, 4 * (ph.q0 + qq) + j + 1)
                n = RH * which + head
                if n >= 2:
                    act.wait_ge(rr_done, n - 1)
                    act.wait_ge(rr_pool, 3 * n - 3)
                nc.scalar.activation(pair[:, head % 2, j % 2], acc[j][:, 0:T], ACT.Copy,
                                     scale=1.0 if which == 0 else RQ ** -0.5).then_inc(out_of["act"], 1)

        def turn_head(eng, ops, ph, head, which):
            n = RH * which + head
            dst = RR[which][1]
            eng.wait_ge(out_of["act"], ph.out0 + 2 * head + 2)
            cos, sin = const("cos_r"), const("sin_r")
            if ops is nc.vector:
                step, p, q_, out, t0, op = rr_dve, 0, 1, 2 * head, 0, ALU.subtract
            else:
                step, p, q_, out, t0, op = rr_pool, 1, 0, 2 * head + 1, 2, ALU.add
            if n:
                if ops is nc.vector:
                    eng.wait_ge(rr_done, n)
                else:
                    eng.wait_ge(rr_pool, 3 * n)
            ops.tensor_tensor(turned[:, t0], pair[:, head % 2, p], cos, ALU.mult).then_inc(step, 1)
            ops.tensor_tensor(turned[:, t0 + 1], pair[:, head % 2, q_], sin, ALU.mult).then_inc(step, 1)
            if ops is nc.vector:
                eng.wait_ge(rr_dve, 2 * n + 2)
                ops.tensor_tensor(dst[:, out], turned[:, t0], turned[:, t0 + 1], op).then_inc(rr_done, 1)
            else:
                eng.wait_ge(rr_pool, 3 * n + 2)
                ops.tensor_tensor(dst[:, out], turned[:, t0], turned[:, t0 + 1], op).then_inc(rr_pool, 1)

        VKIND = {"vr": (vT_ret, 2, v_ret, vs_ret, vr_turned, vr_out, vrs_out),
                 "v": (vT, 4, v_tok, v_s, v_turned, v_out_sem, vs_out)}

        def act_v_tile(act, ph, t):
            src, ring, _, _, turned_sem, _, _ = VKIND[ph.kind]
            act.wait_ge(pe_half, 4 * ph.q0 + t + 1)
            if t >= ring:
                act.wait_ge(turned_sem, t - ring + 1)
            nc.scalar.activation(src[:, t % ring], acc[t % 4][:, 0:T], ACT.Copy).then_inc(out_of["act"], 1)

        def act_v_small(act, ph, t):
            _, _, _, small, _, big_out, small_out = VKIND[ph.kind]
            act.wait_ge(big_out, t + 1)
            nc.scalar.activation(small[0:B, t * P:(t + 1) * P], aux45[0:B, t % 2, 256:256 + P],
                                 ACT.Copy).then_inc(small_out, 1)

        def dve_v_tile(dve, ph, t):
            _, _, big, _, turned_sem, big_out, _ = VKIND[ph.kind]
            dve.wait_ge(turned_sem, t + 1)
            nc.vector.tensor_copy(big[:, :, t * P:(t + 1) * P],
                                  aux45[:, t % 2, 0:256].rearrange("p (c f) -> p c f", c=2)).then_inc(big_out, 1)

        def pe_v_tile(pe, ph, t):
            src, ring, _, _, turned_sem, big_out, small_out = VKIND[ph.kind]
            pe.wait_ge(out_of["act"], ph.out0 + t + 1)
            if t >= 2:
                pe.wait_ge(big_out, t - 1)
                pe.wait_ge(small_out, t - 1)
            nc.tensor.transpose(aux45[:, t % 2, 0:P], src[:, t % ring, 0:P], ident)
            nc.tensor.transpose(aux45[:, t % 2, P:2 * P], src[:, t % ring, P:S], ident)
            nc.tensor.transpose(aux45[0:B, t % 2, 256:256 + P], src[:, t % ring, S:T], ident).then_inc(turned_sem, 1)

        def decay(h, a, b):
            t0 = TABLES["decay"][0] + h * 2 * P
            return tab[:, t0 + a:t0 + b]

        def pe_ret_a(pe, h):
            if h:
                pe.wait_ge(kdec_done, 2 * h)
                pe.wait_ge(orms_done, h)
                pe.wait_ge(adec_done, 2 * h)
            for c in range(2):
                for p in range(2):
                    last = nc.tensor.transpose(bank5[:, (2 * c + p) * P:(2 * c + p + 1) * P],
                                               kr[:, 2 * h + p, c * P:(c + 1) * P], ident)
            last.then_inc(kt_psum, 1)
            for p in range(2):
                nc.tensor.matmul(bank4[:, 0:S], kr[:, 2 * h + p, 0:P], qr[:, 2 * h + p, 0:S],
                                 start=p == 0, stop=p == 1)
            for p in range(2):
                last = nc.tensor.matmul(bank4[:, S:S + P], kr[:, 2 * h + p, P:S], qr[:, 2 * h + p, P:S],
                                        start=p == 0, stop=p == 1)
            last.then_inc(a_psum, 1)

        def act_ret_k(act, h):
            act.wait_ge(kt_psum, h + 1)
            if h:
                act.wait_ge(snew_psum, h)
            for c in range(2):
                col = TABLES["kdec"][0] + 2 * h + c
                nc.scalar.activation(k_dec[:, c], bank5[:, c * 2 * P:(c + 1) * 2 * P], ACT.Copy,
                                     scale=tab[:, col:col + 1]).then_inc(kdec_done, 1)

        def dve_ret_a(dve, h):
            dve.wait_ge(a_psum, h + 1)
            if h:
                dve.wait_ge(o_psum, h)
            nc.vector.tensor_tensor(a_dec[:, 0:S], bank4[:, 0:S], decay(h, 0, S), ALU.mult).then_inc(adec_done, 1)
            nc.vector.tensor_tensor(a_dec[:, S:S + P], bank4[:, S:S + P], decay(h, 0, P),
                                    ALU.mult).then_inc(adec_done, 1)

        def pe_ret_o(pe, h):
            pe.wait_ge(adec_done, 2 * h + 2)
            if h:
                pe.wait_ge(snew_out, 2 * h)
            for e in range(4):
                out = aux67[:, e // 2, (e % 2) * S:(e % 2 + 1) * S]
                cols = slice(h * RV + e * P, h * RV + (e + 1) * P)
                nc.tensor.matmul(out, v_ret[:, 0, cols], a_dec[:, 0:S], start=True, stop=False)
                last = nc.tensor.matmul(out[:, P:S], v_ret[:, 1, cols], a_dec[:, S:S + P], start=False, stop=True)
            last.then_inc(o_psum, 1)

        def act_ret_o(act, h):
            act.wait_ge(o_psum, h + 1)
            if h:
                act.wait_ge(ob_done, h)
            src = aux67[:].rearrange("p c (e f) -> p (c e) f", e=2)
            nc.scalar.activation(o_ret[:], src, ACT.Copy).then_inc(o_out, 1)
            nc.scalar.activation(o_sq[:], src, ACT.Square).then_inc(osq_done, 1)

        def dve_ret_sum(dve, h):
            dve.wait_ge(osq_done, h + 1)
            if h:
                dve.wait_ge(oms_psum, h)
            nc.vector.tensor_reduce(o_sum[:], o_sq[:].rearrange("p e f -> p f e"), AX.X, ALU.add).then_inc(osum_done, 1)

        def pe_ret_sum(pe, h):
            pe.wait_ge(osum_done, h + 1)
            pe.wait_ge(kdec_done, 2 * h + 2)
            nc.tensor.matmul(bank5[:, 0:S], ones, o_sum[:], start=True, stop=True).then_inc(oms_psum, 1)

        def act_ret_rms(act, h):
            act.wait_ge(oms_psum, h + 1)
            if h:
                act.wait_ge(ob_done, h)
            nc.scalar.activation(o_rms[:], bank5[:, 0:S], ACT.Sqrt, bias=eps, scale=1.0 / RV).then_inc(orms_done, 1)

        def dve_ret_norm(dve, ph, h, part):
            if part == 0:
                dve.wait_ge(orms_done, h + 1)
                nc.vector.reciprocal(o_rms[:], o_rms[:]).then_inc(orinv_done, 1)
            if part == 1:
                dve.wait_ge(orinv_done, h + 1)
                nc.vector.tensor_tensor(o_ret[:], o_ret[:], o_rms[:].unsqueeze(1).to_broadcast([P, 4, S]),
                                        ALU.mult).then_inc(on_done, 1)
            if part == 2:
                dve.wait_ge(on_done, h + 1)
                dve.wait_ge(out_of["dve"], ph.out0 + 4 * h + 4)
                nc.vector.tensor_tensor(ob[:, 4 * h:4 * h + 4, 0:S], ob[:, 4 * h:4 * h + 4, 0:S], o_ret[:],
                                        ALU.mult).then_inc(ob_done, 1)

        def pe_ret_state(pe, h):
            pe.wait_ge(kdec_done, 2 * h + 2)
            pe.wait_ge(osq_done, h + 1)
            for p in range(2):
                for c in range(2):
                    last = nc.tensor.matmul(aux67[:, p], k_dec[:, c, p * P:(p + 1) * P],
                                            v_ret[:, c, h * RV:(h + 1) * RV], start=c == 0, stop=c == 1)
            last.then_inc(snew_psum, 1)

        def act_ret_state(act, h):
            act.wait_ge(snew_psum, h + 1)
            if h:
                act.wait_ge(ret_stored, 16 * h)
            for p in range(2):
                nc.scalar.activation(s_new[:, p], aux67[:, p], ACT.Copy).then_inc(snew_out, 1)

        def act_gr_tile(act, ph, t):
            act.wait_ge(pe_half, 4 * ph.q0 + t + 1)
            if t >= 2:
                act.wait_ge(out_of["dve"], ph.out0 + t - 1)
            nc.scalar.activation(sig[:, t % 2], acc[t % 4][:, 0:T], ACT.Sigmoid).then_inc(sig_done, 1)

        def dve_gr_tile(dve, ph, t):
            dve.wait_ge(sig_done, t + 1)
            nc.vector.tensor_tensor(ob[:, t], sig[:, t % 2], acc[t % 4][:, 0:T], ALU.mult).then_inc(out_of["dve"], 1)

        def qk_tile(t, it):
            return qk[:, t] if not moving(it) else qk[:, bass.ds(t + 4 * it, 1)].squeeze(1)

        def act_qk_evac(act, ph, qq, j, it=0):
            t = 4 * qq + j
            act.wait_ge(pe_half, 4 * ph.q0 + t + 1 + 4 * it)
            if t >= 2:
                act.wait_ge(qk_ms_psum, t - 1 + 4 * it)
            nc.scalar.activation(qk_sq[:, j % 2], acc[j][:, 0:T], ACT.Square).then_inc(qk_sq_done, 1)
            col = 3 * KD + (0 if t < AT else 1)
            nc.scalar.activation(qk_tile(t, it), acc[j][:, 0:T], ACT.Copy,
                                 scale=gain[:, col:col + 1]).then_inc(out_of["act"], 1)

        def pe_qk_ms(pe, t, it=0):
            pe.wait_ge(qk_sq_done, t + 1 + 4 * it)
            if t >= 4 and t % 4 == 0:
                pe.wait_ge(qk_rms_done, t // 4 + it)
            if t < B * RH:
                pe.wait_ge(os_out, t + 1 + 4 * it)
            j = t % 4
            nc.tensor.matmul(bank7[32 * j:32 * j + 32, 128:128 + T],
                             blocks[:, 0:P:4], qk_sq[:, t % 2],
                             start=True, stop=True).then_inc(qk_ms_psum, 1)

        def act_qk_rms(act, quad, it=0):
            act.wait_ge(qk_ms_psum, 4 * quad + 4 + 4 * it)
            if quad:
                act.wait_ge(qk_rinv_done, quad + it)
            nc.scalar.activation(qk_rms[:], bank7[:, 128:128 + T], ACT.Sqrt, bias=eps,
                                 scale=1.0 / AE).then_inc(qk_rms_done, 1)

        def dve_qk_rinv(dve, quad, it=0):
            dve.wait_ge(qk_rms_done, quad + 1 + it)
            if quad:
                dve.wait_ge(qk_spread, 4 * quad + 4 * it)
            nc.vector.reciprocal(qk_rinv[:], qk_rms[:]).then_inc(qk_rinv_done, 1)

        def pe_qk_rot(pe, ph, t, it=0):
            pe.wait_ge(out_of["act"], ph.out0 + t + 1 + 4 * it)
            if t:
                pe.wait_ge(qk_sin, t + 4 * it)
            nc.tensor.matmul(bank4[:, 0:T], turn, qk_tile(t, it), start=True, stop=True).then_inc(qk_rot_psum, 1)

        def pool_qk_rot(pool, ph, t):
            pool.wait_ge(out_of["act"], ph.out0 + t + 1)
            nc.gpsimd.tensor_tensor(rot_c[:, t % 2], qk[:, t], const("cos_a"), ALU.mult).then_inc(qk_cos, 1)
            pool.wait_ge(qk_sin, t + 1)
            pool.wait_ge(qk_cos, t + 1)
            nc.gpsimd.tensor_tensor(qk[:, t], rot_c[:, t % 2], rot_s[:, t % 2], ALU.add).then_inc(qk_turned, 1)

        def dve_qk_sin(dve, t, it=0):
            dve.wait_ge(qk_rot_psum, t + 1 + 4 * it)
            if t >= 2:
                dve.wait_ge(qk_turned, t - 1 + 4 * it)
            nc.vector.tensor_tensor(rot_s[:, t % 2], bank4[:, 0:T], const("sin_a"), ALU.mult).then_inc(qk_sin, 1)

        def pe_qk_spread(pe, t, it=0):
            pe.wait_ge(qk_rinv_done, t // 4 + 1 + it)
            if t:
                pe.wait_ge(qk_done, t + 4 * it)
            j = t % 4
            rows = slice(32 * j, 32 * j + 32)
            nc.tensor.matmul(bank5[:, 0:T], const("spread")[rows], qk_rinv[rows], start=True, stop=True).then_inc(qk_spread, 1)

        def dve_qk_norm(dve, t, it=0):
            dve.wait_ge(qk_spread, t + 1 + 4 * it)
            dve.wait_ge(qk_turned, t + 1 + 4 * it)
            nc.vector.tensor_tensor(qk_tile(t, it), qk_tile(t, it), bank5[:, 0:T], ALU.mult).then_inc(qk_done, 1)

        def sp_state_load(sp, b, h, it=0):
            src = state_in[bass.ds(b + it, 1), h].squeeze(0) if moving(it) else state_in[b + it, h]
            src = src.rearrange("(p r) e -> p (r e)", r=2)
            if b:
                sp.wait_ge(state_stored[h], 16 * b + 16 * it)
            sp.dma_start(state[:, h], src).then_inc(state_in_sem[h], 16)

        def sp_state_store(sp, b, h, it=0):
            sp.wait_ge(os_psum, 4 * b + h + 1 + 4 * it)
            dst = state_out[b + it, h] if not moving(it) else state_out[bass.ds(b + it, 1), h].squeeze(0)
            sp.dma_start(dst.rearrange("(p r) e -> p (r e)", r=2), state[:, h]).then_inc(state_stored[h], 16)

        def act_pick(act, b, it=0):
            if b:
                act.wait_ge(vb_psum, RH * b + RH * it)
            nc.scalar.activation(picked[0:PICK], pick[0:PICK, bass.ds(b + it, 1)] if moving(it) else
                                 pick[0:PICK, b:b + 1], ACT.Copy).then_inc(picked_done, 1)

        def pe_state_v(pe, b, h, it=0):
            s = 4 * b + h
            pe.wait_ge(picked_done, b + 1 + it)
            if s:
                pe.wait_ge(state_new, 2 * s + 8 * it)
            nc.tensor.matmul(bank6[:, :], picked[0:PICK, 0:1].to_broadcast([PICK, P]),
                             vr_hl[0:PICK, h * RV:(h + 1) * RV], start=True, stop=True).then_inc(vb_psum, 1)

        def act_state(act, b, h, it=0):
            act.wait_ge(state_in_sem[h], 16 * (b + 1) + 16 * it)
            g0 = TABLES["gamma"][0] + h
            nc.scalar.activation(state[:, h], state[:, h], ACT.Copy, scale=tab[:, g0:g0 + 1]).then_inc(state_scaled, 1)

        def dve_state(dve, b, h, it=0):
            s = 4 * b + h
            dve.wait_ge(state_scaled, s + 1 + 4 * it)
            dve.wait_ge(vb_psum, s + 1 + 4 * it)
            for p in range(2):
                half = state[:, h, p * RV:(p + 1) * RV]
                nc.vector.scalar_tensor_tensor(half, bank6[:, :], kr_s[:, 2 * h + p, bass.ds(b + it, 1)] if moving(it) else kr_s[:, 2 * h + p, b:b + 1], half,
                                               ALU.mult, ALU.add).then_inc(state_new, 1)

        def pe_state_o(pe, b, h, it, e):
            s = 4 * b + h
            if e == 0:
                pe.wait_ge(state_new, 2 * s + 2 + 8 * it)
                if s:
                    pe.wait_ge(os_out, s + 4 * it)
            c = 32 * (h % 2) + B * e
            for p in range(2):
                last = nc.tensor.matmul(bank7[:, c:c + B], state[:, h, p * RV + e * P:p * RV + (e + 1) * P],
                                        qr_s[:, 2 * h + p], start=p == 0, stop=p == 1)
            if e == 3:
                last.then_inc(os_psum, 1)

        def act_state_o(act, b, h, it=0):
            s = 4 * b + h
            act.wait_ge(os_psum, s + 1 + 4 * it)
            own = bank7[:, 32 * (h % 2):32 * (h % 2) + 32].rearrange("p (e b) -> p e b", e=4)
            if moving(it):
                src, dst = (v[:, :, bass.ds(b + it, 1)].squeeze(2) for v in (own, o_s[:, 4 * h:4 * h + 4]))
            else:
                src, dst = own[:, :, b], o_s[:, 4 * h:4 * h + 4, b]
            nc.scalar.activation(dst, src, ACT.Copy).then_inc(os_out, 1)

        def pe_samples_rows(pe, n):
            if n >= 2:
                pe.wait_ge(qks_out, n - 1)
                pe.wait_ge(qs_lo, min(G, n - 1))
            for i in range(4):
                last = nc.tensor.transpose(aux67[0:B, n % 2, i * P:(i + 1) * P], qk[:, 4 * n + i, S:T], ident)
            last.then_inc(qks_psum, 1)

        def act_samples_rows(act, n):
            act.wait_ge(qks_psum, n + 1)
            dst = (q_hl[0:B, :] if n < G else k_s)[:, (n % G) * AW:(n % G + 1) * AW]
            nc.scalar.activation(dst, aux67[0:B, n % 2], ACT.Copy).then_inc(qks_out, 1)

        def dve_samples_low(dve, n):
            dve.wait_ge(qks_out, n + 1)
            cols = slice(n * AW, (n + 1) * AW)
            nc.vector.tensor_tensor(q_hl[32:PICK, cols], aux67[0:B, n % 2], q_hl[0:B, cols].bitcast(F32),
                                    ALU.subtract).then_inc(qs_lo, 1)

        def pe_scores(pe, i):
            h, qb = i // 2, i % 2
            if i:
                pe.wait_ge(att_masked, i)
            rows = slice((h % 2) * AE, (h % 2 + 1) * AE)
            keys = (qb + 1) * P
            for g in range(G):
                t = g * 4 + h // 2
                last = nc.tensor.matmul(aux45[:, g // 2, (g % 2) * S + (S - keys if qb == 0 else 0):
                                              (g % 2) * S + S],
                                        qk[rows, t, qb * P:(qb + 1) * P], qk[rows, AT + t, 0:keys],
                                        start=True, stop=True)
            last.then_inc(att_scores, 1)

        def att_view(t, qb):
            return t[:, :, P:2 * P] if qb == 0 else t

        def dve_scores(dve, i):
            qb, two = i % 2, i % 2
            dve.wait_ge(att_scores, i + 1)
            if i >= 2:
                dve.wait_ge(att_turned, i - 1)
            scores = aux45[:].rearrange("p c f -> p (c f)")[:, 0:G * S].rearrange("p (g k) -> p g k", g=G)
            mask = const("mask").rearrange("p (g k) -> p g k", g=G)
            nc.vector.tensor_tensor(att_view(prob[:, two], qb), att_view(scores, qb), att_view(mask, qb),
                                    ALU.add).then_inc(att_masked, 1)
            dve.wait_ge(att_masked, i + 1)
            nc.vector.tensor_reduce(att_m[:, two, 0:1], att_view(prob[:, two], qb), AX.XY, ALU.max).then_inc(att_step, 1)
            dve.wait_ge(att_step, 2 * i + 1)
            nc.vector.tensor_scalar(att_m[:, two, 1:2], att_m[:, two, 0:1], -SCALE, None,
                                    ALU.mult).then_inc(att_negmax, 1)

        def act_exp(act, i):
            act.wait_ge(att_negmax, i + 1)
            view = att_view(prob[:, i % 2], i % 2)
            nc.scalar.activation(view, view, ACT.Exp, bias=att_m[:, i % 2, 1:2], scale=SCALE,
                                 accum_out=att_m[:, i % 2, 2:3]).then_inc(att_exp, 1)

        def dve_sum_inverse(dve, i):
            dve.wait_ge(att_exp, i + 1)
            nc.vector.reciprocal(att_m[:, i % 2, 3:4], att_m[:, i % 2, 2:3]).then_inc(att_step, 1)

        def act_prob(act, i):
            act.wait_ge(att_step, 2 * i + 2)
            view = att_view(prob[:, i % 2], i % 2)
            nc.scalar.activation(view, view, ACT.Copy, scale=att_m[:, i % 2, 3:4]).then_inc(att_prob, 1)

        def att_blocks(i):
            return [(g, kb) for g in range(G) for kb in range(i % 2 + 1)]

        def turned_copies(i):
            return 3 * ((i + 1) // 2) + (i + 1) % 2

        def pe_turn(pe, i):
            pe.wait_ge(att_prob, i + 1)
            if i:
                pe.wait_ge(att_out, i)
            for n, (g, kb) in enumerate(att_blocks(i)):
                c = kb * P if i % 2 else P
                last = nc.tensor.transpose(aux67[:, n // 4, (n % 4) * P:(n % 4 + 1) * P],
                                           prob[:, i % 2, g, c:c + P], ident)
            last.then_inc(att_turned, 1)

        def turned_copy(eng, i, part):
            n = len(att_blocks(i))
            a, b = (0, min(n, 4)) if part == 0 else (4, n)
            if a >= b:
                return
            eng.wait_ge(att_turned, i + 1)
            if i:
                eng.wait_ge(att_pv, i)
            src = aux67[:].rearrange("p c f -> p (c f)")[:, a * P:b * P]
            if part == 0:
                nc.scalar.activation(probT[:, a * P:b * P], src, ACT.Copy).then_inc(att_turned_out, 1)
            else:
                nc.vector.tensor_copy(probT[:, a * P:b * P], src).then_inc(att_turned_out, 1)

        def pe_pv(pe, i):
            h, qb = i // 2, i % 2
            pe.wait_ge(att_turned_out, turned_copies(i))
            blks = att_blocks(i)
            out = bank7[(h % 2) * AE:(h % 2 + 1) * AE, 256:256 + P]
            for n, (g, kb) in enumerate(blks):
                last = nc.tensor.matmul(out, v_tok[:, kb, g * AW + h * AE:g * AW + (h + 1) * AE],
                                        probT[:, n * P:(n + 1) * P], start=n == 0, stop=n == len(blks) - 1)
            last.then_inc(att_pv, 1)

        def act_pv(act, i):
            h, qb = i // 2, i % 2
            act.wait_ge(att_pv, i + 1)
            rows = slice((h % 2) * AE, (h % 2 + 1) * AE)
            nc.scalar.activation(oa[rows, h // 2, qb * P:(qb + 1) * P], bank7[rows, 256:256 + P],
                                 ACT.Copy).then_inc(att_out, 1)

        def sp_kv_load(sp, n, part):
            i = n % (B * G)
            b, g = i // G, i % G
            if n >= 4:
                m = n - 4
                if m < B * G:
                    sp.wait_ge(kq_done, m + 1)
                else:
                    sp.wait_ge(dec_v_done, m - B * G + 1)
            dil = GROUPS[g][1]
            src = caches[g][b].rearrange("(p d) c -> p d c", d=dil)[:, 0, part * AW:(part + 1) * AW]
            sp.dma_start(kv[:, n % 4], src).then_inc(kv_in[n % 4], 16)

        def pe_dec_q(pe, i):
            b, g = i // G, i % G
            if i >= 2:
                pe.wait_ge((kq_mul[0], q_copied)[i % 2], i // 2)
            nc.tensor.matmul(aux67[:, i % 2], pick[0:PICK, b:b + 1].to_broadcast([PICK, P]),
                             q_hl[0:PICK, g * AW:(g + 1) * AW], start=True, stop=True).then_inc(qb_psum, 1)

        def act_dec_q(act, i):
            act.wait_ge(qb_psum, i + 1)
            if i >= 2:
                act.wait_ge(kq_mul[1], i // 2)
            nc.scalar.activation(q_spread[:], aux67[:, 1], ACT.Copy).then_inc(q_copied, 1)

        def dec_mul(eng, ops, i):
            eng.wait_ge(kv_in[i % 4], 16 * (i // 4 + 1))
            if i % 2 == 0:
                eng.wait_ge(qb_psum, i + 1)
            else:
                eng.wait_ge(q_copied, i // 2 + 1)
            ops.tensor_tensor(kv[:, i % 4], kv[:, i % 4], aux67[:, 0] if i % 2 == 0 else q_spread[:],
                              ALU.mult).then_inc(kq_mul[i % 2], 1)

        def dve_dec_k(dve, i):
            b, g = i // G, i % G
            if i % 2 == 0:
                dec_mul(dve, nc.vector, i)
            dve.wait_ge(kq_mul[i % 2], i // 2 + 1)
            out = dec_s[:, g].rearrange("p (r n b) -> p n r b", r=2, b=B)[:, :, :, b]
            nc.vector.tensor_reduce(out, kv[:, i % 4].rearrange("p (n r e) -> p n r e", r=2, e=AE), AX.X,
                                    ALU.add).then_inc(kq_done, 1)

        def dve_dec_own(dve):
            nc.vector.tensor_tensor(qk_own[:], qk[:, 0:AT, S:T], qk[:, AT:2 * AT, S:T], ALU.mult).then_inc(dec_dve, 1)

        def pe_dec_scores(pe):
            pe.wait_ge(dec_dve, 1)
            pe.wait_ge(kq_done, B * G)
            for g in range(G):
                nc.tensor.transpose(bank6[0:64, g * P:(g + 1) * P], dec_s[:, g], ident)
            for g in range(G):
                for r in range(2):
                    last = nc.tensor.matmul(bank6[32 * r:32 * r + 32, G * P + g:G * P + g + 1],
                                            qk_own[:, 4 * g:4 * g + 4].rearrange("p n b -> p (n b)"),
                                            blocks[:, r * AE:r * AE + 1], start=True, stop=True)
            last.then_inc(dec_pe, 1)

        NK = G * P + G

        def dve_dec_max(dve):
            dve.wait_ge(dec_pe, 1)
            nc.vector.tensor_reduce(dec_m[0:64, 0:1], bank6[0:64, 0:NK], AX.X, ALU.max).then_inc(dec_dve, 1)
            dve.wait_ge(dec_dve, 2)
            nc.vector.tensor_scalar(dec_m[0:64, 1:2], dec_m[0:64, 0:1], -SCALE, None, ALU.mult).then_inc(dec_dve, 1)

        def act_dec_exp(act):
            act.wait_ge(dec_dve, 3)
            nc.scalar.activation(dec_p[0:64, :], bank6[0:64, 0:NK], ACT.Exp, bias=dec_m[0:64, 1:2], scale=SCALE,
                                 accum_out=dec_m[0:64, 2:3]).then_inc(dec_act, 1)

        def dve_dec_prob(dve):
            dve.wait_ge(dec_act, 1)
            nc.vector.reciprocal(dec_m[0:64, 3:4], dec_m[0:64, 2:3]).then_inc(dec_dve, 1)
            dve.wait_ge(dec_dve, 4)
            nc.vector.tensor_scalar(dec_p[0:64, :], dec_p[0:64, :], dec_m[0:64, 3:4], None,
                                    ALU.mult).then_inc(dec_dve, 1)
            dve.wait_ge(dec_dve, 5)
            for g in range(G):
                nc.vector.tensor_scalar(dec_diag[0:64, g], ident[0:64, 0:64], dec_p[0:64, G * P + g:G * P + g + 1],
                                        None, ALU.mult).then_inc(dec_dve, 1)

        def pe_dec_turn(pe):
            pe.wait_ge(dec_dve, 5 + G)
            for g in range(G):
                nc.tensor.transpose(bank5[:, g * 64:(g + 1) * 64], dec_p[0:64, g * P:(g + 1) * P], ident[0:64, 0:64])
            nc.tensor.matmul(bank4[0:B, 0:G * 64], const("rsel", 64), dec_diag[0:64].rearrange("p g r -> p (g r)"),
                             start=True, stop=True).then_inc(dec_pe, 1)

        def act_dec_turn(act):
            act.wait_ge(dec_pe, 2)
            for g in range(G):
                nc.scalar.activation(dec_pT[:, g].rearrange("p (c h b) -> p h c b", c=2, b=4),
                                     bank5[:, g * 64:(g + 1) * 64].rearrange("p (h c b) -> p h c b", c=2, b=4),
                                     ACT.Copy).then_inc(dec_act, 1)
            nc.scalar.activation(dec_own[0:B].rearrange("p g r -> p (g r)"), bank4[0:B, 0:G * 64],
                                 ACT.Copy).then_inc(dec_act, 1)

        def pe_dec_own(pe):
            pe.wait_ge(dec_act, 2 + G)
            for g in range(G):
                for n in range(4):
                    nc.tensor.matmul(bank5[:, n * 16:(n + 1) * 16].rearrange("p (r b) -> p r b", r=2),
                                     v_s[0:B, g * AW + n * P:g * AW + (n + 1) * P],
                                     dec_own[0:B, g].rearrange("p (r n b) -> p n r b", r=2, b=B)[:, n],
                                     start=g == 0 and n == 0, stop=False, skip_group_check=True)

        def pe_dec_v(pe, i):
            b, g = i // G, i % G
            n0 = B * G + i
            pe.wait_ge(kv_in[n0 % 4], 16 * (n0 // 4 + 1))
            nc.tensor.matmul(aux67[32 * (b % 4):32 * (b % 4) + 32, b // 4],
                             dec_pT[:, g, 32 * (b // 4):32 * (b // 4) + 32], kv[:, n0 % 4],
                             start=g == 0, stop=g == G - 1).then_inc(dec_v_done, 1)

        def dve_dec_own_rows(dve, half):
            dve.wait_ge(dec_v_done, B * G // 2 * (half + 1))
            nc.vector.tensor_tensor(v_own[:, half].rearrange("p (h e) -> p h e", h=AH),
                                    aux67[:, half].rearrange("p (h e) -> p h e", h=AH),
                                    const("own_head").unsqueeze(2).to_broadcast([P, AH, AE]),
                                    ALU.mult).then_inc(v_own_done, 1)

        def pe_dec_gather(pe):
            pe.wait_ge(v_own_done, 2)
            for half in range(2):
                for n in range(4):
                    out = bank5[:, n * 16:(n + 1) * 16].rearrange("p (r b) -> p r b", r=2)[:, :, 4 * half:4 * half + 4]
                    last = nc.tensor.matmul(out, v_own[:, half, n * P:(n + 1) * P],
                                            const("own_seq").rearrange("p (r b) -> p r b", r=2),
                                            start=False, stop=half == 1 and n == 3, skip_group_check=True)
            last.then_inc(dec_pe, 1)

        def dve_dec_out(dve):
            dve.wait_ge(dec_pe, 3)
            for r in range(2):
                rows = slice(r * AE, (r + 1) * AE)
                nc.vector.tensor_copy(oa[rows, :, S:T],
                                      bank5[rows, 0:64].rearrange("p (n r b) -> p n r b", r=2, b=B)[:, :, r]
                                      ).then_inc(dec_dve, 1)
        DEC_DVE = 5 + G + 2

        fi1, fo1, p_qr, p_kr, p_vr, p_gr, p_qk, p_v, p_gb, p_pb, p_ga, p_pa, p_wo, fi2, fo2 = phases
        QK_LAST = {0: (18,), 1: (19,), 2: (20, 21), 3: (22, 23)}
        V_TURNED = {4: (0,), 5: (1, 2), 6: (3, 4), 7: (5, 6), 8: (7,), 9: (8,), 10: (9,), 11: (10,)}
        QS_TURNED = {9: (0,), 10: (1,), 11: (2,)}
        DEC_V = {2: range(0, 4), 3: range(4, 9), 4: range(9, 14), 5: range(14, 19), 6: range(19, 24)}
        ATT_AT = 7
        OA_SPLIT = {0: (0,), 1: (1,), 4: (2,), 7: (3,)}

        block = ctx.enter_context(nc.Block())

        @block.sync
        def _(sp):
            for n in range(2):
                half = slice(n * KD // 2, (n + 1) * KD // 2)
                sp.dma_start(x[:, half], xT[:, half]).then_inc(x_in[n], 16)
            sp.dma_start(tab[:, 0:EARLY], tables[:, 0:EARLY]).then_inc(const_in, 16)
            sp.dma_start(gain[:], gains).then_inc(const_in, 16)
            sp.wait_ge(pe_half, 1)
            sp.dma_start(tab[:, EARLY:], tables[:, EARLY:]).then_inc(tab_in, 16)

            ROWS = 256
            pieces = []
            for g in (2, 1, 0):
                n = caches[g].shape[0] * caches[g].shape[1]
                src = caches[g].rearrange("b w c -> (b w) c")
                dst = kv_outs[g].rearrange("b w c -> (b w) c")
                for a in range(0, n, ROWS):
                    if a + ROWS < n:
                        pieces.append((dst, src, a, ROWS))
                    else:
                        pieces += [(dst, src, a, ROWS - 16), (dst, src, a + ROWS - 16, 15)]

            def roll(sp, c, it=0):
                dst, src, a, rows = pieces[c]
                if not moving(it):
                    sp.dma_start(dst[a:a + rows], src[a + 1:a + 1 + rows]).then_inc(rolled, 16)
                else:
                    sp.dma_start(dst[bass.ds(a + ROWS * it, rows)],
                                 src[bass.ds(a + 1 + ROWS * it, rows)]).then_inc(rolled, 16)

            first = 4 * (fi1.quads + fo1.quads) // 3
            with sp.Fori(0, first) as it:
                sp.wait_ge(pe_half, 3 * it + 2)
                roll(sp, 0, it)
            done = first

            def roll_more(sp, n):
                nonlocal done
                for _ in range(n):
                    if done < len(pieces):
                        roll(sp, done)
                        done += 1

            for q in range(p_qr.q0, p_gr.q0 + p_gr.quads):
                for j in range(0, 4, 2):
                    sp.wait_ge(pe_half, 4 * q + j)
                    if q < p_qk.q0 - 1:
                        roll_more(sp, 2 if KIND_OF[q] == "gr" else j // 2 + q % 2 * (1 - j // 2))
                if q >= p_gr.q0 + 1:
                    h = q - p_gr.q0 - 1
                    sp.wait_ge(snew_out, 2 * h + 2)
                    sp.dma_start(ret_out[h].rearrange("(p r) e -> p (r e)", r=2),
                                 s_new[:].rearrange("p r e -> p (r e)")).then_inc(ret_stored, 16)
            sp.wait_ge(snew_out, 2 * RH)
            sp.dma_start(ret_out[RH - 1].rearrange("(p r) e -> p (r e)", r=2),
                         s_new[:].rearrange("p r e -> p (r e)")).then_inc(ret_stored, 16)
            for h in range(RH):
                sp_state_load(sp, 0, h)
            with sp.Fori(0, p_qk.quads) as it:
                for h in range(RH):
                    sp_state_store(sp, 0, h, it)
                    sp_state_load(sp, 1, h, it)
            for b in range(p_qk.quads, B):
                for h in range(RH):
                    sp_state_store(sp, b, h)
                    if b + 1 < B:
                        sp_state_load(sp, b + 1, h)
            sp.wait_ge(qk_done, 2 * AT)
            sp.dma_start(kT_out, qk[:, AT:2 * AT]).then_inc(stored, 16)
            for n in range(2 * B * G):
                sp_kv_load(sp, n, n // (B * G))
                if n == 5:
                    sp.wait_ge(v_out_sem, AT)
                    sp.dma_start(v_out.rearrange("(c p) f -> p c f", c=2), v_tok[:]).then_inc(stored, 16)
            for q in range(p_pb.q0 + 2, fi2.q0):
                sp.wait_ge(pe_half, 4 * q)
                roll_more(sp, 2)
                if KIND_OF[q] in ("pb", "ga"):
                    sp.wait_ge(pe_half, 4 * q + 2)
                    roll_more(sp, 1)
            paced = 4 * fi2.q0
            while done < len(pieces):
                sp.wait_ge(pe_half, paced)
                roll_more(sp, 1)
                paced += 3
            sp.wait_ge(rolled, 16 * len(pieces))
            sp.wait_ge(qks_out, 6)
            sp.wait_ge(vs_out, AT)
            for g in range(G):
                w = caches[g].shape[1]
                sp.dma_start(kv_outs[g][:, w - 1, 0:AW], k_s[0:B, g * AW:(g + 1) * AW]).then_inc(stored, 16)
                sp.dma_start(kv_outs[g][:, w - 1, AW:2 * AW], v_s[0:B, g * AW:(g + 1) * AW]).then_inc(stored, 16)
            for m in range(KD):
                sp.wait_ge(out_of["dve"], fo2.out0 + m + 1)
                sp.dma_start(yT[:, m], x[:, m]).then_inc(stored, 16)
            sp.wait_ge(stored, 16 * STORES)
            sp.wait_ge(ret_stored, 16 * RH)

        @block.scalar
        def _(act):
            load_half(act, 0, 0)
            for m in range(KD):
                if m % (KD // 2) == 0:
                    act.wait_ge(x_in[2 * m // KD], 16)
                act_square(act, 0, m)
                if m == 1:
                    for j in range(1, 4):
                        load_half(act, 0, j)
            act.wait_ge(const_in, 32)
            hi_half(act, 0, 0)
            act_norm(act, 0)
            for j in range(1, 4):
                hi_half(act, 0, j)
            for j in range(3):
                act.wait_ge(lo_done, j + 1)
                load_half(act, 1, j)

            def ffn(fi, fo, norm):
                act_fi_quad(act, fi, 0)
                with act.Fori(0, fi.quads - 3) as it:
                    act_fi_quad(act, fi, 1, it)
                for qq in range(fi.quads - 2, fi.quads):
                    act_fi_quad(act, fi, qq)
                with act.Fori(0, fo.quads // 2 - 1) as it:
                    for m in range(2):
                        act_fo_quad(act, fo, m, 2 * it, norm)
                for m in range(fo.quads - 2, fo.quads):
                    act_fo_quad(act, fo, m, 0, norm)

            ffn(fi1, fo1, 1)
            for which, ph in enumerate((p_qr, p_kr)):
                for qq in range(ph.quads):
                    act_rr_quad(act, ph, qq, which)
            for t in range(16):
                act_ahead(act, p_vr.q0 + t // 4, t % 4)
                act_v_tile(act, p_vr, t)
                if t:
                    act_v_small(act, p_vr, t - 1)
            act_v_small(act, p_vr, 15)
            act.wait_ge(tab_in, 16)
            act.wait_ge(rr_done, 2 * RH)
            act.wait_ge(rr_pool, 6 * RH)
            nc.scalar.activation(qr_s[:], qr[:, :, S:T], ACT.Copy).then_inc(rs_copied, 1)
            nc.scalar.activation(kr_s[:], kr[:, :, S:T], ACT.Copy).then_inc(rs_copied, 1)
            act.wait_ge(cleared, 2)
            act.wait_ge(vrs_out, 16)
            nc.scalar.activation(vr_hl[0:B], vs_ret[0:B], ACT.Copy).then_inc(vr_hi, 1)
            nc.scalar.activation(pick[0:PICK], const("pick", PICK), ACT.Copy).then_inc(pick_done, 1)
            act.wait_ge(pick_done, 1)
            act_pick(act, 0)
            for h in range(RH):
                for j in range(4):
                    if j == 0:
                        act_ret_k(act, h)
                    if j == 1:
                        act_ret_o(act, h)
                    if j == 2:
                        act_ret_state(act, h)
                    if j == 3:
                        act_ret_rms(act, h)
                    act_gr_tile(act, p_gr, 4 * h + j)
                    act_ahead(act, p_gr.q0 + h, j)


            def qk_quad(qq, it=0):
                for j in range(4):
                    t = 4 * qq + j
                    if t >= 2:
                        act_state_o(act, (t - 2) // 4, (t - 2) % 4, it)
                    if j == 0 and qq:
                        act_pick(act, qq, it)
                    if j == 1 and qq:
                        act_qk_rms(act, qq - 1, it)
                    act_ahead(act, p_qk.q0 + qq, j, it)
                    act_qk_evac(act, p_qk, qq, j, it)
                    act_state(act, qq, j, it)

            qk_quad(0)
            with act.Fori(0, AT // 4 - 1) as it:
                qk_quad(1, it)
            with act.Fori(0, AT // 4) as it:
                qk_quad(AT // 4, it)
            act.wait_ge(ret_stored, 16 * RH)
            for t in range(AT):
                s = RH * p_qk.quads + t
                if s - 2 < B * RH:
                    act_state_o(act, (s - 2) // 4, (s - 2) % 4)
                if s % 4 == 0 and s < B * RH:
                    act_pick(act, s // 4)
                if t == 1:
                    act_qk_rms(act, p_qk.quads - 1)
                act_ahead(act, p_v.q0 + t // 4, t % 4)
                act_v_tile(act, p_v, t)
                if s < B * RH:
                    act_state(act, s // 4, s % 4)
                for n in QS_TURNED.get(t, ()):
                    act_samples_rows(act, n)
                for i in V_TURNED.get(t, ()):
                    act_v_small(act, p_v, i)
                if t == 9:
                    act.wait_ge(os_out, B * RH)
                    nc.scalar.activation(o_s2[:], o_s[:], ACT.Square).then_inc(small_act, 1)
                if t == 10:
                    act.wait_ge(small_pe, 1)
                    nc.scalar.activation(os_sum[:].rearrange("p h b -> p (h b)"), bank4[:, 0:RH * B], ACT.Sqrt,
                                         bias=eps, scale=1.0 / RV).then_inc(small_act, 1)

            def split_ob(h):
                nc.scalar.activation(obh[:, 4 * h:4 * h + 4], ob[:, 4 * h:4 * h + 4], ACT.Copy).then_inc(ob_hi, 1)

            act.wait_ge(small_step, 4)
            for h in range(RH):
                act.wait_ge(state_stored[h], 16 * B)
            split_ob(0)
            for t in range(KD):
                if t == 0:
                    act_v_small(act, p_v, AT - 1)
                for i in range(3 * t, 3 * t + 3):
                    if i % 2:
                        act_dec_q(act, i)
                act_ahead(act, p_gb.q0 + t // 4, t % 4)
                if t < 3:
                    split_ob(t + 1)
                act.wait_ge(pe_half, 4 * p_gb.q0 + t + 1)
                act.wait_ge(ob_split, 1 + t // 4)
                nc.scalar.activation(gate_b[:, t], acc[t % 4][:, 0:T], ACT.Sigmoid).then_inc(out_of["act"], 1)

            def att(i):
                if i >= 2:
                    act_pv(act, i - 2)
                if i % 2:
                    turned_copy(act, i - 1, 0)
                if i < 16:
                    act_exp(act, i)
                    act_prob(act, i)
                if i >= 1 and i % 2 == 0:
                    turned_copy(act, i - 1, 0)
                if i == 16:
                    act_pv(act, i - 1)

            def split_oa(n):
                act.wait_ge(att_out, 4 * n + 4)
                nc.scalar.activation(oah[:, n], oa[:, n], ACT.Copy).then_inc(oa_hi, 1)

            for i in range(16):
                if i == 0:
                    act_dec_exp(act)
                if i >= ATT_AT:
                    att(i - ATT_AT)
                act_ahead(act, p_pb.q0 + i // 4, i % 4)
                if i == 1:
                    act_dec_turn(act)
            act.wait_ge(dec_dve, DEC_DVE)
            for t in range(KD):
                att(16 - ATT_AT + t)
                act_ahead(act, p_ga.q0 + t // 4, t % 4)
                act.wait_ge(pe_half, 4 * p_ga.q0 + t + 1)
                nc.scalar.activation(gate_a[:, t], acc[t % 4][:, 0:T], ACT.Copy).then_inc(out_of["act"], 1)
                for n in OA_SPLIT.get(t, ()):
                    split_oa(n)
            act.wait_ge(out_of["act"], p_ga.out0 + KD)
            for m in range(KD):
                nc.scalar.activation(gate_a[:, m], gate_a[:, m], ACT.Sigmoid).then_inc(gate_done, 1)
            for j in range(4):
                for m in (2 * j, 2 * j + 1):
                    act.wait_ge(merge_done, m + 1)
                    nc.scalar.activation(hh[:, m], merge[:, m % 2], ACT.Copy).then_inc(merge_hi, 1)
                act_ahead(act, p_pa.q0, j)
            for m in range(KD):
                act.wait_ge(out_of["dve"], p_wo.out0 + m + 1)
                act_square(act, 2, m)
                if m < 3:
                    act_samples_rows(act, 3 + m)
                if m == KD - 1:
                    act_norm(act, 2)
                act_ahead(act, p_wo.q0 + m // 4, m % 4)
            ffn(fi2, fo2, None)

        @block.vector
        def _(dve):
            for m in range(KD):
                dve_sum_square(dve, 0, m)
            dve.wait_ge(const_in, 32)
            for n in range(2):
                dve.wait_ge(x_in[n], 16)
            lo_half(dve, 0, 0)
            dve_norm(dve, 0)
            for j in range(1, 4):
                lo_half(dve, 0, j)

            def ffn(fi, fo, norm):
                dve_fi_quad(dve, fi, 0)
                with dve.Fori(0, fi.quads - 3) as it:
                    dve_fi_quad(dve, fi, 1, it)
                for qq in range(fi.quads - 2, fi.quads):
                    dve_fi_quad(dve, fi, qq)
                start = 0
                if norm is not None:
                    for m in range(2):
                        dve_fo_quad(dve, fo, m, 0, norm)
                    start = 2
                with dve.Fori(0, (fo.quads - 2 - start) // 2) as it:
                    for m in range(start, start + 2):
                        dve_fo_quad(dve, fo, m, 2 * it, norm)
                for m in range(fo.quads - 2, fo.quads):
                    dve_fo_quad(dve, fo, m, 0, norm)

            ffn(fi1, fo1, 1)
            dve.wait_ge(tab_in, 16)
            for which, ph in enumerate((p_qr, p_kr)):
                for t in range(2 * RH):
                    dve_ahead(dve, ph.q0 + t // 4, t % 4)
                    if t % 2:
                        turn_head(dve, nc.vector, ph, t // 2, which)
            for t in range(16):
                if t:
                    dve_v_tile(dve, p_vr, t - 1)
                dve_ahead(dve, p_vr.q0 + t // 4, t % 4)
            dve_v_tile(dve, p_vr, 15)
            dve.wait_ge(vr_hi, 1)
            nc.vector.tensor_tensor(vr_hl[32:PICK], vs_ret[0:B], vr_hl[0:B].bitcast(F32), ALU.subtract).then_inc(vr_lo, 1)
            for h in range(RH):
                for j in range(4):
                    if j == 0:
                        dve_ret_a(dve, h)
                    if j == 2:
                        dve_ret_sum(dve, h)
                    dve_gr_tile(dve, p_gr, 4 * h + j)
                    dve_ahead(dve, p_gr.q0 + h, j)
                    if j == 0 and h:
                        for part in range(3):
                            dve_ret_norm(dve, p_gr, h - 1, part)


            def qk_quad(qq, it=0):
                for j in range(4):
                    t = 4 * qq + j
                    if t:
                        dve_state(dve, (t - 1) // 4, (t - 1) % 4, it)
                    if t >= 2:
                        dve_qk_sin(dve, t - 2, it)
                    if t >= 6:
                        dve_qk_norm(dve, t - 6, it)
                    if j == 1 and qq:
                        dve_qk_rinv(dve, qq - 1, it)
                    dve_ahead(dve, p_qk.q0 + qq, j, it)
                    if t < 3:
                        dve_ret_norm(dve, p_gr, RH - 1, t)

            qk_quad(0)
            qk_quad(1)
            with dve.Fori(0, p_qk.quads - 2) as it:
                qk_quad(2, it)
            for t in range(AT):
                s = RH * p_qk.quads + t
                if s - 1 < B * RH:
                    dve_state(dve, (s - 1) // 4, (s - 1) % 4)
                if t < 2:
                    dve_qk_sin(dve, 2 * AT - 2 + t)
                for i in QK_LAST.get(t, ()):
                    dve_qk_norm(dve, i)
                if t == 1:
                    dve_qk_rinv(dve, p_qk.quads - 1)
                if t == 10:
                    dve.wait_ge(small_act, 1)
                    nc.vector.tensor_reduce(os_sum[:], o_s2[:].rearrange("p (h e) b -> p h b e", e=4), AX.X,
                                            ALU.add).then_inc(small_step, 1)
                if t == 11:
                    dve.wait_ge(small_act, 2)
                    nc.vector.reciprocal(os_sum[:], os_sum[:]).then_inc(small_step, 1)
                    dve.wait_ge(small_step, 2)
                    nc.vector.tensor_tensor(o_s[:].rearrange("p (h e) b -> p h e b", e=4),
                                            o_s[:].rearrange("p (h e) b -> p h e b", e=4),
                                            os_sum[:].unsqueeze(2).to_broadcast([P, RH, 4, B]),
                                            ALU.mult).then_inc(small_step, 1)
                    dve.wait_ge(small_step, 3)
                    nc.vector.tensor_tensor(ob[:, :, S:T], ob[:, :, S:T], o_s[:], ALU.mult).then_inc(small_step, 1)
                    dve_dec_own(dve)
                dve_ahead(dve, p_v.q0 + t // 4, t % 4)
                for i in V_TURNED.get(t, ()):
                    dve_v_tile(dve, p_v, i)
                for n in QS_TURNED.get(t, ()):
                    dve_samples_low(dve, n)
            for t in range(KD):
                if t == 0:
                    dve_v_tile(dve, p_v, AT - 1)
                for i in range(3 * t, 3 * t + 3):
                    dve_dec_k(dve, i)
                dve_ahead(dve, p_gb.q0 + t // 4, t % 4)

            def pb_tile(m):
                dve.wait_ge(pe_half, 4 * p_pb.q0 + 2 * m + 2)
                nc.vector.tensor_tensor(gate_b[:, m], gate_b[:, m], acc[m % 4][:, 0:T],
                                        ALU.mult).then_inc(out_of["dve"], 1)

            def att(i):
                if i < 16:
                    dve_scores(dve, i)
                if i < 16:
                    dve_sum_inverse(dve, i)
                if i >= 1:
                    turned_copy(dve, i - 1, 1)

            for i in range(16):
                if i == 0:
                    dve_dec_max(dve)
                if i == 1:
                    dve.wait_ge(out_of["act"], p_gb.out0 + KD)
                    dve_dec_prob(dve)
                if i == 5:
                    dve_dec_own_rows(dve, 0)
                if i == ATT_AT:
                    dve_dec_own_rows(dve, 1)
                    dve_dec_out(dve)
                if i >= ATT_AT:
                    att(i - ATT_AT)
                if i % 2:
                    pb_tile(i // 2)
                dve_ahead(dve, p_pb.q0 + i // 4, i % 4)
            for t in range(KD):
                att(16 - ATT_AT + t)
                dve_ahead(dve, p_ga.q0 + t // 4, t % 4)
                for n in OA_SPLIT.get(t, ()):
                    dve.wait_ge(oa_hi, n + 1)
                    nc.vector.tensor_tensor(oal[:, n], oa[:, n], oah[:, n].bitcast(F32),
                                            ALU.subtract).then_inc(oa_split, 1)
            for j in range(4):
                for m in (2 * j, 2 * j + 1):
                    dve.wait_ge(pe_half, 4 * p_pa.q0 + j + 1)
                    dve.wait_ge(gate_done, m + 1)
                    nc.vector.tensor_tensor(merge_a[:, m % 2], gate_a[:, m], acc[m % 4][:, 0:T],
                                            ALU.mult).then_inc(out_of["dve"], 1)
                    dve.wait_ge(out_of["dve"], p_pa.out0 + m + 1)
                    if m >= 2:
                        dve.wait_ge(merge_lo[m % 2], m // 2)
                    nc.vector.tensor_tensor(merge[:, m % 2], merge_a[:, m % 2], gate_b[:, m],
                                            ALU.add).then_inc(merge_done, 1)
                dve.wait_ge(merge_hi, 2 * j + 2)
                nc.vector.tensor_tensor(hl[:, 2 * j + 1], merge[:, 1], hh[:, 2 * j + 1].bitcast(F32),
                                        ALU.subtract).then_inc(merge_lo[1], 1)
                dve_ahead(dve, p_pa.q0, j)
            for m in range(KD):
                dve.wait_ge(pe_half, 4 * p_wo.q0 + m + 1)
                dve_add_x(dve, p_wo, m, 1.0, m % 4)
                dve_sum_square(dve, 2, m)
                if m == KD - 1:
                    dve_norm(dve, 2)
                dve_ahead(dve, p_wo.q0 + m // 4, m % 4)
            ffn(fi2, fo2, None)

        @block.gpsimd
        def _(pool):
            def ffn(fi):
                with pool.Fori(0, fi.quads) as it:
                    pool_fi_quad(pool, fi, 0, it)

            pool_norm(pool, 0)
            nc.gpsimd.memset(vr_hl[0:PICK].bitcast(F32), 0.0).then_inc(cleared, 1)
            nc.gpsimd.memset(q_hl[0:PICK].bitcast(F32), 0.0).then_inc(cleared, 1)
            ffn(fi1)
            pool_norm(pool, 1)
            pool.wait_ge(tab_in, 16)
            for which, ph in enumerate((p_qr, p_kr)):
                for h in range(RH):
                    turn_head(pool, nc.gpsimd, ph, h, which)

            for t in range(2 * AT):
                pool_qk_rot(pool, p_qk, t)
            def split_ob(h):
                pool.wait_ge(ob_hi, h + 1)
                nc.gpsimd.tensor_tensor(obl[:, 4 * h:4 * h + 4], ob[:, 4 * h:4 * h + 4],
                                        obh[:, 4 * h:4 * h + 4].bitcast(F32), ALU.subtract).then_inc(ob_split, 1)

            for h, items in enumerate(((1,), (3, 5), (7,), range(9, B * G, 2))):
                split_ob(h)
                for i in items:
                    dec_mul(pool, nc.gpsimd, i)
            for m in range(0, KD, 2):
                pool.wait_ge(merge_hi, m + 1)
                nc.gpsimd.tensor_tensor(hl[:, m], merge[:, m % 2], hh[:, m].bitcast(F32),
                                        ALU.subtract).then_inc(merge_lo[0], 1)
            pool_norm(pool, 2)
            ffn(fi2)

        @block.tensor
        def _(pe):
            def ffn(fi, fo, r):
                norm = normed_tile(pe, r)
                pe_wide_first(fi, norm)
                with pe.Fori(0, fi.quads - 1) as it:
                    for j in range(4):
                        pe_wide_half(pe, fi, 1, j, it)
                with pe.Fori(0, fo.quads // 2) as it:
                    for m in range(2):
                        pe_fo_quad(pe, fo, m, m, 2 * it)

            def pe_wide_first(ph, norm):
                for j in range(4):
                    pe_wide_half(pe, ph, 0, j, 0, norm if j == 0 else None)

            pe.wait_ge(const_in, 32)
            pe_norm(pe, 0)
            ffn(fi1, fo1, 0)
            pe_norm(pe, 1)
            for ph in (p_qr, p_kr):
                for qq in range(ph.quads):
                    for j in range(4):
                        pe_wide_half(pe, ph, qq, j, 0, normed_tile(pe, 1) if ph is p_qr and qq == 0 and j == 0 else None)
            pe.wait_ge(tab_in, 16)
            for t in range(16):
                pe_wide_half(pe, p_vr, t // 4, t % 4, between={7: [lambda: pe_v_tile(pe, p_vr, t - 1)]} if t else None)
            pe.wait_ge(rr_done, 2 * RH)
            pe.wait_ge(rr_pool, 6 * RH)

            def ret_a(h):
                if h == 0:
                    pe.wait_ge(vr_out, 16)
                    pe.wait_ge(vrs_out, 16)
                pe_ret_a(pe, h)

            for h in range(RH):
                pe_wide_half(pe, p_gr, h, 0, between={2: [lambda: pe_v_tile(pe, p_vr, 15)] if h == 0 else [],
                                                      6: [lambda: ret_a(h)]})
                pe_wide_half(pe, p_gr, h, 1, between={4: [lambda: pe_ret_o(pe, h)]})
                pe_wide_half(pe, p_gr, h, 2, between={7: [lambda: pe_ret_state(pe, h)]})
                pe_wide_half(pe, p_gr, h, 3, between={6: [lambda: pe_ret_sum(pe, h)]})

            def slot_steps(t, it=0):
                steps = {k: [] for k in range(KD)}
                last_q = 2 * AT
                if t >= 2 and t - 2 < B * RH:
                    if t % 4 == 2 and t >= 6 and t - 3 < last_q:
                        steps[1].append(lambda: pe.wait_ge(qk_rms_done, t // 4 + it))
                    for e in range(4):
                        steps[1].append(lambda e=e: pe_state_o(pe, (t - 2) // 4, (t - 2) % 4, it, e))
                if t >= 1 and t - 1 < B * RH:
                    steps[0].append(lambda: pe_state_v(pe, (t - 1) // 4, (t - 1) % 4, it))
                if t >= 2 and t - 2 < last_q:
                    steps[0].append(lambda: pe_qk_rot(pe, p_qk, t - 2, it))
                spreads = QK_LAST.get(t - last_q, ()) if t >= last_q else (t - 6,) if t >= 6 else ()
                for k, i in zip((0, 6), spreads):
                    steps[k].append(lambda i=i: pe_qk_spread(pe, i, it))
                if t >= 2 and t - 2 < last_q:
                    steps[3].append(lambda: pe_qk_ms(pe, t - 2, it))
                return steps

            def bank_waits():
                pe.wait_ge(orms_done, RH)
                pe.wait_ge(adec_done, 2 * RH)
                pe.wait_ge(snew_out, 2 * RH)
                pe.wait_ge(vr_lo, 1)

            def qk_quad(qq, it=0):
                for j in range(4):
                    steps = slot_steps(4 * qq + j, it)
                    if 4 * qq + j == 1:
                        steps[0].insert(0, bank_waits)
                    pe_wide_half(pe, p_qk, qq, j, it, between=steps)

            qk_quad(0)
            qk_quad(1)
            with pe.Fori(0, p_qk.quads - 2) as it:
                qk_quad(2, it)

            def v_tile(i):
                if i == 0:
                    pe.wait_ge(qk_sin, 2 * AT)
                    pe.wait_ge(qk_done, 2 * AT)
                if i == AT - 2:
                    pe.wait_ge(small_act, 2)
                pe_v_tile(pe, p_v, i)

            def small_sum():
                pe.wait_ge(small_step, 1)
                pe.wait_ge(v_out_sem, AT - 3)
                pe.wait_ge(vs_out, AT - 3)
                nc.tensor.matmul(bank4[:, 0:RH * B], ones, os_sum[:].rearrange("p h b -> p (h b)"), start=True,
                                 stop=True).then_inc(small_pe, 1)

            def q_rows(n):
                if n == 0:
                    pe.wait_ge(os_out, B * RH)
                pe_samples_rows(pe, n)

            for t in range(AT):
                steps = slot_steps(RH * p_qk.quads + t)
                for k, i in zip((6, 7), V_TURNED.get(t, ())):
                    steps[k].append(lambda i=i: v_tile(i))
                for k, n in zip((3, 5), QS_TURNED.get(t, ())):
                    steps[k].append(lambda n=n: q_rows(n))
                if t == 10:
                    steps[7].append(small_sum)
                pe_wide_half(pe, p_v, t // 4, t % 4, between=steps)

            def first_key():
                pe.wait_ge(qks_out, 3)
                pe.wait_ge(qs_lo, 3)
                pe_dec_q(pe, 0)

            for t in range(KD):
                if t == 0:
                    steps = {3: [lambda: pe_v_tile(pe, p_v, AT - 1)], 5: [first_key], 6: [lambda: pe_dec_q(pe, 1)],
                             7: [lambda: pe_dec_q(pe, 2)]}
                else:
                    steps = {k: [lambda i=3 * t + n: pe_dec_q(pe, i)] for n, k in enumerate((2, 4, 7))}
                pe_wide_half(pe, p_gb, t // 4, t % 4, between=steps)
            pe.wait_ge(ob_split, RH)

            def att_steps(i):
                steps = {k: [] for k in range(KD)}
                if i < 16:
                    steps[0 if i else 5].append(lambda: pe_scores(pe, i))
                if i >= 2:
                    steps[2].append(lambda: pe_pv(pe, i - 2))
                if i == 0:
                    steps[2].append(lambda: pe_dec_gather(pe))
                    steps[5].insert(0, lambda: pe.wait_ge(dec_dve, DEC_DVE))
                if i >= 1:
                    steps[5 if i % 2 else 7].append(lambda: pe_turn(pe, i - 1))
                if i == 16:
                    steps[7].append(lambda: pe_pv(pe, i - 1))
                return steps

            for i in range(16):
                m = i // 2
                pe_wait_half(pe, p_pb.q0 + i // 4, i % 4)
                if i % 2 == 0:
                    pe_wait_acc(pe, p_pb, m, 4)
                steps = att_steps(i - ATT_AT) if i >= ATT_AT else {k: [] for k in range(KD)}
                if i == 0:
                    steps[5].append(lambda: pe_dec_scores(pe))
                if i == 1:
                    steps[7].append(lambda: pe_dec_turn(pe))
                if i == 2:
                    steps[3].append(lambda: pe_dec_own(pe))
                for n, v in enumerate(DEC_V.get(i, ())):
                    steps[4 + n if i == 2 else (1, 3, 4, 6, 7)[n]].append(lambda v=v: pe_dec_v(pe, v))
                for t in range(8):
                    for step in steps[t]:
                        step()
                    k = 8 * (i % 2) + t
                    last = three_passes(acc[m % 4][:, 0:T], i % 4, t, obh[:, k], obl[:, k], k == 0, k == 15)
                last.then_inc(pe_half, 1)
            for t in range(KD):
                pe_wide_half(pe, p_ga, t // 4, t % 4, between=att_steps(16 - ATT_AT + t))
            for j in range(4):
                pe_wait_half(pe, p_pa.q0, j)
                for m in (2 * j, 2 * j + 1):
                    pe_wait_acc(pe, p_pa, m, 4)
                    for k in range(4):
                        if m == 0:
                            pe.wait_ge(oa_split, k + 1)
                        last = three_passes(acc[m % 4][:, 0:T], j, 4 * (m % 2) + k, oah[:, k], oal[:, k],
                                            k == 0, k == 3)
                last.then_inc(pe_half, 1)

            def k_rows(n):
                pe.wait_ge(att_out, 16)
                pe_samples_rows(pe, n)

            for m in range(KD):
                pe_wide_half(pe, p_wo, m // 4, m % 4, 0, (lambda k: pe.wait_ge(merge_lo[k % 2], k // 2 + 1)) if m == 0 else None,
                             {4: [lambda: k_rows(3 + m)]} if m < 3 else None)
            pe_norm(pe, 2)
            ffn(fi2, fo2, 2)


def tiles_of(w, order):
    return [w[k * P:(k + 1) * P, cols] for k, cols in order]


def unit_array(w, orders):
    return np.stack([np.concatenate(tiles_of(w, order), axis=1) for order in orders])


def weight_units(i):
    def cols(a, step=1):
        return slice(a, a + P * step, step)

    def wide(w, starts, kt=KD):
        return unit_array(w, [[(k, c) for c in starts[n:n + 2] for k in range(kt)] for n in range(0, len(starts), 2)])

    def ffn_in(w):
        return wide(w, [cols(o + t * P) for t in range(FT) for o in (0, DFF)])

    def ffn_out(w):
        return unit_array(w, [[(k, cols(m * P)) for k in range(h * 11, h * 11 + 11)] for m in range(KD) for h in range(2)])

    w = i["w_in"][0]
    at = np.cumsum([0, G * AW, G * AW, G * AW, RH * RQ, RH * RQ, RH * RV, RH * RV, D, D])
    qa, ka, va, qr, kr, vr, gr, ga, gb = (int(a) for a in at[:9])

    def run(start, n):
        return [cols(start + t * P) for t in range(n)]

    def halves(start):
        return [cols(start + h * RQ + p, 2) for h in range(RH) for p in range(2)]

    pb = unit_array(i["w_pb"][0], [[(k, cols(m * P)) for k in range(16)] for m in range(KD)])
    pa = unit_array(i["w_pa"][0], [[(k, cols(m * P)) for m in range(n, n + 4) for k in range(4)] for n in (0, 4)])
    w16 = np.concatenate([
        ffn_in(i["ffn1_in"][0]), wide(w, halves(qr)), wide(w, halves(kr)), wide(w, run(vr, 16)), wide(w, run(gr, 16)),
        wide(w, run(qa, AT) + run(ka, AT)), wide(w, run(va, AT)), wide(w, run(gb, KD)), pb, wide(w, run(ga, KD)), pa,
        wide(i["w_o"][0], run(0, KD)), ffn_in(i["ffn2_in"][0])])
    w11 = np.concatenate([ffn_out(i["ffn1_out"][0]), ffn_out(i["ffn2_out"][0])])
    return w16, w11


def kernel(**inputs):
    import concourse.bacc as bacc
    from concourse.bass_utils import run_bass_kernel_spmd

    i = {k: np.asarray(v) for k, v in inputs.items()}
    tokens = np.concatenate([i["x_prompt"][0], i["x_sample"][:, 0]])
    xT = np.ascontiguousarray(tokens.T.reshape(KD, P, T).transpose(1, 0, 2))
    norms = [i[n][0].reshape(KD, P).T for n in ("ffn1_norm", "mix_norm", "ffn2_norm")]
    heads = [np.tile(i[n][0], 2)[:, None] for n in ("a_q_norm", "a_k_norm")]
    w16, w11 = weight_units(i)
    caches = [i[f"cache_kv_a{g}"][0].reshape(B, -1, 2 * AW) for g in range(G)]
    arrays = {"xT": xT, "tables": build_tables(), "gains": np.ascontiguousarray(np.concatenate(norms + heads, axis=1)),
              "w16": w16, "w11": w11, "cache0": caches[0], "cache1": caches[1], "cache2": caches[2],
              "state_in": i["state_ret"][0]}
    outs = {"yT": (P, KD, T), "kT_out": (P, AT, T), "v_out": (S, G * AW), "ret_out": (RH, RQ, RV),
            "kv0_out": caches[0].shape, "kv1_out": caches[1].shape, "kv2_out": caches[2].shape,
            "state_out": (B, RH, RQ, RV)}
    nc = bacc.Bacc("TRN2", target_bir_lowering=False, num_devices=1)
    args = [nc.dram_tensor(n, a.shape, mybir.dt.from_np(a.dtype), kind="ExternalInput").ap() for n, a in arrays.items()]
    args += [nc.dram_tensor(n, s, F32, kind="ExternalOutput").ap() for n, s in outs.items()]
    trunk_step(nc, *args)
    r = run_bass_kernel_spmd(nc, [arrays], core_ids=[0]).results[0]

    y = r["yT"].transpose(2, 1, 0).reshape(T, D)
    k = r["kT_out"].transpose(2, 1, 0).reshape(T, G, AH, AE)[:S]
    v = r["v_out"].reshape(S, G, AH, AE)
    prompt = []
    for g, (window, _) in enumerate(GROUPS):
        keep = min(window, S)
        prompt.append(np.stack([k[S - keep:, g], v[S - keep:, g]], axis=1)[None, None])
    sample = [r[f"kv{g}_out"].reshape(i[f"cache_kv_a{g}"].shape) for g in range(G)]
    return (y[None, :S], y[S:, None], *prompt, r["ret_out"][None, None], *sample, r["state_out"][None])
```
